# Optimizing a Trainium2 kernel written in Bass

```python
import jax, jax.numpy as jnp
from jax import lax
import numpy as np

D_MODEL = 1024
BATCH = 1
SEQ = 512
DEPTH = 2

RET_HEADS = 4
RET_DK = 128
RET_DV = 128
FOX_HEADS = 8
FOX_DH = 64
D_FF = 2816
CHUNK = 128
Q_BLOCK = 128
ROPE_BASE = 10000.0
EPS = 1e-6

RET_QK = RET_HEADS * RET_DK
RET_V = RET_HEADS * RET_DV
FOX_W = FOX_HEADS * FOX_DH
IN_SPLITS = (RET_QK, RET_QK, RET_V, RET_V, FOX_W, FOX_W, FOX_W, FOX_HEADS, D_MODEL, D_MODEL)
IN_COLS = sum(IN_SPLITS)


def rmsnorm(x, g):
    xf = x.astype(jnp.float32)
    y = xf * lax.rsqrt(jnp.mean(xf * xf, axis=-1, keepdims=True) + EPS)
    return (y * g.astype(jnp.float32)).astype(x.dtype)

def swiglu(h, w_in, w_out):
    gu = h @ w_in
    a, b = gu[..., :D_FF], gu[..., D_FF:]
    return (jax.nn.silu(a) * b) @ w_out

def split_cols(p):
    outs = []
    off = 0
    for w in IN_SPLITS:
        outs.append(p[..., off:off + w])
        off += w
    return outs

def to_heads(t, n_heads):
    b, s, _ = t.shape
    return t.reshape(b, s, n_heads, -1).transpose(0, 2, 1, 3)

def from_heads(t):
    b, h, s, d = t.shape
    return t.transpose(0, 2, 1, 3).reshape(b, s, h * d)

def rope(t):
    s, d = t.shape[2], t.shape[3]
    inv = jnp.power(ROPE_BASE, -jnp.arange(0, d, 2, dtype=jnp.float32) / d)
    ang = jnp.arange(s, dtype=jnp.float32)[:, None] * inv[None, :]
    cos, sin = jnp.cos(ang), jnp.sin(ang)
    tf = t.astype(jnp.float32)
    t1, t2 = tf[..., : d // 2], tf[..., d // 2:]
    return jnp.concatenate([t1 * cos - t2 * sin, t1 * sin + t2 * cos], axis=-1).astype(t.dtype)

def retention_chunkwise(q, k, v):
    in_dtype = v.dtype
    q = q.astype(jnp.float32)
    k = k.astype(jnp.float32) * (q.shape[-1] ** -0.5)
    v = v.astype(jnp.float32)
    b, h, s, dk = q.shape
    dv = v.shape[-1]
    n = s // CHUNK
    log_gamma = jnp.log1p(-jnp.exp2(-5.0 - jnp.arange(h, dtype=jnp.float32)))
    idx = jnp.arange(CHUNK, dtype=jnp.float32)
    diff = idx[:, None] - idx[None, :]
    decay_intra = jnp.where(diff >= 0, jnp.exp(log_gamma[:, None, None] * jnp.maximum(diff, 0.0)), 0.0)
    xi = jnp.exp(log_gamma[:, None] * (idx + 1.0))
    zeta = jnp.exp(log_gamma[:, None] * (CHUNK - 1.0 - idx))
    gamma_c = jnp.exp(log_gamma * CHUNK)

    qc = q.reshape(b, h, n, CHUNK, dk)
    kc = k.reshape(b, h, n, CHUNK, dk)
    vc = v.reshape(b, h, n, CHUNK, dv)

    scores = jnp.einsum('bhncd,bhnsd->bhncs', qc, kc) * decay_intra[None, :, None]
    inner = jnp.einsum('bhncs,bhnse->bhnce', scores, vc)

    kv = jnp.einsum('bhncd,bhnce->bhnde', kc * zeta[None, :, None, :, None], vc)

    def step(state, kv_n):
        return gamma_c[None, :, None, None] * state + kv_n, state

    _, state_prev = lax.scan(step, jnp.zeros((b, h, dk, dv), jnp.float32), jnp.moveaxis(kv, 2, 0))
    state_prev = jnp.moveaxis(state_prev, 0, 2)
    cross = jnp.einsum('bhncd,bhnde->bhnce', qc * xi[None, :, None, :, None], state_prev)
    return (inner + cross).reshape(b, h, s, dv).astype(in_dtype)

def forgetting_attention(q, k, v, log_f):
    b, h, s, d = q.shape
    c = jnp.cumsum(log_f, axis=-1)
    kpos = jnp.arange(s)
    scale = d ** -0.5
    n_blocks = s // Q_BLOCK

    def block(i):
        start = i * Q_BLOCK
        qb = lax.dynamic_slice_in_dim(q, start, Q_BLOCK, axis=2)
        cb = lax.dynamic_slice_in_dim(c, start, Q_BLOCK, axis=2)
        qpos = start + jnp.arange(Q_BLOCK)
        logits = jnp.einsum('bhqd,bhkd->bhqk', qb, k).astype(jnp.float32) * scale
        logits = logits + (cb[..., :, None] - c[..., None, :])
        logits = jnp.where(kpos[None, :] <= qpos[:, None], logits, -1e30)
        p = jax.nn.softmax(logits, axis=-1)
        return jnp.einsum('bhqk,bhkd->bhqd', p.astype(v.dtype), v)

    out = lax.map(block, jnp.arange(n_blocks))
    return jnp.moveaxis(out, 0, 2).reshape(b, h, s, d)

def mixing_sublayer(h, w_in, b_forget, ret_norm, w_o_ret, w_o_fox, w_out):
    proj = h @ w_in
    rq, rk, rv, rg, fq, fk, fv, ff, gate_r, gate_f = split_cols(proj)

    ret = retention_chunkwise(rope(to_heads(rq, RET_HEADS)), rope(to_heads(rk, RET_HEADS)), to_heads(rv, RET_HEADS))
    retf = ret.astype(jnp.float32)
    retf = retf * lax.rsqrt(jnp.mean(retf * retf, axis=-1, keepdims=True) + EPS)
    ret = from_heads(retf.astype(h.dtype)) * ret_norm
    y_ret = (jax.nn.silu(rg) * ret) @ w_o_ret

    log_f = jax.nn.log_sigmoid((ff + b_forget).astype(jnp.float32))
    fox = forgetting_attention(to_heads(fq, FOX_HEADS), to_heads(fk, FOX_HEADS), to_heads(fv, FOX_HEADS),
                               log_f.transpose(0, 2, 1))
    y_fox = from_heads(fox) @ w_o_fox

    merged = jax.nn.sigmoid(gate_r) * y_ret + jax.nn.sigmoid(gate_f) * y_fox
    return merged @ w_out

def first_inputs(seed: int = 0) -> dict:
    key = jax.random.key(seed)
    ks = jax.random.split(key, 16)
    f32 = jnp.float32

    def nrm(k, shape, fan_in):
        return jax.random.normal(k, shape, f32) * (fan_in ** -0.5)

    def gain(k, shape):
        return 1.0 + 0.02 * jax.random.normal(k, shape, f32)

    return {
        "x": jax.random.normal(ks[0], (BATCH, SEQ, D_MODEL), f32),
        "norm_ffn1": gain(ks[1], (DEPTH, D_MODEL)),
        "w_ffn1_in": nrm(ks[2], (DEPTH, D_MODEL, 2 * D_FF), D_MODEL),
        "w_ffn1_out": nrm(ks[3], (DEPTH, D_FF, D_MODEL), D_FF),
        "norm_mix": gain(ks[4], (DEPTH, D_MODEL)),
        "w_in": nrm(ks[5], (DEPTH, D_MODEL, IN_COLS), D_MODEL),
        "b_forget": jax.random.uniform(ks[6], (DEPTH, FOX_HEADS), f32, minval=1.0, maxval=4.0),
        "ret_norm": gain(ks[7], (DEPTH, RET_V)),
        "w_o_ret": nrm(ks[8], (DEPTH, RET_V, D_MODEL), RET_V),
        "w_o_fox": nrm(ks[9], (DEPTH, FOX_W, D_MODEL), FOX_W),
        "w_out": nrm(ks[10], (DEPTH, D_MODEL, D_MODEL), D_MODEL),
        "norm_ffn2": gain(ks[11], (DEPTH, D_MODEL)),
        "w_ffn2_in": nrm(ks[12], (DEPTH, D_MODEL, 2 * D_FF), D_MODEL),
        "w_ffn2_out": nrm(ks[13], (DEPTH, D_FF, D_MODEL), D_FF),
        "norm_final": gain(ks[14], (D_MODEL,)),
    }

def first_block(x, norm_ffn1, w_ffn1_in, w_ffn1_out, norm_mix, w_in, b_forget, ret_norm,
              w_o_ret, w_o_fox, w_out, norm_ffn2, w_ffn2_in, w_ffn2_out, norm_final):
    for l in range(DEPTH):
        x = x + 0.5 * swiglu(rmsnorm(x, norm_ffn1[l]), w_ffn1_in[l], w_ffn1_out[l])
        h = rmsnorm(x, norm_mix[l])
        x = x + mixing_sublayer(h, w_in[l], b_forget[l], ret_norm[l], w_o_ret[l], w_o_fox[l], w_out[l])
        x = x + 0.5 * swiglu(rmsnorm(x, norm_ffn2[l]), w_ffn2_in[l], w_ffn2_out[l])
    return rmsnorm(x, norm_final)


BLOCK = 128
NORM_EPS = 1e-6
SWA_WINDOW = 128
SWA_HEADS = 4
SWA_KV_HEADS = 2
SWA_HEAD_DIM = 64
CONV_WIDTH = 256
CONV_K = 3
MLA_HEADS = 4
MLA_Q_RANK = 256
MLA_KV_RANK = 128
MLA_NOPE_DIM = 64
MLA_ROPE_DIM = 32
MLA_V_DIM = 64
ROPE_THETA = 10000.0
SB_HEADS = 4
SB_HEAD_DIM = 64
GROUP_WIDTH = 256
N_GROUPS = 4
D_MIX = GROUP_WIDTH * N_GROUPS

A_Q = SWA_HEADS * SWA_HEAD_DIM
A_KV = SWA_KV_HEADS * SWA_HEAD_DIM
SB_W = SB_HEADS * SB_HEAD_DIM
IN_SIZES = (A_Q, A_KV, A_KV,
            CONV_WIDTH, CONV_WIDTH, CONV_WIDTH,
            MLA_Q_RANK, MLA_KV_RANK, MLA_ROPE_DIM,
            SB_W, SB_W, SB_W,
            D_MIX)
D_IN = int(sum(IN_SIZES))
SPLIT_IDX = [int(v) for v in np.cumsum(IN_SIZES)[:-1]]


def rmsnorm_2(x, g):
    x32 = x.astype(jnp.float32)
    y = x32 * lax.rsqrt(jnp.mean(x32 * x32, axis=-1, keepdims=True) + NORM_EPS)
    return (y * g.astype(jnp.float32)).astype(x.dtype)

def to_blocks(t):
    b, s = t.shape[:2]
    t = t.reshape((b, s // BLOCK, BLOCK) + t.shape[2:])
    return jnp.moveaxis(t, 1, 0)

def from_blocks(t):
    t = jnp.moveaxis(t, 0, 1)
    return t.reshape((t.shape[0], t.shape[1] * t.shape[2]) + t.shape[3:])

def rope_2(x, pos):
    half = x.shape[-1] // 2
    freqs = ROPE_THETA ** (-jnp.arange(half, dtype=jnp.float32) / half)
    ang = pos.astype(jnp.float32)[..., None] * freqs
    ang = ang.reshape(ang.shape[:2] + (1,) * (x.ndim - 3) + (half,))
    cos, sin = jnp.cos(ang), jnp.sin(ang)
    x32 = x.astype(jnp.float32)
    x1, x2 = x32[..., :half], x32[..., half:]
    return jnp.concatenate([x1 * cos - x2 * sin, x1 * sin + x2 * cos], axis=-1).astype(x.dtype)

def swa_sink_attention(q, k, v, sinks):
    b, s, h, d = q.shape
    kvh = k.shape[2]
    g = h // kvh
    nb = s // BLOCK
    qb = q.reshape(b, nb, BLOCK, kvh, g, d).astype(jnp.float32)
    kb = k.reshape(b, nb, BLOCK, kvh, d).astype(jnp.float32)
    vb = v.reshape(b, nb, BLOCK, kvh, d).astype(jnp.float32)
    prev = lambda t: jnp.concatenate([jnp.zeros_like(t[:, :1]), t[:, :-1]], axis=1)
    kk = jnp.concatenate([prev(kb), kb], axis=2)
    vv = jnp.concatenate([prev(vb), vb], axis=2)
    scores = jnp.einsum('bnqhgd,bnkhd->bnhgqk', qb, kk) * (d ** -0.5)
    qi = jnp.arange(BLOCK)[:, None]
    kj = jnp.arange(2 * BLOCK)[None, :]
    diff = qi + BLOCK - kj
    blk = jnp.arange(nb)[:, None, None]
    valid = (diff >= 0) & (diff < SWA_WINDOW) & (blk * BLOCK + kj - BLOCK >= 0)
    scores = jnp.where(valid[None, :, None, None], scores, -jnp.inf)
    sink = jnp.broadcast_to(sinks.astype(jnp.float32).reshape(1, 1, kvh, g, 1, 1), scores.shape[:-1] + (1,))
    probs = jax.nn.softmax(jnp.concatenate([scores, sink], axis=-1), axis=-1)[..., :-1]
    out = jnp.einsum('bnhgqk,bnkhd->bnqhgd', probs, vv)
    return out.reshape(b, s, h * d).astype(q.dtype)

def short_gated_conv(bg, cg, xin, conv_w, conv_b):
    u = cg * xin
    y = lax.conv_general_dilated(u, conv_w[:, None, :], window_strides=(1,),
                                 padding=[(CONV_K - 1, 0)],
                                 dimension_numbers=('NWC', 'WIO', 'NWC'),
                                 feature_group_count=u.shape[-1])
    return bg * (y + conv_b)

def causal_softmax_attention(q, k, v):
    b, s, h, dk = q.shape
    scale = dk ** -0.5
    kf = k.astype(jnp.float32)
    vf = v.astype(jnp.float32)
    kpos = jnp.arange(s)

    def step(args):
        qblk, i = args
        sc = jnp.einsum('bqhd,bkhd->bhqk', qblk.astype(jnp.float32), kf) * scale
        qpos = i * BLOCK + jnp.arange(BLOCK)
        sc = jnp.where(kpos[None, :] <= qpos[:, None], sc, -jnp.inf)
        p = jax.nn.softmax(sc, axis=-1)
        return jnp.einsum('bhqk,bkhd->bqhd', p, vf)

    out = lax.map(step, (to_blocks(q), jnp.arange(s // BLOCK)))
    return from_blocks(out).reshape(b, s, -1).astype(q.dtype)

def mla(cq, ckv, kr, pos, g_q, w_uq, g_kv, w_ukv):
    b, s, _ = cq.shape
    q = (rmsnorm_2(cq, g_q) @ w_uq).reshape(b, s, MLA_HEADS, MLA_NOPE_DIM + MLA_ROPE_DIM)
    q = jnp.concatenate([q[..., :MLA_NOPE_DIM], rope_2(q[..., MLA_NOPE_DIM:], pos)], axis=-1)
    kv = (rmsnorm_2(ckv, g_kv) @ w_ukv).reshape(b, s, MLA_HEADS, MLA_NOPE_DIM + MLA_V_DIM)
    k_nope, v = kv[..., :MLA_NOPE_DIM], kv[..., MLA_NOPE_DIM:]
    k_rope = jnp.broadcast_to(rope_2(kr, pos)[:, :, None, :], (b, s, MLA_HEADS, MLA_ROPE_DIM))
    k = jnp.concatenate([k_nope, k_rope], axis=-1)
    return causal_softmax_attention(q, k, v)

def stick_breaking_attention(q, k, v):
    b, s, h, d = q.shape
    scale = d ** -0.5
    kf = k.astype(jnp.float32)
    vf = v.astype(jnp.float32)
    kpos = jnp.arange(s)

    def step(args):
        qblk, i = args
        z = jnp.einsum('bqhd,bkhd->bhqk', qblk.astype(jnp.float32), kf) * scale
        qpos = i * BLOCK + jnp.arange(BLOCK)
        mask = kpos[None, :] < qpos[:, None]
        log_keep = jnp.where(mask, jax.nn.log_sigmoid(-z), 0.0)
        after = lax.cumsum(log_keep, axis=3, reverse=True) - log_keep
        a = jnp.where(mask, jnp.exp(jax.nn.log_sigmoid(z) + after), 0.0)
        return jnp.einsum('bhqk,bkhd->bqhd', a, vf)

    out = lax.map(step, (to_blocks(q), jnp.arange(s // BLOCK)))
    return from_blocks(out).reshape(b, s, -1).astype(q.dtype)

def hybrid_layer(x, pos, g_pre, w_in, sinks, conv_w, conv_b, g_cq, w_uq, g_ckv, w_ukv, g_grp, w_out, g_post):
    b, s, _ = x.shape
    h = rmsnorm_2(x, g_pre) @ w_in
    (a_q, a_k, a_v, b_b, b_c, b_x, c_q, c_kv, c_kr, d_q, d_k, d_v, gate) = jnp.split(h, SPLIT_IDX, axis=-1)
    ya = swa_sink_attention(a_q.reshape(b, s, SWA_HEADS, SWA_HEAD_DIM),
                            a_k.reshape(b, s, SWA_KV_HEADS, SWA_HEAD_DIM),
                            a_v.reshape(b, s, SWA_KV_HEADS, SWA_HEAD_DIM), sinks)
    yb = short_gated_conv(b_b, b_c, b_x, conv_w, conv_b)
    yc = mla(c_q, c_kv, c_kr, pos, g_cq, w_uq, g_ckv, w_ukv)
    yd = stick_breaking_attention(d_q.reshape(b, s, SB_HEADS, SB_HEAD_DIM),
                                  d_k.reshape(b, s, SB_HEADS, SB_HEAD_DIM),
                                  d_v.reshape(b, s, SB_HEADS, SB_HEAD_DIM))
    y = jnp.stack([ya, yb, yc, yd], axis=2)
    y = rmsnorm_2(y, g_grp.reshape(N_GROUPS, GROUP_WIDTH)).reshape(b, s, D_MIX)
    y = y * jax.nn.silu(gate)
    return x + rmsnorm_2(y @ w_out, g_post)

def second_inputs(seed: int = 0) -> dict:
    key = jax.random.key(seed)
    ks = jax.random.split(key, 16)
    f32 = jnp.float32
    nrm = lambda k, shape, scale: jax.random.normal(k, shape, f32) * scale
    gain = lambda k, shape: 1.0 + 0.02 * jax.random.normal(k, shape, f32)
    x = jax.random.normal(ks[0], (BATCH, SEQ, D_MODEL), f32)
    positions = jnp.broadcast_to(jnp.arange(SEQ, dtype=jnp.int32)[None, :], (BATCH, SEQ))
    return {
        "x": x,
        "positions": positions,
        "norm_pre": gain(ks[1], (DEPTH, D_MODEL)),
        "w_in": nrm(ks[2], (DEPTH, D_MODEL, D_IN), D_MODEL ** -0.5),
        "attn_sinks": nrm(ks[3], (DEPTH, SWA_HEADS), 0.5),
        "conv_w": nrm(ks[4], (DEPTH, CONV_K, CONV_WIDTH), CONV_K ** -0.5),
        "conv_b": nrm(ks[5], (DEPTH, CONV_WIDTH), 0.01),
        "mla_q_norm": gain(ks[6], (DEPTH, MLA_Q_RANK)),
        "mla_w_uq": nrm(ks[7], (DEPTH, MLA_Q_RANK, MLA_HEADS * (MLA_NOPE_DIM + MLA_ROPE_DIM)), MLA_Q_RANK ** -0.5),
        "mla_kv_norm": gain(ks[8], (DEPTH, MLA_KV_RANK)),
        "mla_w_ukv": nrm(ks[9], (DEPTH, MLA_KV_RANK, MLA_HEADS * (MLA_NOPE_DIM + MLA_V_DIM)), MLA_KV_RANK ** -0.5),
        "group_norm": gain(ks[10], (DEPTH, D_MIX)),
        "w_out": nrm(ks[11], (DEPTH, D_MIX, D_MODEL), D_MIX ** -0.5),
        "norm_post": gain(ks[12], (DEPTH, D_MODEL)),
    }

def second_block(x, positions, norm_pre, w_in, attn_sinks, conv_w, conv_b, mla_q_norm, mla_w_uq,
              mla_kv_norm, mla_w_ukv, group_norm, w_out, norm_post):
    for l in range(DEPTH):
        x = hybrid_layer(x, positions, norm_pre[l], w_in[l], attn_sinks[l], conv_w[l], conv_b[l],
                         mla_q_norm[l], mla_w_uq[l], mla_kv_norm[l], mla_w_ukv[l],
                         group_norm[l], w_out[l], norm_post[l])
    return x


def setup_inputs(seed=0):
    out = dict(first_inputs(seed))
    for name, value in second_inputs(seed + 1).items():
        if name != "x":
            out[name + "_2"] = value
    return out


def reference(
    x, norm_ffn1, w_ffn1_in, w_ffn1_out, norm_mix, w_in, b_forget, ret_norm, w_o_ret, w_o_fox,
    w_out, norm_ffn2, w_ffn2_in, w_ffn2_out, norm_final, positions_2, norm_pre_2, w_in_2,
    attn_sinks_2, conv_w_2, conv_b_2, mla_q_norm_2, mla_w_uq_2, mla_kv_norm_2, mla_w_ukv_2,
    group_norm_2, w_out_2, norm_post_2,
):
    x = first_block(
        x, norm_ffn1, w_ffn1_in, w_ffn1_out, norm_mix, w_in, b_forget, ret_norm, w_o_ret,
        w_o_fox, w_out, norm_ffn2, w_ffn2_in, w_ffn2_out, norm_final,
    )
    return second_block(
        x, positions_2, norm_pre_2, w_in_2, attn_sinks_2, conv_w_2, conv_b_2, mla_q_norm_2,
        mla_w_uq_2, mla_kv_norm_2, mla_w_ukv_2, group_norm_2, w_out_2, norm_post_2,
    )


_drawn_inputs = setup_inputs


def setup_inputs(seed=0):
    import zlib

    import numpy as np

    out = dict(_drawn_inputs(seed))
    spreads = {}
    factors = {'ret_norm': 3.362,
     'norm_ffn2': 2.733,
     'attn_sinks_2': 8.0,
     'conv_b_2': 8.0,
     'mla_q_norm_2': 5.922,
     'mla_kv_norm_2': 3.596}
    for name, (base, spread) in spreads.items():
        noise = np.random.default_rng([zlib.crc32(name.encode()), seed]).standard_normal(out[name].shape)
        drawn = base * np.exp(spread * noise) if base else spread * noise
        out[name] = __import__('jax').numpy.asarray(drawn.astype(out[name].dtype))
    for name, factor in factors.items():
        out[name] = (out[name] * factor).astype(out[name].dtype)
    return out
```

```python
from contextlib import ExitStack

import numpy as np
import concourse.bass as bass
import concourse.mybir as mybir

F32 = mybir.dt.float32
F32R = mybir.dt.float32r
I32 = mybir.dt.int32
ALU = mybir.AluOpType
ACT = mybir.ActivationFunctionType
AX_X = mybir.AxisListType.X

P = 128
D, S, DEPTH, F = 1024, 512, 2, 2816
KD = D // P
TT = S // P
KF = F // P
RH, RDK = 4, 128
FH, FDH = 8, 64
MH, M_NOPE, M_ROPE, M_V, QR, KVR = 4, 64, 32, 64, 256, 128
MLA_K = 112
SWH, SDH = 4, 64
BH, BDH = 4, 64
CONV_W, CONV_K = 256, 3
GROUP = 256
TM_COLS = SDH * 2 + BH * BDH
KR_AT = MH * (M_NOPE + M_V)
KR_W = 48
EPS = 1e-6
NEG = -1e31

UNITS = 8
PANEL = UNITS * P
RAW_SLOTS, SPLIT_SLOTS = 4, 2
KT_MAJOR = 16

FFN_IN = 2 * KF
FFN_PANELS = FFN_IN + KF
AT_RV = FFN_PANELS
AT_FV = AT_RV + KD // 2
AT_RG = AT_FV + KD // 2
AT_RET = AT_RG + RH
AT_FOX = AT_RET + 4 * RH
AT_MERGE = AT_FOX + FH
AT_WOUT = AT_MERGE + 2 * KD
AT_FFN2 = AT_WOUT + KD
LAYER1 = AT_FFN2 + FFN_PANELS
BT_TM = 0
BT_CQ = BT_TM + KD // 2
BT_CKV = BT_CQ + 2
BT_AK = BT_CKV + 1
BT_AQ = BT_AK + 1
BT_DQ = BT_AQ + 2
BT_DK = BT_DQ + 2
BT_UQ = BT_DK + 2
BT_UKV = BT_UQ + 1
BT_CONV = BT_UKV + 1
BT_GATE = BT_CONV + 6
BT_WOUT = BT_GATE + KD
LAYER2 = BT_WOUT + KD
SECOND = DEPTH * LAYER1
N_PANELS = SECOND + DEPTH * LAYER2
NORMS = 3 * DEPTH + 1 + DEPTH + 1
FINAL = 3 * DEPTH

V_RET = NORMS * KD
V_GRP = V_RET + DEPTH * RH
V_POST = V_GRP + DEPTH * KD
V_QN = V_POST + DEPTH * KD
V_KVN = V_QN + DEPTH * 2
V_CW = V_KVN + DEPTH
V_CB = V_CW + DEPTH * 6
V_BF = V_CB + DEPTH * 2
V_SINK = V_BF + DEPTH
N_VEC = V_SINK + DEPTH * SWH
C_ID, C_ONE, C_NONE, C_NTRI, C_CAUSAL, C_SWA, C_SWA0, C_STRICT, C_KEEP = (
    0, 128, 256, 384, 512, 640, 896, 1152, 1280)
C_FREQ, C_HOT, C_M8 = 1408, 1409, 1417
N_CONST = C_M8 + P


class Steps:

    def __init__(self, sem, *names, started=0):
        self.sem, self.names, self.n, self.started = sem, names, len(names), started

    def at(self, round_, name):
        return self.sem, round_ * self.n + (self.names.index(name) + 1 + self.started)

    def before(self, round_):
        return self.sem, round_ * self.n + self.started


def build(nc, stream, x_in, vec, const, decay, rope, ff_w, pos, out):
    ctx = ExitStack()
    with ctx:
        def sb(name, shape, dt=F32, stack=ctx):
            return stack.enter_context(nc.sbuf_tensor(name, shape, dt))

        def sem(name):
            return ctx.enter_context(nc.semaphore(name))

        bank = [ctx.enter_context(nc.psum_tensor(f"bank{i}", [P, S], F32)) for i in range(8)]

        x = sb("x", [P, KD, S])
        xh = sb("xh", [P, KD, S], F32R)
        xl = sb("xl", [P, KD, S], F32R)
        sq = sb("sq", [P, S])
        ssq = sb("ssq", [P, S])
        diag = sb("diag", [P, S])
        rstd = sb("rstd", [P, S])
        std_col = sb("std_col", [P, TT])
        rstd_col = sb("rstd_col", [P, TT])
        raw = sb("raw", [P, RAW_SLOTS, PANEL])
        wh = sb("wh", [P, SPLIT_SLOTS, PANEL], F32R)
        wl = sb("wl", [P, SPLIT_SLOTS, PANEL], F32R)
        vecs = sb("vecs", [P, N_VEC])
        cst = sb("cst", [P, N_CONST])
        eps = sb("eps", [P, 1])
        one = sb("one", [P, 1])
        start_d = sb("start_d", [P, 3])
        start_a = sb("start_a", [P, 2])
        cos2 = sb("cos2", [P, S])
        sin2 = sb("sin2", [P, S])
        ident, ones = cst[:, C_ID:C_ID + P], cst[:, C_ONE:C_ONE + P]
        causal = cst[:, C_CAUSAL:C_CAUSAL + P]

        ffn = ExitStack()
        uh = sb("uh", [P, KF, S], F32R, ffn)
        ul = sb("ul", [P, KF, S], F32R, ffn)
        ta = sb("ta", [P, S], F32, ffn)
        tb = sb("tb", [P, S], F32, ffn)
        sa = sb("sa", [P, S], F32, ffn)
        u32 = sb("u32", [P, S], F32, ffn)
        ffn.close()
        init = ExitStack()
        x0 = sb("x0", [P, KD, S], F32, init)
        posi = sb("posi", [P, S], I32, init)
        ang = sb("ang", [P, S], F32, init)
        turn = sb("turn", [P, S], F32, init)
        init.close()
        mix = ExitStack()
        yrh = sb("yrh", [P, RH, S], F32R, mix)
        yrl = sb("yrl", [P, RH, S], F32R, mix)
        yfh = sb("yfh", [P, FH // 2, S], F32R, mix)
        yfl = sb("yfl", [P, FH // 2, S], F32R, mix)
        gate_r = sb("gate_r", [P, KD, S], F32, mix)
        heads = ExitStack()
        dec = sb("dec", [P, RH, S], F32, heads)
        rp = sb("rp", [P, 2, S], F32, heads)
        v_fox = sb("v_fox", [P, TT, S], F32, heads)
        cum = sb("cum", [P, S], F32, heads)
        ffraw = sb("ffraw", [P, DEPTH, UNITS * FH], F32, heads)
        ffh = sb("ffh", [P, UNITS * FH + P], F32R, heads)
        ffl = sb("ffl", [P, UNITS * FH + P], F32R, heads)
        ret_mem = ExitStack()
        tq = sb("tq", [P, S], F32, ret_mem)
        tk = sb("tk", [P, S], F32, ret_mem)
        sw = sb("sw", [P, S], F32, ret_mem)
        m1 = sb("m1", [P, S], F32, ret_mem)
        qr = sb("qr", [P, S], F32, ret_mem)
        kr = sb("kr", [P, S], F32, ret_mem)
        pt = sb("pt", [P, 10 * P], F32, ret_mem)
        hsum = sb("hsum", [P, TT], F32, ret_mem)
        hstd = sb("hstd", [P, TT], F32, ret_mem)
        hinv = sb("hinv", [P, TT], F32, ret_mem)
        v_ret = sb("v_ret", [P, TT, S], F32, ret_mem)
        rgs = sb("rgs", [P, RH, S], F32, ret_mem)
        ret_mem.close()
        tg = yn = tk
        y32 = tq
        fox_mem = ExitStack()
        fp = sb("fp", [P, 2, 10 * P], F32, fox_mem)
        cm = sb("cm", [P, 2, S], F32, fox_mem)
        fq = sb("fq", [P, S], F32, fox_mem)
        fk = sb("fk", [P, S], F32, fox_mem)
        fpt = sb("fpt", [P, 10 * P], F32, fox_mem)
        fo = sb("fo", [P, TT, P], F32, fox_mem)
        fmx = sb("fmx", [P, 2, TT], F32, fox_mem)
        fnm = sb("fnm", [P, 2, TT], F32, fox_mem)
        fsum = sb("fsum", [P, 2, TT], F32, fox_mem)
        finv = sb("finv", [P, 2, TT], F32, fox_mem)
        fox_mem.close()
        fz, fa = fp[:, 0, 0:S], fp[:, 1, 0:S]
        heads.close()
        merge_mem = ExitStack()
        mh = sb("mh", [P, KD, S], F32R, merge_mem)
        ml = sb("ml", [P, KD, S], F32R, merge_mem)
        sr = sb("sr", [P, S], F32, merge_mem)
        sf = sb("sf", [P, S], F32, merge_mem)
        tgf = sb("tgf", [P, S], F32, merge_mem)
        mr = sb("mr", [P, S], F32, merge_mem)
        mf = sb("mf", [P, S], F32, merge_mem)
        mg = sb("mg", [P, S], F32, merge_mem)
        merge_mem.close()
        mix.close()
        hyb = ExitStack()
        y_swa = sb("y_swa", [P, TT, GROUP], F32, hyb)
        y_mla = sb("y_mla", [P, TT, GROUP], F32, hyb)
        y_sb = sb("y_sb", [P, TT, GROUP], F32, hyb)
        y_conv = sb("y_conv", [P, 2, S], F32, hyb)
        qkv_mem = ExitStack()
        vtm = sb("vtm", [P, TT, TM_COLS], F32, qkv_mem)
        cqh = sb("cqh", [P, 2, S], F32R, qkv_mem)
        cql = sb("cql", [P, 2, S], F32R, qkv_mem)
        ckh = sb("ckh", [P, S], F32R, qkv_mem)
        ckl = sb("ckl", [P, S], F32R, qkv_mem)
        aq = sb("aq", [P, 2, S], F32, qkv_mem)
        ak = sb("ak", [P, S], F32, qkv_mem)
        dq = sb("dq", [P, 2, S], F32, qkv_mem)
        dk = sb("dk", [P, 2, S], F32, qkv_mem)
        mq = sb("mq", [P, MH, S], F32, qkv_mem)
        mk = sb("mk", [P, MH, S], F32, qkv_mem)
        vm = sb("vm", [P, TT, MH * M_V], F32, qkv_mem)
        lat_mem = ExitStack()
        cq = sb("cq", [P, 2, S], F32, lat_mem)
        ckv = sb("ckv", [P, S], F32, lat_mem)
        qsq = sb("qsq", [P, 2, S], F32, lat_mem)
        ksq = sb("ksq", [P, S], F32, lat_mem)
        qin = sb("qin", [P, S], F32, lat_mem)
        kin = sb("kin", [P, S], F32, lat_mem)
        cn = sb("cn", [P, S], F32, lat_mem)
        t1 = sb("t1", [P, S], F32, lat_mem)
        t2 = sb("t2", [P, S], F32, lat_mem)
        msw = sb("msw", [P, S], F32, lat_mem)
        krs = sb("krs", [P, S], F32, lat_mem)
        kx = sb("kx", [P, S], F32, lat_mem)
        cgs = sb("cgs", [P, S], F32, lat_mem)
        cxs = sb("cxs", [P, S], F32, lat_mem)
        cu = sb("cu", [P, CONV_K - 1 + S], F32, lat_mem)
        cy = sb("cy", [P, S], F32, lat_mem)
        lat_mem.close()
        att_mem = ExitStack()
        pr = sb("pr", [P, 2, 10 * P], F32, att_mem)
        prt = sb("prt", [P, 10 * P], F32, att_mem)
        smx = sb("smx", [P, 2, TT], F32, att_mem)
        snm = sb("snm", [P, 2, TT], F32, att_mem)
        ssum = sb("ssum", [P, 2, TT], F32, att_mem)
        sinv = sb("sinv", [P, 2, TT], F32, att_mem)
        esk = sb("esk", [P, 2, TT], F32, att_mem)
        lsg = sb("lsg", [P, 2, 10 * P], F32, att_mem)
        spl = sb("spl", [P, 2, 10 * P], F32, att_mem)
        att_mem.close()
        grp_mem = ExitStack()
        yt = sb("yt", [P, KD, S], F32, grp_mem)
        bsq = sb("bsq", [P, 2, S], F32, grp_mem)
        bstd = sb("bstd", [P, S], F32, grp_mem)
        binv = sb("binv", [P, S], F32, grp_mem)
        gt = sb("gt", [P, S], F32, grp_mem)
        gs = sb("gs", [P, S], F32, grp_mem)
        yg = sb("yg", [P, S], F32, grp_mem)
        gsq = sb("gsq", [P, TT, GROUP], F32, grp_mem)
        gsum = sb("gsum", [P, 3, TT], F32, grp_mem)
        gstd = sb("gstd", [P, 3, TT], F32, grp_mem)
        ginv = sb("ginv", [P, 3, TT], F32, grp_mem)
        grp_mem.close()
        qkv_mem.close()
        out_mem = ExitStack()
        ygh = sb("ygh", [P, KD, S], F32R, out_mem)
        ygl = sb("ygl", [P, KD, S], F32R, out_mem)
        z = sb("z", [P, KD, S], F32, out_mem)
        out_mem.close()
        hyb.close()

        raw_in = [sem(f"raw_in{i}") for i in range(RAW_SLOTS)]
        split_hi, split_lo = sem("split_hi"), sem("split_lo")
        panel_done = sem("panel_done")
        loaded = sem("loaded")
        tab_in = sem("tab_in")
        tab_free = sem("tab_free")
        memsets = sem("memsets")
        one_set = sem("one_set")
        stored = sem("stored")
        prep = Steps(sem("prep_dve"), "X", "XH", "XL", "ACC")
        prep_sq = Steps(sem("prep_act"), "SQ")
        chain_pe = Steps(sem("chain_pe"), "COL", "BC")
        chain_sd = Steps(sem("chain_act"), "SD")
        chain = Steps(sem("chain_dve"), "RC", "DG", "RB")
        fin = Steps(sem("ffn_in_dve"), "A", "B", "U", "UL")
        fin_act = Steps(sem("ffn_in_act"), "SILU", "UH")
        fout = Steps(sem("ffn_out_pe"), *range(KD))
        tm = Steps(sem("tm_dve"), *[f"RV{i}" for i in range(TT)], *[f"FV{i}" for i in range(TT)])
        ffs = Steps(sem("forget_dve"), "H", "L", "Z", "ZB", "LF", "C")
        ffs_pe = Steps(sem("forget_pe"), "FF")
        ffs_act = Steps(sem("forget_act"), "ABS", "EXP", "LN")
        rg = Steps(sem("rg_dve"), "T", started=1)
        rg_act = Steps(sem("rg_act"), "S", started=1)
        ret_pe = Steps(sem("ret_pe"), "SC", "PV", "TR")
        ret = Steps(sem("ret_dve"), "Q", "K", "QC", "QS", "QR", "KC", "KS", "KR", "G0", "P0", "P1", "P2", "P3",
                    "G1", "RC", "N0", "N1", "N2", "N3", "Y", "YL", started=1)
        ret_act = Steps(sem("ret_act"), "Q0", "Q1", "K0", "K1", "S0", "S1", "S2", "S3", "SD", "YH")
        fox_pe = Steps(sem("fox_pe"), "SA", "SB", "TA0", "TA1", "TA2", "VA", "TB0", "TB1", "TB2", "VB", "TR")
        fox = Steps(sem("fox_dve"), "CA", "CB", "Q", "K", "MA", "NA", "MB", "NB", "EA", "RA", "OA",
                    "EB", "RB", "OB", "YL", started=1)
        fox_act = Steps(sem("fox_act"), "XA", "XB", "EA0", "EA2", "EB0", "EB2", "YH", started=1)
        mrg_d = Steps(sem("merge_dve"), "G", "R", "F", "M", "L")
        mrg_a = Steps(sem("merge_act"), "SR", "SF", "MH")

        trig = Steps(sem("trig_dve"), "F", "A", *[f"{w}{i}" for w in "sc" for i in range(6)], "NEG")
        trig_act = Steps(sem("trig_act"), "SIN", "COS")
        pj = Steps(sem("proj_dve"), "T0", "T1", "T2", "T3", "Q0", "Q1", "KV", "AK", "A0", "A1", "D0", "D1", "E0", "E1")
        lat_pe = Steps(sem("latent_pe"), "Q", "K")
        lat = Steps(sem("latent_dve"), "SUM", "IQ", "IK", "N0", "L0", "N1", "L1", "NK", "LK")
        lat_act = Steps(sem("latent_act"), "S0", "S1", "SK", "DQ", "DK", "H0", "H1", "HK")
        mla = Steps(sem("mla_q_dve"), "Z", *[f"{w}{h}" for h in range(MH) for w in "CSR"])
        mla_act = Steps(sem("mla_q_act"), *[f"{w}{h}" for h in range(MH) for w in "PVW"])
        kv = Steps(sem("mla_kv_dve"), "V0", "V1", "KS", "KC", "KM", "KR")
        kv_act = Steps(sem("mla_kv_act"), "N0", "N1", "N2", "N3", "X", "Y0", "Y1", "C1", "C2", "C3")
        conv = Steps(sem("conv_dve"), "C", "X", "U", "A", "B", "D", "G", "Y")
        mla_sc = Steps(sem("mla_scores_pe"), "SC")
        mla_mx = Steps(sem("mla_max_dve"), "M", "N")
        mla_ex = Steps(sem("mla_exp_act"), "X")
        mla_pe = Steps(sem("mla_values_pe"), "T0", "T1", "T2", "V")
        mla_dve = Steps(sem("mla_values_dve"), "E", "R", "O")
        mla_ev = Steps(sem("mla_values_act"), "E0", "E2")
        swa_sc = Steps(sem("swa_scores_pe"), "SC")
        swa_mx = Steps(sem("swa_max_dve"), "M", "S", "N")
        swa_ex = Steps(sem("swa_exp_act"), "X", "K")
        swa_pe = Steps(sem("swa_values_pe"), "T0", "T1", "V")
        swa_dve = Steps(sem("swa_values_dve"), "E", "Q", "R", "O")
        swa_ev = Steps(sem("swa_values_act"), "E0")
        sb_sc = Steps(sem("stick_scores_pe"), "Z")
        sb_ln = Steps(sem("stick_log_act"), "AB", "EX", "LN")
        sb_keep = Steps(sem("stick_log_dve"), "SP", "LS", "K")
        sb_pe = Steps(sem("stick_values_pe"), "A", "V")
        sb_dve = Steps(sem("stick_values_dve"), "T")
        sb_act = Steps(sem("stick_values_act"), "P", "O")
        gn_pe = Steps(sem("group_pe"), "B", "T0", "T1", "T2")
        gn = Steps(sem("group_dve"), "SUM", "I0", "N0", "I1", "N1", "I2", "N2", "A0", "A1", "C0", "C1", "IB", "B0", "B1",
                   "D0", "D1")
        gn_act = Steps(sem("group_act"), "Q0", "Q1", "S0", "S1", "S2", "DB", "D0", "D1", "D2")
        gate = Steps(sem("gate_dve"), "G", "Y", "L")
        gate_act = Steps(sem("gate_act"), "S", "H")
        z_act = Steps(sem("z_act"), "Z", "Q")
        z_sum = Steps(sem("z_dve"), "A")
        post_pe = Steps(sem("post_pe"), "COL", "BC")
        post_sd = Steps(sem("post_act"), "SD")
        post = Steps(sem("post_dve"), "RC", "DG", "RB", *[f"Z{d}" for d in range(KD)])

        SETS = (((2, 0), (3, 0), (2, 128), (4, 0)), ((1, 0), (5, 0), (1, 128), (0, 0)))
        FIRST_BLOCK = (0, 1, 3, 6)
        STICK_AT = (0, 512, 1024, 896)

        OFF = (0, 512, 896, 1152)

        block = ctx.enter_context(nc.Block())

        @block.sync
        def _(sp):
            loads = [(x0[:], x_in), (vecs[:], vec), (cst[:], const), (posi[:], pos)]
            for dst, src in loads:
                sp.dma_start(dst, src).then_inc(loaded, 16)
            for n in range(RAW_SLOTS):
                sp.dma_start(raw[:, n, :], stream[n]).then_inc(raw_in[n], 16)
            with sp.Fori(1, N_PANELS // RAW_SLOTS) as g:
                for n in range(RAW_SLOTS):
                    sp.wait_ge(split_lo, g * RAW_SLOTS + (n + 1 - RAW_SLOTS))
                    sp.dma_start(raw[:, n, :], stream[g * RAW_SLOTS + n]).then_inc(raw_in[n], 16)
            for d in range(KD):
                sp.wait_ge(*prep.at((NORMS - 1) * KD + d, "X"))
                sp.dma_start(out[d], x[:, d, :]).then_inc(stored, 16)
            sp.wait_ge(stored, 16 * KD)

        @block.gpsimd
        def _(pool):
            def split(n, g, first=False):
                slot = n % SPLIT_SLOTS
                pool.wait_ge(raw_in[n], 16 * (g + 1))
                if not (first and n < SPLIT_SLOTS):
                    pool.wait_ge(panel_done, g * RAW_SLOTS + (n + 1 - SPLIT_SLOTS))
                pool.tensor_tensor(wh[:, slot, :], raw[:, n, :], one[:].to_broadcast([P, PANEL]), ALU.mult).then_inc(split_hi, 1)
                pool.wait_ge(split_hi, g * RAW_SLOTS + (n + 1))
                pool.tensor_tensor(wl[:, slot, :], raw[:, n, :], wh[:, slot, :].bitcast(F32),
                                   ALU.subtract).then_inc(split_lo, 1)

            pool.memset(one[:], 1.0).then_inc(one_set, 1)
            pool.wait_ge(one_set, 1)
            for n in range(RAW_SLOTS):
                split(n, 0, True)
            with pool.Fori(1, N_PANELS // RAW_SLOTS) as g:
                for n in range(RAW_SLOTS):
                    split(n, g)

        @block.tensor
        def _(pe):
            def mm3(o, w, rhs_h, rhs_l, first, last):
                s, c = w
                pe.matmul(o, wh[:, s, c], rhs_h, start=first, stop=False)
                pe.matmul(o, wh[:, s, c], rhs_l, start=False, stop=False)
                return pe.matmul(o, wl[:, s, c], rhs_h, start=False, stop=last)

            def unit(u):
                return slice(u * P, (u + 1) * P)

            def panel_ready(idx):
                pe.wait_ge(split_lo, idx + 1)

            def x_ready(n, d):
                pe.wait_ge(*prep.at(n * KD + d, "XL"))

            def col_panel(o, slot, idx, norm=None):
                panel_ready(idx)
                for k in range(KD):
                    if norm is not None:
                        x_ready(norm, k)
                    last = mm3(o, (slot, unit(k)), xh[:, k, :], xl[:, k, :], k == 0, k == KD - 1)
                last.then_inc(panel_done, 1)

            def chain_col(n, b):
                pe.wait_ge(*prep.at(n * KD + KD - 1, "ACC"))
                for t in range(TT):
                    last = pe.matmul(bank[b][:, t:t + 1], ssq[:, t * P:(t + 1) * P], ones[:, 0:1],
                                     start=True, stop=True)
                last.then_inc(chain_pe.sem, 1)

            def chain_bc(n, b):
                pe.wait_ge(*chain.at(n, "DG"))
                pe.matmul(bank[b][:], ones, diag[:], start=True, stop=True).then_inc(chain_pe.sem, 1)

            def ffn_in(f, n, idx):
                def pair(j, at, it, first):
                    q = 2 * (j % 2)
                    if first:
                        pe.wait_ge(*prep.at(n * KD + 4 + q + 1, "X"))
                    else:
                        pe.wait_ge(*fin.at(it - 2, "B"))
                    col_panel(bank[q][:], 0, at, n if first and j == 0 else None)
                    if first and j == 0:
                        chain_col(n, 4)
                    col_panel(bank[q + 1][:], 1, at + 1)
                    if first and j == 0:
                        chain_bc(n, 5)

                for j in range(2):
                    pair(j, idx + 2 * j, None, True)
                with pe.Fori(1, KF // 2) as i:
                    for j in range(2):
                        pair(j, idx + i * 4 + 2 * j, f * KF + i * 2 + j, False)

            def ffn_out(f, idx):
                ob = [bank[i] for i in (4, 5, 6, 7, 0, 1, 2, 3)]

                def k_panel(slot, p_idx, it, kt, first):
                    panel_ready(p_idx)
                    pe.wait_ge(*fin.at(it, "UL"))
                    for d in range(KD):
                        if first and d == 4:
                            pe.wait_ge(*fin.at(f * KF + KF - 1, "B"))
                        last = mm3(ob[d][:], (slot, unit(d)), uh[:, kt, :], ul[:, kt, :], first, False)
                    last.then_inc(panel_done, 1)

                for kt in range(2):
                    k_panel(kt % 2, idx + kt, f * KF + kt, kt, kt == 0)
                with pe.Fori(1, KT_MAJOR // 2) as i:
                    for q in range(2):
                        k_panel(q, idx + i * 2 + q, f * KF + i * 2 + q, i * 2 + q, False)
                rest = KF - KT_MAJOR
                pe.wait_ge(*fin.at(f * KF + KF - 1, "UL"))
                for u in range(KD * rest):
                    p, d, kt = u // UNITS, u // rest, KT_MAJOR + u % rest
                    if u % UNITS == 0:
                        panel_ready(idx + KT_MAJOR + p)
                    last = mm3(ob[d][:], (p % 2, unit(u % UNITS)), uh[:, kt, :], ul[:, kt, :], False, kt == KF - 1)
                    if u % UNITS == UNITS - 1:
                        last.then_inc(panel_done, 1)
                    elif kt == KF - 1:
                        last.then_inc(fout.sem, 1)

            def token_major(idx, banks, cols, norm=None):
                for p in range(KD // 2):
                    panel_ready(idx + p)
                    for kk in range(2):
                        k = 2 * p + kk
                        if norm is not None:
                            x_ready(norm, k)
                        for t in range(TT):
                            o = bank[banks[t]][:, 0:cols]
                            w = slice(kk * S, kk * S + cols)
                            tok = slice(t * P, (t + 1) * P)
                            pe.matmul(o, xh[:, k, tok], wh[:, p % 2, w], start=k == 0, stop=False)
                            pe.matmul(o, xl[:, k, tok], wh[:, p % 2, w], start=False, stop=False)
                            last = pe.matmul(o, xh[:, k, tok], wl[:, p % 2, w], start=False, stop=k == KD - 1)
                    last.then_inc(panel_done, 1)
                    if norm is not None and p == 0:
                        chain_col(norm, 0)
                    if norm is not None and p == 2:
                        chain_bc(norm, 1)

            def retention(l, idx):
                with pe.Fori(0, RH) as h:
                    it = l * RH + h
                    at = idx + h * 4
                    pe.wait_ge(*rg.at(l * RH + RH - 1, "T"))
                    col_panel(bank[0][:], 0, at)
                    pe.wait_ge(*ret.before(it))
                    col_panel(bank[1][:], 1, at + 1)
                    col_panel(bank[2][:], 0, at + 2)
                    pe.wait_ge(*ret.at(it, "KR"))
                    for i in range(TT):
                        last = pe.matmul(bank[4 + i][:, 0:S - i * P], kr[:, i * P:(i + 1) * P], qr[:, i * P:S],
                                         start=True, stop=True)
                    last.then_inc(ret_pe.sem, 1)
                    col_panel(bank[3][:], 1, at + 3)
                    pe.wait_ge(*ret.at(it, "P3"))
                    for t in range(TT):
                        for i in range(t + 1):
                            last = pe.matmul(bank[0][:, t * P:(t + 1) * P], pt[:, OFF[i] + (t - i) * P:OFF[i] + (t - i + 1) * P],
                                             v_ret[:, i, bass.ds(h * RDK, RDK)], start=i == 0, stop=i == t)
                    last.then_inc(ret_pe.sem, 1)
                    pe.wait_ge(*ret.at(it, "N3"))
                    for t in range(TT):
                        last = pe.transpose(bank[1][:, t * P:(t + 1) * P], yn[:, t * P:(t + 1) * P], ident)
                    last.then_inc(ret_pe.sem, 1)

            def forgetting(l, idx):
                with pe.Fori(0, FH // 2) as t2:
                    it = l * (FH // 2) + t2
                    pe.wait_ge(*ret.before((l + 1) * RH))
                    col_panel(bank[0][:], 0, idx + t2 * 2)
                    col_panel(bank[1][:], 1, idx + t2 * 2 + 1)
                    pe.wait_ge(*fox.at(it, "K"))
                    for e in range(2):
                        rows = slice(e * FDH, (e + 1) * FDH)
                        for qt in range(TT):
                            b, c = SETS[e][qt]
                            n = (qt + 1) * P
                            q_ = slice(qt * P, n)
                            pe.matmul(bank[b][:, c:c + n], fq[rows, q_], fk[rows, 0:n], start=True, stop=False)
                            pe.matmul(bank[b][:, c:c + n], cst[0:FH, C_M8:C_M8 + P], cm[0:FH, e, 0:n],
                                      start=False, stop=False)
                            last = pe.matmul(bank[b][:, c + n - P:c + n], ident, causal, start=False, stop=True)
                        last.then_inc(fox_pe.sem, 1)
                    for e, (x_, ev, o_) in enumerate((("XA", ("EA0", "EA", "EA2"), "OA"),
                                                      ("XB", ("EB0", "EB", "EB2"), "OB"))):
                        pe.wait_ge(*fox_act.at(it, x_))
                        if e == 0:
                            pe.wait_ge(*fox.before(it))
                            pe.wait_ge(*fox_act.before(it))
                        else:
                            pe.wait_ge(*fox_act.at(it, "EA2"))
                            pe.wait_ge(*fox.at(it, "EA"))
                        transposes(fp[:, e, :], fox_pe.sem, lambda: pe.wait_ge(*fox_act.at(it, ev[0])))
                        pe.wait_ge(*fox_act.at(it, ev[2]))
                        pe.wait_ge(*fox.at(it, ev[1]))
                        for qt in range(TT):
                            for j in range(qt + 1):
                                blk = FIRST_BLOCK[qt] + j
                                last = pe.matmul(bank[3 + 2 * e][:, qt * FDH:(qt + 1) * FDH],
                                                 fpt[:, blk * P:(blk + 1) * P],
                                                 v_fox[:, j, bass.ds(t2 * P + e * FDH, FDH)],
                                                 start=j == 0, stop=j == qt)
                        last.then_inc(fox_pe.sem, 1)
                    pe.wait_ge(*fox.at(it, "OB"))
                    pe.wait_ge(*fox_act.at(it, "EB2"))
                    for t in range(TT):
                        last = pe.transpose(bank[6][:, t * P:(t + 1) * P], fo[:, t, :], ident)
                    last.then_inc(fox_pe.sem, 1)

            def transposes(p_, sem_, wait_bank6):
                for j, blk in enumerate((6, 7, 8, 9)):
                    last = pe.transpose(bank[6][:, j * P:(j + 1) * P], p_[:, blk * P:(blk + 1) * P], ident)
                last.then_inc(sem_, 1)
                for j, blk in enumerate((0, 3, 4, 5)):
                    last = pe.transpose(bank[7][:, j * P:(j + 1) * P], p_[:, blk * P:(blk + 1) * P], ident)
                last.then_inc(sem_, 1)
                wait_bank6()
                for j, blk in enumerate((1, 2)):
                    last = pe.transpose(bank[6][:, j * P:(j + 1) * P], p_[:, blk * P:(blk + 1) * P], ident)
                last.then_inc(sem_, 1)

            def merge(l, idx):
                def tile(d, q, it, first):
                    b = bank[3 * q:3 * q + 3]
                    if not first:
                        pe.wait_ge(*mrg_d.at(it - 2, "F"))
                    col_panel(b[0][:], 0, idx + d * 2)
                    panel_ready(idx + d * 2 + 1)
                    for k in range(RH):
                        mm3(b[1][:], (1, unit(k)), yrh[:, k, :], yrl[:, k, :], k == 0, k == RH - 1)
                    for k in range(FH // 2):
                        last = mm3(b[2][:], (1, unit(RH + k)), yfh[:, k, :], yfl[:, k, :], k == 0, k == FH // 2 - 1)
                    last.then_inc(panel_done, 1)

                pe.wait_ge(*fox.before((l + 1) * (FH // 2)))
                for q in range(2):
                    tile(q, q, l * KD + q, True)
                with pe.Fori(1, KD // 2) as i:
                    for q in range(2):
                        tile(i * 2 + q, q, l * KD + i * 2 + q, False)

            def mix_out(l, n, idx):
                for d in range(KD):
                    if d >= 2:
                        pe.wait_ge(*prep.at(n * KD + d - 2, "X"))
                    panel_ready(idx + d)
                    for k in range(KD):
                        if d == 0:
                            pe.wait_ge(*mrg_d.at(l * KD + k, "L"))
                        last = mm3(bank[6 + d % 2][:], (d % 2, unit(k)), mh[:, k, :], ml[:, k, :],
                                   k == 0, k == KD - 1)
                    last.then_inc(panel_done, 1)

            def mla_scores(m, h):
                for qt in range(TT):
                    b, c = SETS[h % 2][qt]
                    n = (qt + 1) * P
                    pe.matmul(bank[b][:, c:c + n], mq[0:MLA_K, h, qt * P:n], mk[0:MLA_K, h, 0:n],
                              start=True, stop=False)
                    last = pe.matmul(bank[b][:, c + n - P:c + n], ident, causal, start=False, stop=True)
                last.then_inc(mla_sc.sem, 1)

            def mla_values(m, h):
                it = m * MH + h
                pe.wait_ge(*mla_ex.at(it, "X"))
                transposes(pr[:, h % 2, :], mla_pe.sem, lambda: pe.wait_ge(*mla_ev.at(it, "E0")))
                pe.wait_ge(*mla_ev.at(it, "E2"))
                pe.wait_ge(*mla_dve.at(it, "E"))
                for qt in range(TT):
                    for j in range(qt + 1):
                        blk = FIRST_BLOCK[qt] + j
                        last = pe.matmul(bank[3 + 2 * (h % 2)][:, qt * M_V:(qt + 1) * M_V],
                                         prt[:, blk * P:(blk + 1) * P], vm[:, j, h * M_V:(h + 1) * M_V],
                                         start=j == 0, stop=j == qt)
                last.then_inc(mla_pe.sem, 1)

            SWA_SETS = ((2, 4, 3), (1, 0, 5))

            def swa_scores(m, h):
                rows = slice(SDH * (h // 2), SDH * (h // 2 + 1))
                for qt in range(TT):
                    o = bank[SWA_SETS[h % 2][qt // 2]]
                    c = 2 * P * (qt % 2)
                    mask = C_SWA if qt else C_SWA0
                    k0 = max(qt - 1, 0) * P
                    n = (qt + 1) * P - k0
                    pe.matmul(o[:, c:c + 2 * P], ident, cst[:, mask:mask + 2 * P], start=True, stop=False)
                    last = pe.matmul(o[:, c + 2 * P - n:c + 2 * P], aq[rows, h % 2, qt * P:(qt + 1) * P],
                                     ak[rows, k0:k0 + n], start=False, stop=True)
                last.then_inc(swa_sc.sem, 1)

            def swa_values(m, h):
                it = m * SWH + h
                pe.wait_ge(*swa_ex.at(it, "X"))
                if h == 0:
                    pe.wait_ge(*mla_ev.at(m * MH + MH - 1, "E2"))
                    pe.wait_ge(*mla_dve.at(m * MH + MH - 1, "E"))
                for b, blocks in ((6, (4, 5, 6, 7)), (7, (1, 2, 3))):
                    for j, blk in enumerate(blocks):
                        last = pe.transpose(bank[b][:, j * P:(j + 1) * P], pr[:, h % 2, blk * P:(blk + 1) * P], ident)
                    last.then_inc(swa_pe.sem, 1)
                pe.wait_ge(*swa_ev.at(it, "E0"))
                pe.wait_ge(*swa_dve.at(it, "E"))
                for qt in range(TT):
                    for j in range(max(qt - 1, 0), qt + 1):
                        blk = 2 * qt + j - qt + 1
                        last = pe.matmul(bank[SWA_SETS[h % 2][2]][:, qt * SDH:(qt + 1) * SDH],
                                         prt[:, blk * P:(blk + 1) * P],
                                         vtm[:, j, SDH * (h // 2):SDH * (h // 2 + 1)],
                                         start=j == max(qt - 1, 0), stop=j == qt)
                last.then_inc(swa_pe.sem, 1)

            STICK = ((0, 0), (1, 0), (2, 0), (1, 384))
            STICK_BANKS = ((2, 3, 4), (1, 5, 0))

            def stick_scores(m, h):
                rows = slice(BDH * (h % 2), BDH * (h % 2 + 1))
                for j in range(TT):
                    b, c = STICK[j]
                    n = S - j * P
                    last = pe.matmul(bank[STICK_BANKS[h % 2][b]][:, c:c + n], dk[rows, h // 2, j * P:(j + 1) * P],
                                     dq[rows, h // 2, j * P:S], start=True, stop=True)
                last.then_inc(sb_sc.sem, 1)

            def stick_after(m, h):
                pe.wait_ge(*sb_keep.at(m * BH + h, "K"))
                for i in range(TT):
                    b, c = STICK[i]
                    o = bank[STICK_BANKS[h % 2][b]]
                    for j in range(i, TT):
                        n = S - j * P
                        at = STICK_AT[j]
                        tri = cst[:, C_NTRI:C_NTRI + P] if j == i else cst[:, C_NONE:C_NONE + P]
                        pe.matmul(o[:, c + (j - i) * P:c + S - i * P], tri, spl[:, h % 2, at:at + n],
                                  start=j == i, stop=False)
                    last = pe.matmul(o[:, c:c + P], ident, cst[:, C_STRICT:C_STRICT + P], start=False, stop=True)
                last.then_inc(sb_pe.sem, 1)

            def stick_values(m, h):
                pe.wait_ge(*sb_act.at(m * BH + h, "P"))
                for qt in range(TT):
                    for j in range(qt + 1):
                        at = STICK_AT[j] + (qt - j) * P
                        last = pe.matmul(bank[6 + h % 2][:, qt * BDH:(qt + 1) * BDH], lsg[:, h % 2, at:at + P],
                                         vtm[:, j, 2 * SDH + h * BDH:2 * SDH + (h + 1) * BDH],
                                         start=j == 0, stop=j == qt)
                last.then_inc(sb_pe.sem, 1)

            def hybrid(m):
                q0 = SECOND + m * LAYER2
                n = FINAL + 1 + m
                token_major(q0 + BT_TM, (4, 5, 6, 7), TM_COLS, n)
                col_panel(bank[2][:], 0, q0 + BT_CQ)
                col_panel(bank[3][:], 1, q0 + BT_CQ + 1)
                pe.wait_ge(*chain.at(n, "RB"))
                col_panel(bank[0][:], 0, q0 + BT_CKV)
                col_panel(bank[1][:], 1, q0 + BT_AK)
                pe.wait_ge(*pj.at(m, "T1"))
                pe.wait_ge(*lat.at(m, "SUM"))
                pe.matmul(bank[4][:], ones, qsq[:, 0, :], start=True, stop=True).then_inc(lat_pe.sem, 1)
                pe.wait_ge(*lat_act.at(m, "SK"))
                pe.matmul(bank[5][:], ones, ksq[:], start=True, stop=True).then_inc(lat_pe.sem, 1)
                for i, (b, free) in enumerate(((2, "Q0"), (3, "Q1"), (0, "KV"), (1, "AK"), (2, "A0"), (3, "A1"))):
                    pe.wait_ge(*pj.at(m, free))
                    col_panel(bank[b][:], i % 2, q0 + BT_AQ + i)
                pe.wait_ge(*lat.at(m, "LK"))
                panel_ready(q0 + BT_UQ)
                for h in range(MH):
                    for k in range(2):
                        last = mm3(bank[4 + h][:], (0, unit(2 * h + k)), cqh[:, k, :], cql[:, k, :], k == 0, k == 1)
                last.then_inc(panel_done, 1)
                panel_ready(q0 + BT_UKV)
                for h in range(MH):
                    pe.wait_ge(*pj.at(m, ("D0", "D1", "E0", "E1")[h]))
                    mm3(bank[h][:], (1, slice(h * M_NOPE, h * M_NOPE + P)), ckh[:], ckl[:], True, True)
                for t in range(TT):
                    if t % 2 == 0:
                        pe.wait_ge(*mla.at(m, f"R{t // 2}"))
                    o = bank[4 + t // 2][:, (t % 2) * GROUP:(t % 2 + 1) * GROUP]
                    w = slice(MH * M_NOPE, MH * (M_NOPE + M_V))
                    tok = slice(t * P, (t + 1) * P)
                    pe.matmul(o, ckh[:, tok], wh[:, 1, w], start=True, stop=False)
                    pe.matmul(o, ckl[:, tok], wh[:, 1, w], start=False, stop=False)
                    pe.matmul(o, ckh[:, tok], wl[:, 1, w], start=False, stop=True)
                pe.wait_ge(*mla.at(m, "R2"))
                for k in range(KD):
                    c = KR_AT + k * KR_W
                    last = mm3(bank[6][:], (1, slice(c, c + P)), xh[:, k, :], xl[:, k, :], k == 0, k == KD - 1)
                last.then_inc(panel_done, 1)
                for i in range(2):
                    for j in range(3):
                        if i == 0:
                            pe.wait_ge(*kv_act.at(m, f"N{j}"))
                        elif j == 0:
                            pe.wait_ge(*kv.at(m, "V1"))
                        elif j == 1:
                            pe.wait_ge(*kv.at(m, "KS"))
                        else:
                            pe.wait_ge(*mla.at(m, "R3"))
                        c = 3 * i + j
                        col_panel(bank[(0, 1, 2, 5, 6, 7)[c]][:], c % 2, q0 + BT_CONV + c)
                pe.wait_ge(*kv_act.at(m, "C3"))
                pe.wait_ge(*kv.at(m, "KR"))
                pe.wait_ge(*conv.at(m * 2, "G"))
                mla_scores(m, 0)
                pe.wait_ge(*conv.at(m * 2 + 1, "Y"))
                for h in range(MH):
                    if h < MH - 1:
                        if h:
                            pe.wait_ge(*mla_dve.at(m * MH + h - 1, "O"))
                        mla_scores(m, h + 1)
                    else:
                        pe.wait_ge(*mla_dve.at(m * MH + h - 1, "O"))
                        swa_scores(m, 0)
                    mla_values(m, h)
                for h in range(SWH):
                    pe.wait_ge(*(swa_dve.at(m * SWH + h - 1, "O") if h else mla_dve.at(m * MH + MH - 1, "O")))
                    if h < SWH - 1:
                        swa_scores(m, h + 1)
                    else:
                        stick_scores(m, 0)
                    swa_values(m, h)
                for h in range(BH):
                    if h == 0:
                        pe.wait_ge(*swa_dve.at(m * SWH + SWH - 1, "O"))
                        pe.wait_ge(*swa_ev.at(m * SWH + SWH - 1, "E0"))
                    if h < BH - 1:
                        if h:
                            pe.wait_ge(*sb_dve.at(m * BH + h - 1, "T"))
                        stick_scores(m, h + 1)
                    stick_after(m, h)
                    if h >= 2:
                        pe.wait_ge(*sb_act.at(m * BH + h - 2, "O"))
                    stick_values(m, h)
                def turn(y, i):
                    pe.wait_ge(*gn.at(m, f"N{i}"))
                    for c in range(2):
                        for t in range(TT):
                            last = pe.transpose(bank[2 + 2 * i + c][:, t * P:(t + 1) * P], y[:, t, c * P:(c + 1) * P],
                                                ident)
                    last.then_inc(gn_pe.sem, 1)

                pe.wait_ge(*sb_dve.at(m * BH + BH - 1, "T"))
                pe.wait_ge(*gn.at(m, "SUM"))
                pe.matmul(bank[0][:], ones, bsq[:, 0, :], start=True, stop=True).then_inc(gn_pe.sem, 1)
                col_panel(bank[1][:], 0, q0 + BT_GATE)
                turn(y_swa, 0)
                turn(y_mla, 1)
                pe.wait_ge(*gn_act.at(m, "DB"))
                col_panel(bank[0][:], 1, q0 + BT_GATE + 1)
                pe.wait_ge(*sb_act.at(m * BH + BH - 1, "O"))
                turn(y_sb, 2)
                for d in range(2, KD):
                    pe.wait_ge(*gate.at(m * KD + d - 2, "G"))
                    col_panel(bank[(d + 1) % 2][:], d % 2, q0 + BT_GATE + d)
                for d in range(KD):
                    if d < 2:
                        pe.wait_ge(*gn.at(m, f"A{d}"))
                    else:
                        pe.wait_ge(*z_act.at(m * KD + d - 2, "Z"))
                    panel_ready(q0 + BT_WOUT + d)
                    for k in range(KD):
                        if d == 0:
                            pe.wait_ge(*gate.at(m * KD + k, "L"))
                        last = mm3(bank[2 + d % 2][:], (d % 2, unit(k)), ygh[:, k, :], ygl[:, k, :], k == 0, k == KD - 1)
                    last.then_inc(panel_done, 1)
                pe.wait_ge(*z_sum.at(m * KD + KD - 1, "A"))
                for t in range(TT):
                    last = pe.matmul(bank[4][:, t:t + 1], ssq[:, t * P:(t + 1) * P], ones[:, 0:1], start=True, stop=True)
                last.then_inc(post_pe.sem, 1)
                pe.wait_ge(*post.at(m, "DG"))
                pe.matmul(bank[5][:], ones, diag[:], start=True, stop=True).then_inc(post_pe.sem, 1)

            pe.wait_ge(loaded, 64)
            with pe.Fori(0, DEPTH) as l:
                p0 = l * LAYER1
                ffn_in(l * 2, l * 3, p0)
                ffn_out(l * 2, p0 + FFN_IN)
                n = l * 3 + 1
                for t in range(TT):
                    pe.wait_ge(*prep.at(n * KD + t, "X"))
                token_major(p0 + AT_RV, (4, 5, 6, 7), S, n)
                pe.wait_ge(*chain.at(n, "RB"))
                token_major(p0 + AT_FV, (0, 1, 2, 3), S)
                pe.wait_ge(*tm.at(l, "RV3"))
                pe.wait_ge(*ffs.at(l, "L"))
                for k in range(KD):
                    c = slice(k * FH, k * FH + P)
                    pe.matmul(bank[4][:], ffh[:, c], xh[:, k, :], start=k == 0, stop=False)
                    pe.matmul(bank[4][:], ffh[:, c], xl[:, k, :], start=False, stop=False)
                    last = pe.matmul(bank[4][:], ffl[:, c], xh[:, k, :], start=False, stop=k == KD - 1)
                last.then_inc(ffs_pe.sem, 1)
                with pe.Fori(0, RH // 2) as i:
                    for q in range(2):
                        pe.wait_ge(*tm.at(l, "FV3"))
                        pe.wait_ge(*rg.before(l * RH + i * 2))
                        col_panel(bank[q][:], q, p0 + AT_RG + i * 2 + q)
                retention(l, p0 + AT_RET)
                forgetting(l, p0 + AT_FOX)
                merge(l, p0 + AT_MERGE)
                mix_out(l, n + 1, p0 + AT_WOUT)
                ffn_in(l * 2 + 1, l * 3 + 2, p0 + AT_FFN2)
                ffn_out(l * 2 + 1, p0 + AT_FFN2 + FFN_IN)

            chain_col(FINAL, 4)
            chain_bc(FINAL, 5)
            with pe.Fori(0, DEPTH) as m:
                hybrid(m)

        @block.scalar
        def _(act):
            def squares(n):
                with act.Fori(0, KD) as d:
                    act.wait_ge(*prep.at(n * KD + d, "X"))
                    act.activation(sq[:], x[:, d, :], ACT.Square).then_inc(prep_sq.sem, 1)

            def chain_std(n, b):
                act.wait_ge(*chain_pe.at(n, "COL"))
                act.activation(std_col[:], bank[b][:, 0:TT], ACT.Sqrt, bias=eps[:], scale=1.0 / D)\
                   .then_inc(chain_sd.sem, 1)

            def ffn_in(f, n):
                chain_std(n, 4)
                with act.Fori(0, KF) as j:
                    it = f * KF + j
                    act.wait_ge(*fin.at(it, "A"))
                    act.activation(sa[:], ta[:], ACT.Silu).then_inc(fin_act.sem, 1)
                    act.wait_ge(*fin.at(it, "U"))
                    act.activation(uh[:, j, :], u32[:], ACT.Copy).then_inc(fin_act.sem, 1)

            def retention(l):
                with act.Fori(0, RH) as h:
                    it = l * RH + h
                    for src, name in ((tq, "Q"), (tk, "K")):
                        act.wait_ge(*ret.at(it, name))
                        if name == "K":
                            act.wait_ge(*ret.at(it, "QS"))
                        act.activation(sw[0:64, :], src[64:128, :], ACT.Copy).then_inc(ret_act.sem, 1)
                        act.activation(sw[64:128, :], src[0:64, :], ACT.Copy).then_inc(ret_act.sem, 1)
                    act.wait_ge(*ret_pe.at(it, "PV"))
                    for t in range(TT):
                        act.activation(sw[:, t * P:(t + 1) * P], bank[0][:, t * P:(t + 1) * P], ACT.Square,
                                       accum_out=hsum[:, t:t + 1]).then_inc(ret_act.sem, 1)
                    act.wait_ge(*ret_act.at(it, "S3"))
                    act.activation(hstd[:], hsum[:], ACT.Sqrt, bias=eps[:], scale=1.0 / RDK).then_inc(ret_act.sem, 1)
                    act.wait_ge(*ret.at(it, "Y"))
                    act.activation(yrh[:, h, :], y32[:], ACT.Copy).then_inc(ret_act.sem, 1)

            def forgetting(l):
                with act.Fori(0, FH // 2) as t2:
                    it = l * (FH // 2) + t2
                    for e, name in enumerate(("NA", "NB")):
                        act.wait_ge(*fox.at(it, name))
                        for qt in range(TT):
                            b, c = SETS[e][qt]
                            n = (qt + 1) * P
                            last = act.activation(fp[:, e, FIRST_BLOCK[qt] * P:FIRST_BLOCK[qt] * P + n], bank[b][:, c:c + n],
                                                  ACT.Exp, bias=fnm[:, e, qt:qt + 1], scale=FDH ** -0.5,
                                                  accum_out=fsum[:, e, qt:qt + 1])
                        last.then_inc(fox_act.sem, 1)
                    for e, (t0, t2_, v) in enumerate((("TA0", "TA2", None), ("TB0", "TB2", "VA"))):
                        act.wait_ge(*fox_pe.at(it, t0))
                        if v:
                            act.wait_ge(*fox_pe.at(it, v))
                        act.activation(fpt[:, 6 * P:10 * P], bank[6][:], ACT.Copy).then_inc(fox_act.sem, 1)
                        act.wait_ge(*fox_pe.at(it, t2_))
                        act.activation(fpt[:, P:3 * P], bank[6][:, 0:2 * P], ACT.Copy).then_inc(fox_act.sem, 1)
                    act.wait_ge(*fox_pe.at(it, "TR"))
                    act.activation(yfh[:, t2, :], bank[6][:], ACT.Copy).then_inc(fox_act.sem, 1)

            def mla_probs(m, h):
                it = m * MH + h
                act.wait_ge(*mla_mx.at(it, "N"))
                for qt in range(TT):
                    b, c = SETS[h % 2][qt]
                    n = (qt + 1) * P
                    at = FIRST_BLOCK[qt] * P
                    last = act.activation(pr[:, h % 2, at:at + n], bank[b][:, c:c + n], ACT.Exp,
                                          bias=snm[:, h % 2, qt:qt + 1], scale=(M_NOPE + M_ROPE) ** -0.5,
                                          accum_out=ssum[:, h % 2, qt:qt + 1])
                last.then_inc(mla_ex.sem, 1)

            def swa_probs(m, h):
                it = m * SWH + h
                act.wait_ge(*swa_mx.at(it, "N"))
                for qt in range(TT):
                    o = bank[((2, 4), (1, 0))[h % 2][qt // 2]]
                    c = 2 * P * (qt % 2)
                    last = act.activation(pr[:, h % 2, qt * 2 * P:(qt + 1) * 2 * P], o[:, c:c + 2 * P], ACT.Exp,
                                          bias=snm[:, h % 2, qt:qt + 1], scale=SDH ** -0.5,
                                          accum_out=ssum[:, h % 2, qt:qt + 1])
                last.then_inc(swa_ex.sem, 1)
                act.activation(esk[:, h % 2, :], snm[:, h % 2, :], ACT.Exp,
                               bias=vecs[:, bass.ds(m * SWH + V_SINK + h, 1)]).then_inc(swa_ex.sem, 1)

            PIECES = ((0, 0, 512), (1, 512, 512), (2, 1024, 256))

            def stick_logs(m, h):
                it = m * BH + h
                buf = lsg[:, h % 2, :]
                act.wait_ge(*sb_sc.at(it, "Z"))
                for b, c, n in PIECES:
                    last = act.activation(buf[:, c:c + n], bank[((2, 3, 4), (1, 5, 0))[h % 2][b]][:, 0:n], ACT.Abs)
                last.then_inc(sb_ln.sem, 1)
                act.wait_ge(*sb_ln.at(it, "AB"))
                act.activation(buf, buf, ACT.Exp, scale=-1.0).then_inc(sb_ln.sem, 1)
                act.wait_ge(*sb_ln.at(it, "EX"))
                act.activation(buf, buf, ACT.Ln, bias=ones[:, 0:1]).then_inc(sb_ln.sem, 1)

            def hybrid(m):
                n = FINAL + 1 + m
                chain_std(n, 0)
                for i in range(2):
                    act.wait_ge(*pj.at(m, f"Q{i}"))
                    act.activation(qsq[:, i, :], cq[:, i, :], ACT.Square).then_inc(lat_act.sem, 1)
                act.wait_ge(*pj.at(m, "KV"))
                act.activation(ksq[:], ckv[:], ACT.Square).then_inc(lat_act.sem, 1)
                act.wait_ge(*lat_pe.at(m, "Q"))
                act.activation(qin[:], bank[4][:], ACT.Sqrt, bias=eps[:], scale=1.0 / QR).then_inc(lat_act.sem, 1)
                act.wait_ge(*lat_pe.at(m, "K"))
                act.activation(kin[:], bank[5][:], ACT.Sqrt, bias=eps[:], scale=1.0 / KVR).then_inc(lat_act.sem, 1)
                for name, dst in (("N0", cqh[:, 0, :]), ("N1", cqh[:, 1, :]), ("NK", ckh[:])):
                    act.wait_ge(*lat.at(m, name))
                    act.activation(dst, cn[:], ACT.Copy).then_inc(lat_act.sem, 1)
                act.wait_ge(panel_done, SECOND + m * LAYER2 + BT_UQ + 1)
                act.wait_ge(*mla.at(m, "Z"))
                for h in range(MH):
                    b = bank[4 + h]
                    act.activation(mq[0:M_NOPE, h, :], b[0:M_NOPE, :], ACT.Copy).then_inc(mla_act.sem, 1)
                    if h:
                        act.wait_ge(*mla.at(m, f"S{h - 1}"))
                    act.activation(msw[64:80, :], b[96:112, :], ACT.Copy).then_inc(mla_act.sem, 1)
                    act.activation(msw[96:112, :], b[64:80, :], ACT.Copy).then_inc(mla_act.sem, 1)
                act.wait_ge(panel_done, SECOND + m * LAYER2 + BT_UKV + 1)
                for h in range(MH):
                    act.activation(mk[0:M_NOPE, h, :], bank[h][0:M_NOPE, :], ACT.Copy).then_inc(kv_act.sem, 1)
                act.wait_ge(*kv.at(m, "KS"))
                act.wait_ge(*mla.at(m, f"S{MH - 1}"))
                act.activation(kx[64:112, :], krs[0:KR_W, :], ACT.Copy).then_inc(kv_act.sem, 1)
                act.activation(msw[64:80, :], krs[32:48, :], ACT.Copy).then_inc(kv_act.sem, 1)
                act.activation(msw[96:112, :], krs[0:16, :], ACT.Copy).then_inc(kv_act.sem, 1)
                act.wait_ge(*kv.at(m, "KR"))
                for h in range(1, MH):
                    act.activation(mk[64:112, h, :], mk[64:112, 0, :], ACT.Copy).then_inc(kv_act.sem, 1)
                mla_probs(m, 0)
                for h in range(MH):
                    it = m * MH + h
                    if h < MH - 1:
                        mla_probs(m, h + 1)
                    else:
                        swa_probs(m, 0)
                    act.wait_ge(*mla_pe.at(it, "T0"))
                    act.activation(prt[:, 6 * P:10 * P], bank[6][:], ACT.Copy).then_inc(mla_ev.sem, 1)
                    act.wait_ge(*mla_pe.at(it, "T2"))
                    act.activation(prt[:, P:3 * P], bank[6][:, 0:2 * P], ACT.Copy).then_inc(mla_ev.sem, 1)
                for h in range(SWH):
                    it = m * SWH + h
                    if h < SWH - 1:
                        swa_probs(m, h + 1)
                    act.wait_ge(*swa_pe.at(it, "T0"))
                    act.activation(prt[:, 4 * P:8 * P], bank[6][:], ACT.Copy).then_inc(swa_ev.sem, 1)
                stick_logs(m, 0)
                for h in range(BH):
                    it = m * BH + h
                    if h < BH - 1:
                        if h:
                            act.wait_ge(*sb_pe.at(it - 1, "V"))
                        stick_logs(m, h + 1)
                    act.wait_ge(*sb_dve.at(it, "T"))
                    act.activation(lsg[:, h % 2, :], lsg[:, h % 2, :], ACT.Exp).then_inc(sb_act.sem, 1)
                    act.wait_ge(*sb_pe.at(it, "V"))
                    act.activation(y_sb[:, :, h * BDH:(h + 1) * BDH],
                                   bank[6 + h % 2][:, 0:TT * BDH].rearrange("p (t c) -> p t c", c=BDH),
                                   ACT.Copy).then_inc(sb_act.sem, 1)
                for i in range(2):
                    act.activation(bsq[:, i, :], y_conv[:, i, :], ACT.Square).then_inc(gn_act.sem, 1)
                for i, y in enumerate((y_swa, y_mla, y_sb)):
                    if i == 0:
                        act.wait_ge(*swa_dve.at(m * SWH + SWH - 1, "O"))
                    else:
                        act.wait_ge(*gn_act.at(m, f"S{i - 1}"))
                    if i == 2:
                        act.wait_ge(*sb_act.at(m * BH + BH - 1, "O"))
                    for t in range(TT):
                        last = act.activation(gsq[:, t, :], y[:, t, :], ACT.Square, accum_out=gsum[:, i, t:t + 1])
                    last.then_inc(gn_act.sem, 1)
                act.wait_ge(*gn_pe.at(m, "B"))
                act.activation(bstd[:], bank[0][:], ACT.Sqrt, bias=eps[:], scale=1.0 / GROUP).then_inc(gn_act.sem, 1)
                for i in range(3):
                    act.wait_ge(*gn_act.at(m, f"S{i}"))
                    act.activation(gstd[:, i, :], gsum[:, i, :], ACT.Sqrt, bias=eps[:], scale=1.0 / GROUP)\
                       .then_inc(gn_act.sem, 1)
                for d in range(KD):
                    it = m * KD + d
                    act.wait_ge(*gate.at(it, "G"))
                    act.activation(gs[:], gt[:], ACT.Silu).then_inc(gate_act.sem, 1)
                    act.wait_ge(*gate.at(it, "Y"))
                    act.activation(ygh[:, d, :], yg[:], ACT.Copy).then_inc(gate_act.sem, 1)
                for d in range(KD):
                    it = m * KD + d
                    act.wait_ge(panel_done, SECOND + m * LAYER2 + BT_WOUT + d + 1)
                    act.activation(z[:, d, :], bank[2 + d % 2][:], ACT.Copy).then_inc(z_act.sem, 1)
                    act.wait_ge(*z_act.at(it, "Z"))
                    if d:
                        act.wait_ge(*z_sum.at(it - 1, "A"))
                    act.activation(sq[:], z[:, d, :], ACT.Square).then_inc(z_act.sem, 1)
                act.wait_ge(*post_pe.at(m, "COL"))
                act.activation(std_col[:], bank[4][:, 0:TT], ACT.Sqrt, bias=eps[:], scale=1.0 / D)\
                   .then_inc(post_sd.sem, 1)
                squares(n + 1)

            act.wait_ge(loaded, 64)
            act.wait_ge(memsets, 1)
            for i, st in enumerate((rg_act, fox_act)):
                act.activation(start_a[:, i:i + 1], eps[:], ACT.Copy).then_inc(st.sem, 1)
            squares(0)
            act.wait_ge(*trig.at(0, "s5"))
            act.activation(sin2[64:112, :], ang[64:112, :], ACT.Sin).then_inc(trig_act.sem, 1)
            act.wait_ge(*trig.at(0, "c5"))
            act.activation(cos2[64:112, :], turn[64:112, :], ACT.Sin).then_inc(trig_act.sem, 1)
            with act.Fori(0, DEPTH) as l:
                ffn_in(l * 2, l * 3)
                squares(l * 3 + 1)
                act.wait_ge(*prep.at((l * 3 + 1) * KD + KD - 1, "X"))
                act.dma_start(dec[:], decay).then_inc(tab_in, 16)
                act.dma_start(rp[:], rope).then_inc(tab_in, 16)
                act.dma_start(ffraw[:], ff_w).then_inc(tab_in, 16)
                chain_std(l * 3 + 1, 0)
                act.wait_ge(*ffs.at(l, "ZB"))
                act.activation(fa[0:FH], fz[0:FH], ACT.Abs).then_inc(ffs_act.sem, 1)
                act.wait_ge(*ffs_act.at(l, "ABS"))
                act.activation(fa[0:FH], fa[0:FH], ACT.Exp, scale=-1.0).then_inc(ffs_act.sem, 1)
                act.wait_ge(*ffs_act.at(l, "EXP"))
                act.activation(fa[0:FH], fa[0:FH], ACT.Ln, bias=ones[0:FH, 0:1]).then_inc(ffs_act.sem, 1)
                with act.Fori(0, RH) as h:
                    act.wait_ge(*rg.at(l * RH + h, "T"))
                    act.activation(rgs[:, h, :], tg[:], ACT.Silu).then_inc(rg_act.sem, 1)
                retention(l)
                forgetting(l)
                with act.Fori(0, KD) as d:
                    it = l * KD + d
                    act.wait_ge(*mrg_d.at(it, "G"))
                    act.activation(sr[:], gate_r[:, d, :], ACT.Sigmoid).then_inc(mrg_a.sem, 1)
                    act.activation(sf[:], tgf[:], ACT.Sigmoid).then_inc(mrg_a.sem, 1)
                    act.wait_ge(*mrg_d.at(it, "M"))
                    act.activation(mh[:, d, :], mg[:], ACT.Copy).then_inc(mrg_a.sem, 1)
                squares(l * 3 + 2)
                ffn_in(l * 2 + 1, l * 3 + 2)
                squares(l * 3 + 3)
            chain_std(FINAL, 4)
            squares(FINAL + 1)
            with act.Fori(0, DEPTH) as m:
                hybrid(m)

        @block.vector
        def _(dve):
            def prepare(n, d, g):
                gain = vecs[:, bass.ds(g * KD + d, 1)]
                dve.wait_ge(*prep.at(n * KD + d, "X"))
                dve.tensor_scalar(xh[:, d, :], x[:, d, :], gain, None, ALU.mult).then_inc(prep.sem, 1)
                dve.wait_ge(*prep.at(n * KD + d, "XH"))
                dve.scalar_tensor_tensor(out=xl[:, d, :], in0=x[:, d, :], scalar=gain,
                                         in1=xh[:, d, :].bitcast(F32), op0=ALU.mult,
                                         op1=ALU.subtract).then_inc(prep.sem, 1)

            def add_squares(n, d, first):
                dve.wait_ge(*prep_sq.at(n * KD + d, "SQ"))
                if first:
                    dve.tensor_copy(ssq[:], sq[:]).then_inc(prep.sem, 1)
                else:
                    dve.tensor_tensor(ssq[:], ssq[:], sq[:], ALU.add).then_inc(prep.sem, 1)

            def norm_chain(n, b):
                dve.wait_ge(*chain_sd.at(n, "SD"))
                dve.reciprocal(rstd_col[:], std_col[:]).then_inc(chain.sem, 1)
                dve.wait_ge(*chain.at(n, "RC"))
                for t in range(TT):
                    last = dve.tensor_scalar(diag[:, t * P:(t + 1) * P], ident, rstd_col[:, t:t + 1], None, ALU.mult)
                last.then_inc(chain.sem, 1)
                dve.wait_ge(*chain_pe.at(n, "BC"))
                dve.tensor_copy(rstd[:], bank[b][:]).then_inc(chain.sem, 1)

            def scaled(dst, src, st):
                dve.tensor_tensor(dst, src, rstd[:], ALU.mult).then_inc(st.sem, 1)

            def ffn_in(f, n, idx):
                norm_chain(n, 5)
                with dve.Fori(0, KF // 2) as i:
                    dve.wait_ge(*chain.at(n, "RB"))
                    for q in range(2):
                        it = f * KF + i * 2 + q
                        at = idx + i * 4 + 2 * q
                        dve.wait_ge(panel_done, at + 1)
                        scaled(ta[:], bank[2 * q][:], fin)
                        dve.wait_ge(panel_done, at + 2)
                        scaled(tb[:], bank[2 * q + 1][:], fin)
                        dve.wait_ge(*fin_act.at(it, "SILU"))
                        dve.wait_ge(*fin.at(it, "B"))
                        dve.tensor_tensor(u32[:], sa[:], tb[:], ALU.mult).then_inc(fin.sem, 1)
                        dve.wait_ge(*fin_act.at(it, "UH"))
                        dve.tensor_tensor(ul[:, i * 2 + q, :], u32[:], uh[:, i * 2 + q, :].bitcast(F32),
                                          ALU.subtract).then_inc(fin.sem, 1)

            def ffn_out(f, n, idx):
                rest = KF - KT_MAJOR
                steps = 0
                for d in range(KD):
                    done = (d + 1) * rest
                    if done % UNITS == 0:
                        dve.wait_ge(panel_done, idx + KT_MAJOR + done // UNITS)
                    else:
                        dve.wait_ge(fout.sem, f * (KD - 2) + steps + 1)
                        steps += 1
                    dve.scalar_tensor_tensor(out=x[:, d, :], in0=bank[(4 + d) % 8][:], scalar=0.5,
                                             in1=x[:, d, :], op0=ALU.mult, op1=ALU.add).then_inc(prep.sem, 1)
                    prepare(n, d, n)
                    add_squares(n, d, d == 0)

            def retention(l, idx):
                with dve.Fori(0, RH) as h:
                    it = l * RH + h
                    dve.wait_ge(*rg_act.before((l + 1) * RH))
                    at = idx + h * 4
                    dve.wait_ge(*ret.before(it))
                    for k, (dst, b) in enumerate(((tq, 0), (tk, 1))):
                        dve.wait_ge(panel_done, at + k + 1)
                        scaled(dst[:], bank[b][:], ret)
                    for dst, src, name in ((qr, tq, "Q"), (kr, tk, "K")):
                        dve.wait_ge(*ret.at(it, name))
                        if name == "K":
                            dve.wait_ge(*ret.at(it, "QR"))
                        dve.tensor_tensor(m1[:], src[:], rp[:, 0, :], ALU.mult).then_inc(ret.sem, 1)
                        dve.wait_ge(*ret_act.at(it, name + "1"))
                        dve.tensor_tensor(dst[:], sw[:], rp[:, 1, :], ALU.mult).then_inc(ret.sem, 1)
                        dve.wait_ge(*ret.at(it, name + "S"))
                        dve.tensor_tensor(dst[:], dst[:], m1[:], ALU.add).then_inc(ret.sem, 1)
                    dve.wait_ge(panel_done, at + 3)
                    scaled(gate_r[:, h * 2, :], bank[2][:], ret)
                    dve.wait_ge(*ret_pe.at(it, "SC"))
                    for i in range(TT):
                        dve.tensor_tensor(pt[:, OFF[i]:OFF[i] + S - i * P], bank[4 + i][:, 0:S - i * P],
                                          dec[:, h, 0:S - i * P], ALU.mult).then_inc(ret.sem, 1)
                    dve.wait_ge(panel_done, at + 4)
                    scaled(gate_r[:, h * 2 + 1, :], bank[3][:], ret)
                    dve.wait_ge(*ret_act.at(it, "SD"))
                    dve.reciprocal(hinv[:], hstd[:]).then_inc(ret.sem, 1)
                    dve.wait_ge(*ret.at(it, "RC"))
                    for t in range(TT):
                        dve.tensor_scalar(yn[:, t * P:(t + 1) * P], bank[0][:, t * P:(t + 1) * P],
                                          hinv[:, t:t + 1], None, ALU.mult).then_inc(ret.sem, 1)
                    dve.wait_ge(*ret_pe.at(it, "TR"))
                    dve.scalar_tensor_tensor(out=y32[:], in0=bank[1][:], scalar=vecs[:, bass.ds(l * RH + h + V_RET, 1)],
                                             in1=rgs[:, h, :], op0=ALU.mult, op1=ALU.mult).then_inc(ret.sem, 1)
                    dve.wait_ge(*ret_act.at(it, "YH"))
                    dve.tensor_tensor(yrl[:, h, :], y32[:], yrh[:, h, :].bitcast(F32), ALU.subtract)\
                       .then_inc(ret.sem, 1)

            def forgetting(l, idx):
                with dve.Fori(0, FH // 2) as t2:
                    it = l * (FH // 2) + t2
                    dve.wait_ge(*ffs.at(l, "C"))
                    for e in range(2):
                        dve.tensor_scalar(cm[0:FH, e, :], cum[0:FH, :], cst[0:FH, bass.ds(t2 * 2 + C_HOT + e, 1)],
                                          None, ALU.mult).then_inc(fox.sem, 1)
                    for k, dst in enumerate((fq, fk)):
                        dve.wait_ge(panel_done, idx + t2 * 2 + k + 1)
                        scaled(dst[:], bank[k][:], fox)
                    for e, (s_, m_) in enumerate((("SA", "MA"), ("SB", "MB"))):
                        dve.wait_ge(*fox_pe.at(it, s_))
                        for qt in range(TT):
                            b, c = SETS[e][qt]
                            last = dve.tensor_reduce(fmx[:, e, qt:qt + 1], bank[b][:, c:c + (qt + 1) * P], AX_X, ALU.max)
                        last.then_inc(fox.sem, 1)
                        dve.wait_ge(*fox.at(it, m_))
                        dve.tensor_scalar(fnm[:, e, :], fmx[:, e, :], -FDH ** -0.5, None, ALU.mult).then_inc(fox.sem, 1)
                    for e, (t1, x_, v, r, prev) in enumerate((("TA1", "XA", "VA", "RA", None), ("TB1", "XB", "VB", "RB", "VA"))):
                        dve.wait_ge(*fox_pe.at(it, t1))
                        if prev:
                            dve.wait_ge(*fox_pe.at(it, prev))
                        dve.tensor_copy(fpt[:, 0:P], bank[7][:, 0:P])
                        dve.tensor_copy(fpt[:, 3 * P:6 * P], bank[7][:, P:4 * P]).then_inc(fox.sem, 1)
                        dve.wait_ge(*fox_act.at(it, x_))
                        dve.reciprocal(finv[:, e, :], fsum[:, e, :]).then_inc(fox.sem, 1)
                        dve.wait_ge(*fox.at(it, r))
                        dve.wait_ge(*fox_pe.at(it, v))
                        dve.tensor_tensor(
                            fo[:, :, e * FDH:(e + 1) * FDH],
                            bank[3 + 2 * e][:, 0:TT * FDH].rearrange("p (t c) -> p t c", c=FDH),
                            finv[:, e, :].rearrange("p (t c) -> p t c", c=1).to_broadcast([P, TT, FDH]),
                            ALU.mult).then_inc(fox.sem, 1)
                    dve.wait_ge(*fox_act.at(it, "YH"))
                    dve.tensor_tensor(yfl[:, t2, :], bank[6][:], yfh[:, t2, :].bitcast(F32), ALU.subtract)\
                       .then_inc(fox.sem, 1)

            def merge(l, idx):
                with dve.Fori(0, KD // 2) as i:
                    for q in range(2):
                        d = i * 2 + q
                        it = l * KD + d
                        dve.wait_ge(panel_done, idx + i * 4 + 2 * q + 1)
                        scaled(tgf[:], bank[3 * q][:], mrg_d)
                        dve.wait_ge(panel_done, idx + i * 4 + 2 * q + 2)
                        dve.wait_ge(*mrg_a.at(it, "SF"))
                        dve.tensor_tensor(mr[:], bank[3 * q + 1][:], sr[:], ALU.mult).then_inc(mrg_d.sem, 1)
                        dve.tensor_tensor(mf[:], bank[3 * q + 2][:], sf[:], ALU.mult).then_inc(mrg_d.sem, 1)
                        dve.wait_ge(*mrg_d.at(it, "F"))
                        dve.tensor_tensor(mg[:], mr[:], mf[:], ALU.add).then_inc(mrg_d.sem, 1)
                        dve.wait_ge(*mrg_a.at(it, "MH"))
                        dve.tensor_tensor(ml[:, d, :], mg[:], mh[:, d, :].bitcast(F32), ALU.subtract)\
                           .then_inc(mrg_d.sem, 1)

            def angles():
                R = slice(64, 112)
                a, b, p_ = ang[R, :], turn[R, :], rstd[R, :]
                full = 2 * np.pi
                c1 = 6.28125
                c2 = float(np.float32(full - c1))
                c3 = float(full - c1 - c2)
                dve.tensor_copy(p_, posi[R, :]).then_inc(trig.sem, 1)
                dve.wait_ge(*trig.at(0, "F"))
                dve.tensor_scalar(b, p_, cst[R, C_FREQ:C_FREQ + 1], None, ALU.mult).then_inc(trig.sem, 1)
                for w, dst, shift in (("s", a, 0.0), ("c", b, 0.25)):
                    dve.wait_ge(*trig.at(0, "A" if w == "s" else "s5"))
                    dve.tensor_scalar(p_, b, 1 / full, shift, ALU.mult, ALU.add).then_inc(trig.sem, 1)
                    dve.wait_ge(*trig.at(0, w + "0"))
                    dve.tensor_scalar(p_, p_, 12582912.0, 12582912.0, ALU.add, ALU.subtract).then_inc(trig.sem, 1)
                    dve.wait_ge(*trig.at(0, w + "1"))
                    src = b
                    for i, c in enumerate((c1, c2, c3)):
                        dve.scalar_tensor_tensor(out=dst, in0=p_, scalar=-c, in1=src, op0=ALU.mult, op1=ALU.add)\
                           .then_inc(trig.sem, 1)
                        dve.wait_ge(*trig.at(0, w + str(i + 2)))
                        src = dst
                    if w == "s":
                        dve.tensor_scalar(dst, dst, np.pi, -np.pi, ALU.min, ALU.max).then_inc(trig.sem, 1)
                    else:
                        dve.tensor_scalar(dst, dst, np.pi / 2, np.pi, ALU.add, ALU.min).then_inc(trig.sem, 1)
                dve.wait_ge(*trig_act.at(0, "COS"))
                dve.tensor_scalar(sin2[64:96, :], sin2[64:96, :], -1.0, None, ALU.mult).then_inc(trig.sem, 1)

            def mla_max(m, h):
                it = m * MH + h
                dve.wait_ge(*mla_sc.at(it, "SC"))
                for qt in range(TT):
                    b, c = SETS[h % 2][qt]
                    last = dve.tensor_reduce(smx[:, h % 2, qt:qt + 1], bank[b][:, c:c + (qt + 1) * P], AX_X, ALU.max)
                last.then_inc(mla_mx.sem, 1)
                dve.wait_ge(*mla_mx.at(it, "M"))
                dve.tensor_scalar(snm[:, h % 2, :], smx[:, h % 2, :], -(M_NOPE + M_ROPE) ** -0.5, None, ALU.mult)\
                   .then_inc(mla_mx.sem, 1)

            def swa_max(m, h):
                it = m * SWH + h
                dve.wait_ge(*swa_sc.at(it, "SC"))
                for i, b in enumerate(((2, 4), (1, 0))[h % 2]):
                    last = dve.tensor_reduce(smx[:, h % 2, 2 * i:2 * i + 2],
                                             bank[b][:].rearrange("p (t k) -> p t k", k=2 * P), AX_X, ALU.max)
                last.then_inc(swa_mx.sem, 1)
                dve.wait_ge(*swa_mx.at(it, "M"))
                dve.tensor_scalar(smx[:, h % 2, :], smx[:, h % 2, :], SDH ** -0.5,
                                  vecs[:, bass.ds(m * SWH + V_SINK + h, 1)], ALU.mult, ALU.max).then_inc(swa_mx.sem, 1)
                dve.wait_ge(*swa_mx.at(it, "S"))
                dve.tensor_scalar(snm[:, h % 2, :], smx[:, h % 2, :], -1.0, None, ALU.mult).then_inc(swa_mx.sem, 1)

            def normalised(dst, h, b, st):
                dve.tensor_tensor(dst[:, :, h * SDH:(h + 1) * SDH],
                                  bank[b][:, 0:TT * SDH].rearrange("p (t c) -> p t c", c=SDH),
                                  sinv[:, h % 2, :].rearrange("p (t c) -> p t c", c=1).to_broadcast([P, TT, SDH]),
                                  ALU.mult).then_inc(st.sem, 1)

            PIECES = ((0, 0, 512), (1, 512, 512), (2, 1024, 256))

            def stick_log_sums(m, h):
                it = m * BH + h
                banks = ((2, 3, 4), (1, 5, 0))[h % 2]
                dve.wait_ge(*sb_ln.at(it, "LN"))
                for b, c, n in PIECES:
                    last = dve.scalar_tensor_tensor(out=spl[:, h % 2, c:c + n], in0=bank[banks[b]][:, 0:n], scalar=0.0,
                                                    in1=lsg[:, h % 2, c:c + n], op0=ALU.max, op1=ALU.add)
                last.then_inc(sb_keep.sem, 1)
                dve.wait_ge(*sb_keep.at(it, "SP"))
                for b, c, n in PIECES:
                    last = dve.scalar_tensor_tensor(out=lsg[:, h % 2, c:c + n], in0=bank[banks[b]][:, 0:n], scalar=0.0,
                                                    in1=lsg[:, h % 2, c:c + n], op0=ALU.min, op1=ALU.subtract)
                last.then_inc(sb_keep.sem, 1)
                for c in STICK_AT:
                    last = dve.tensor_tensor(spl[:, h % 2, c:c + P], spl[:, h % 2, c:c + P],
                                             cst[:, C_KEEP:C_KEEP + P], ALU.mult)
                last.then_inc(sb_keep.sem, 1)

            def hybrid(m):
                q0 = SECOND + m * LAYER2
                n = FINAL + 1 + m
                norm_chain(n, 1)
                dve.wait_ge(panel_done, q0 + BT_TM + KD // 2)
                for t in range(TT):
                    dve.tensor_scalar(vtm[:, t, :], bank[4 + t][:, 0:TM_COLS], rstd_col[:, t:t + 1], None, ALU.mult)\
                       .then_inc(pj.sem, 1)
                dve.wait_ge(*chain.at(n, "RB"))
                for i, (dst, b) in enumerate(((cq[:, 0, :], 2), (cq[:, 1, :], 3), (ckv[:], 0))):
                    dve.wait_ge(panel_done, q0 + BT_CQ + i + 1)
                    scaled(dst, bank[b][:], pj)
                dve.wait_ge(*lat_act.at(m, "S1"))
                dve.tensor_tensor(qsq[:, 0, :], qsq[:, 0, :], qsq[:, 1, :], ALU.add).then_inc(lat.sem, 1)
                for i, (dst, b) in enumerate(((ak[:], 1), (aq[:, 0, :], 2), (aq[:, 1, :], 3))):
                    dve.wait_ge(panel_done, q0 + BT_AK + i + 1)
                    scaled(dst, bank[b][:], pj)
                dve.wait_ge(*lat_act.at(m, "DK"))
                dve.reciprocal(qin[:], qin[:]).then_inc(lat.sem, 1)
                dve.reciprocal(kin[:], kin[:]).then_inc(lat.sem, 1)
                for i, (src, g, inv, high, low) in enumerate((
                        (cq[:, 0, :], m * 2 + V_QN, qin, cqh[:, 0, :], cql[:, 0, :]),
                        (cq[:, 1, :], m * 2 + V_QN + 1, qin, cqh[:, 1, :], cql[:, 1, :]),
                        (ckv[:], m + V_KVN, kin, ckh[:], ckl[:]))):
                    dve.wait_ge(*lat.at(m, ("IK", "L0", "L1")[i]))
                    dve.scalar_tensor_tensor(out=cn[:], in0=src, scalar=vecs[:, bass.ds(g, 1)], in1=inv[:],
                                             op0=ALU.mult, op1=ALU.mult).then_inc(lat.sem, 1)
                    dve.wait_ge(*lat_act.at(m, ("H0", "H1", "HK")[i]))
                    dve.tensor_tensor(low, cn[:], high.bitcast(F32), ALU.subtract).then_inc(lat.sem, 1)
                for i, (dst, b) in enumerate(((dq, 0), (dq, 1), (dk, 2), (dk, 3))):
                    dve.wait_ge(panel_done, q0 + BT_DQ + i + 1)
                    if dst is dq:
                        dve.scalar_tensor_tensor(out=dq[:, i, :], in0=bank[b][:], scalar=BDH ** -0.5, in1=rstd[:],
                                                 op0=ALU.mult, op1=ALU.mult).then_inc(pj.sem, 1)
                    else:
                        scaled(dk[:, i - 2, :], bank[b][:], pj)
                R = slice(64, 112)
                dve.memset(msw[R, :], 0.0).then_inc(mla.sem, 1)
                for h in range(MH):
                    dve.wait_ge(*mla_act.at(m, f"W{h}"))
                    if h:
                        dve.wait_ge(*mla.at(m, f"R{h - 1}"))
                    dve.tensor_tensor(t1[R, :], bank[4 + h][R, :], cos2[R, :], ALU.mult).then_inc(mla.sem, 1)
                    dve.tensor_tensor(t2[R, :], msw[R, :], sin2[R, :], ALU.mult).then_inc(mla.sem, 1)
                    dve.wait_ge(*mla.at(m, f"S{h}"))
                    dve.tensor_tensor(mq[R, h, :], t1[R, :], t2[R, :], ALU.add).then_inc(mla.sem, 1)
                dve.wait_ge(panel_done, q0 + BT_UKV + 1)
                for i in range(2):
                    dve.tensor_copy(vm[:, 2 * i:2 * i + 2, :], bank[4 + i][:].rearrange("p (t c) -> p t c", t=2))\
                       .then_inc(kv.sem, 1)
                dve.tensor_tensor(krs[0:KR_W, :], bank[6][0:KR_W, :], rstd[0:KR_W, :], ALU.mult).then_inc(kv.sem, 1)
                dve.wait_ge(*kv_act.at(m, "Y1"))
                dve.wait_ge(*mla.at(m, f"R{MH - 1}"))
                dve.tensor_tensor(t1[R, :], kx[R, :], cos2[R, :], ALU.mult).then_inc(kv.sem, 1)
                dve.tensor_tensor(t2[R, :], msw[R, :], sin2[R, :], ALU.mult).then_inc(kv.sem, 1)
                dve.wait_ge(*kv.at(m, "KM"))
                dve.tensor_tensor(mk[R, 0, :], t1[R, :], t2[R, :], ALU.add).then_inc(kv.sem, 1)
                for i in range(2):
                    it = m * 2 + i
                    banks = (0, 1, 2) if i == 0 else (5, 6, 7)
                    at = q0 + BT_CONV + 3 * i
                    if i:
                        dve.wait_ge(*conv.at(it - 1, "Y"))
                    else:
                        dve.memset(cu[:, 0:CONV_K - 1], 0.0)
                    dve.wait_ge(panel_done, at + 1)
                    scaled(cgs[:], bank[banks[0]][:], conv)
                    dve.wait_ge(panel_done, at + 2)
                    scaled(cxs[:], bank[banks[1]][:], conv)
                    dve.wait_ge(*conv.at(it, "X"))
                    dve.tensor_tensor(cu[:, CONV_K - 1:], cgs[:], cxs[:], ALU.mult).then_inc(conv.sem, 1)
                    dve.wait_ge(*conv.at(it, "U"))
                    w = m * 6 + V_CW + 3 * i
                    dve.tensor_scalar(cy[:], cu[:, 0:S], vecs[:, bass.ds(w, 1)], vecs[:, bass.ds(m * 2 + V_CB + i, 1)],
                                      ALU.mult, ALU.add).then_inc(conv.sem, 1)
                    for j, name in ((1, "A"), (2, "B")):
                        dve.wait_ge(*conv.at(it, name))
                        dve.scalar_tensor_tensor(out=cy[:], in0=cu[:, j:j + S], scalar=vecs[:, bass.ds(w + j, 1)],
                                                 in1=cy[:], op0=ALU.mult, op1=ALU.add).then_inc(conv.sem, 1)
                    dve.wait_ge(panel_done, at + 3)
                    scaled(cgs[:], bank[banks[2]][:], conv)
                    dve.wait_ge(*conv.at(it, "G"))
                    dve.tensor_tensor(y_conv[:, i, :], cgs[:], cy[:], ALU.mult).then_inc(conv.sem, 1)
                mla_max(m, 0)
                for h in range(MH):
                    it = m * MH + h
                    if h < MH - 1:
                        mla_max(m, h + 1)
                    else:
                        swa_max(m, 0)
                    dve.wait_ge(*mla_pe.at(it, "T1"))
                    dve.tensor_copy(prt[:, 0:P], bank[7][:, 0:P])
                    dve.tensor_copy(prt[:, 3 * P:6 * P], bank[7][:, P:4 * P]).then_inc(mla_dve.sem, 1)
                    dve.reciprocal(sinv[:, h % 2, :], ssum[:, h % 2, :]).then_inc(mla_dve.sem, 1)
                    dve.wait_ge(*mla_dve.at(it, "R"))
                    dve.wait_ge(*mla_pe.at(it, "V"))
                    normalised(y_mla, h, 3 + 2 * (h % 2), mla_dve)
                for h in range(SWH):
                    it = m * SWH + h
                    if h < SWH - 1:
                        swa_max(m, h + 1)
                    dve.wait_ge(*swa_pe.at(it, "T1"))
                    dve.tensor_copy(prt[:, P:4 * P], bank[7][:, 0:3 * P]).then_inc(swa_dve.sem, 1)
                    dve.wait_ge(*swa_ex.at(it, "K"))
                    dve.tensor_tensor(ssum[:, h % 2, :], ssum[:, h % 2, :], esk[:, h % 2, :], ALU.add).then_inc(swa_dve.sem, 1)
                    dve.wait_ge(*swa_dve.at(it, "Q"))
                    dve.reciprocal(sinv[:, h % 2, :], ssum[:, h % 2, :]).then_inc(swa_dve.sem, 1)
                    dve.wait_ge(*swa_dve.at(it, "R"))
                    dve.wait_ge(*swa_pe.at(it, "V"))
                    normalised(y_swa, h, 3 + 2 * (h % 2), swa_dve)
                stick_log_sums(m, 0)
                for h in range(BH):
                    it = m * BH + h
                    banks = ((2, 3, 4), (1, 5, 0))[h % 2]
                    if h < BH - 1:
                        stick_log_sums(m, h + 1)
                    dve.wait_ge(*sb_pe.at(it, "A"))
                    for b, c, n_ in PIECES:
                        last = dve.tensor_tensor(lsg[:, h % 2, c:c + n_], lsg[:, h % 2, c:c + n_],
                                                 bank[banks[b]][:, 0:n_], ALU.add)
                    last.then_inc(sb_dve.sem, 1)
                dve.wait_ge(*gn_act.at(m, "Q1"))
                dve.tensor_tensor(bsq[:, 0, :], bsq[:, 0, :], bsq[:, 1, :], ALU.add).then_inc(gn.sem, 1)
                for i, y in enumerate((y_swa, y_mla, y_sb)):
                    dve.wait_ge(*gn_act.at(m, f"D{i}"))
                    dve.reciprocal(ginv[:, i, :], gstd[:, i, :]).then_inc(gn.sem, 1)
                    dve.wait_ge(*gn.at(m, f"I{i}"))
                    dve.tensor_tensor(y[:], y[:], ginv[:, i, :].rearrange("p (t c) -> p t c", c=1)
                                      .to_broadcast([P, TT, GROUP]), ALU.mult).then_inc(gn.sem, 1)

                def gained(i, d, src):
                    dve.tensor_scalar(yt[:, d, :], src, vecs[:, bass.ds(m * KD + V_GRP + d, 1)], None, ALU.mult)\
                       .then_inc(gn.sem, 1)

                for i, d in ((0, 0), (1, 4)):
                    dve.wait_ge(*gn_pe.at(m, f"T{i}"))
                    for c in range(2):
                        gained(i, d + c, bank[2 + 2 * i + c][:])
                dve.reciprocal(binv[:], bstd[:]).then_inc(gn.sem, 1)
                dve.wait_ge(*gn.at(m, "IB"))
                for c in range(2):
                    dve.scalar_tensor_tensor(out=yt[:, 2 + c, :], in0=y_conv[:, c, :],
                                             scalar=vecs[:, bass.ds(m * KD + V_GRP + 2 + c, 1)], in1=binv[:],
                                             op0=ALU.mult, op1=ALU.mult).then_inc(gn.sem, 1)
                dve.wait_ge(*gn_pe.at(m, "T2"))
                for c in range(2):
                    gained(2, 6 + c, bank[6 + c][:])
                dve.wait_ge(*gn.at(m, "D1"))
                for d in range(KD):
                    it = m * KD + d
                    dve.wait_ge(panel_done, q0 + BT_GATE + d + 1)
                    scaled(gt[:], bank[(d + 1) % 2][:], gate)
                    dve.wait_ge(*gate_act.at(it, "S"))
                    dve.tensor_tensor(yg[:], yt[:, d, :], gs[:], ALU.mult).then_inc(gate.sem, 1)
                    dve.wait_ge(*gate_act.at(it, "H"))
                    dve.tensor_tensor(ygl[:, d, :], yg[:], ygh[:, d, :].bitcast(F32), ALU.subtract)\
                       .then_inc(gate.sem, 1)
                for d in range(KD):
                    dve.wait_ge(*z_act.at(m * KD + d, "Q"))
                    if d == 0:
                        dve.tensor_copy(ssq[:], sq[:]).then_inc(z_sum.sem, 1)
                    else:
                        dve.wait_ge(*z_sum.at(m * KD + d - 1, "A"))
                        dve.tensor_tensor(ssq[:], ssq[:], sq[:], ALU.add).then_inc(z_sum.sem, 1)
                dve.wait_ge(*post_sd.at(m, "SD"))
                dve.reciprocal(rstd_col[:], std_col[:]).then_inc(post.sem, 1)
                dve.wait_ge(*post.at(m, "RC"))
                for t in range(TT):
                    last = dve.tensor_scalar(diag[:, t * P:(t + 1) * P], ident, rstd_col[:, t:t + 1], None, ALU.mult)
                last.then_inc(post.sem, 1)
                dve.wait_ge(*post_pe.at(m, "BC"))
                dve.tensor_copy(rstd[:], bank[5][:]).then_inc(post.sem, 1)
                dve.wait_ge(*post.at(m, "RB"))
                for d in range(KD):
                    dve.scalar_tensor_tensor(out=z[:, d, :], in0=z[:, d, :],
                                             scalar=vecs[:, bass.ds(m * KD + V_POST + d, 1)], in1=rstd[:],
                                             op0=ALU.mult, op1=ALU.mult).then_inc(post.sem, 1)
                    dve.wait_ge(*post.at(m, f"Z{d}"))
                    dve.tensor_tensor(x[:, d, :], x[:, d, :], z[:, d, :], ALU.add).then_inc(prep.sem, 1)
                    prepare(n + 1, d, n + 1)
                    add_squares(n + 1, d, d == 0)

            dve.memset(eps[:], EPS).then_inc(memsets, 1)
            for i, st in enumerate((rg, ret, fox)):
                dve.memset(start_d[:, i:i + 1], 0.0).then_inc(st.sem, 1)
            dve.wait_ge(loaded, 64)
            for d in range(KD):
                dve.tensor_copy(x[:, d, :], x0[:, d, :]).then_inc(prep.sem, 1)
                prepare(0, d, 0)
                add_squares(0, d, d == 0)
            angles()
            with dve.Fori(0, DEPTH) as l:
                p0 = l * LAYER1
                ffn_in(l * 2, l * 3, p0)
                n = l * 3 + 1
                ffn_out(l * 2, n, p0 + FFN_IN)
                dve.wait_ge(tab_in, l * 48 + 48)
                FW = UNITS * FH
                dve.memset(ffh[:, FW:].bitcast(F32), 0.0)
                dve.memset(ffl[:, FW:].bitcast(F32), 0.0)
                dve.tensor_copy(ffh[:, 0:FW], ffraw[:, l, :]).then_inc(ffs.sem, 1)
                dve.wait_ge(*ffs.at(l, "H"))
                dve.tensor_tensor(ffl[:, 0:FW], ffraw[:, l, :], ffh[:, 0:FW].bitcast(F32), ALU.subtract)\
                   .then_inc(ffs.sem, 1)
                norm_chain(n, 1)
                for dst, at, banks in ((v_ret, AT_RV, (4, 5, 6, 7)), (v_fox, AT_FV, (0, 1, 2, 3))):
                    dve.wait_ge(panel_done, p0 + at + KD // 2)
                    for t in range(TT):
                        dve.tensor_scalar(dst[:, t, :], bank[banks[t]][:], rstd_col[:, t:t + 1], None, ALU.mult)\
                           .then_inc(tm.sem, 1)
                dve.wait_ge(*ffs_pe.at(l, "FF"))
                dve.wait_ge(*chain.at(n, "RB"))
                dve.tensor_tensor(fz[0:FH], bank[4][0:FH, :], rstd[0:FH, :], ALU.mult).then_inc(ffs.sem, 1)
                dve.wait_ge(*ffs.at(l, "Z"))
                dve.tensor_scalar(fz[0:FH], fz[0:FH], vecs[0:FH, bass.ds(l + V_BF, 1)], None, ALU.add)\
                   .then_inc(ffs.sem, 1)
                dve.wait_ge(*ffs_act.at(l, "LN"))
                dve.scalar_tensor_tensor(out=fz[0:FH], in0=fz[0:FH], scalar=0.0, in1=fa[0:FH],
                                         op0=ALU.min, op1=ALU.subtract).then_inc(ffs.sem, 1)
                dve.wait_ge(*ffs.at(l, "LF"))
                dve.tensor_tensor_scan(cum[0:FH, :], cst[0:FH, C_ONE:C_ONE + 1].to_broadcast([FH, S]), fz[0:FH], 0.0, ALU.mult, ALU.add)\
                   .then_inc(ffs.sem, 1)
                with dve.Fori(0, RH // 2) as i:
                    for q in range(2):
                        dve.wait_ge(panel_done, p0 + AT_RG + i * 2 + q + 1)
                        dve.wait_ge(*rg_act.before(l * RH + i * 2 + q))
                        scaled(tg[:], bank[q][:], rg)
                retention(l, p0 + AT_RET)
                forgetting(l, p0 + AT_FOX)
                merge(l, p0 + AT_MERGE)
                n2 = l * 3 + 2
                for d in range(KD):
                    dve.wait_ge(panel_done, p0 + AT_WOUT + d + 1)
                    dve.tensor_tensor(x[:, d, :], bank[6 + d % 2][:], x[:, d, :], ALU.add).then_inc(prep.sem, 1)
                    prepare(n2, d, n2)
                    add_squares(n2, d, d == 0)
                ffn_in(l * 2 + 1, n2, p0 + AT_FFN2)
                ffn_out(l * 2 + 1, l * 3 + 3, p0 + AT_FFN2 + FFN_IN)
            norm_chain(FINAL, 5)
            dve.wait_ge(*chain.at(FINAL, "RB"))
            for d in range(KD):
                dve.scalar_tensor_tensor(out=x[:, d, :], in0=x[:, d, :],
                                         scalar=vecs[:, FINAL * KD + d:FINAL * KD + d + 1],
                                         in1=rstd[:], op0=ALU.mult, op1=ALU.mult).then_inc(prep.sem, 1)
                prepare(FINAL + 1, d, FINAL + 1)
                add_squares(FINAL + 1, d, d == 0)
            with dve.Fori(0, DEPTH) as m:
                hybrid(m)


def table_of_constants():
    c = np.zeros((P, N_CONST), np.float32)
    i, j = np.arange(P)[:, None], np.arange(P)[None, :]
    c[:, C_ID:C_ID + P] = i == j
    c[:, C_ONE:C_ONE + P] = 1
    c[:, C_NONE:C_NONE + P] = -1
    c[:, C_NTRI:C_NTRI + P] = -1.0 * (i > j)
    c[:, C_CAUSAL:C_CAUSAL + P] = np.where(j <= i, 0, NEG)
    c[:, C_SWA:C_SWA + P] = np.where(j > i, 0, NEG)
    c[:, C_SWA + P:C_SWA + 2 * P] = np.where(j <= i, 0, NEG)
    c[:, C_SWA0:C_SWA0 + P] = NEG
    c[:, C_SWA0 + P:C_SWA0 + 2 * P] = np.where(j <= i, 0, NEG)
    c[:, C_STRICT:C_STRICT + P] = np.where(j > i, 0, NEG)
    c[:, C_KEEP:C_KEEP + P] = j > i
    half = M_ROPE // 2
    freqs = np.float32(10000.0) ** (-np.arange(half, dtype=np.float32) / np.float32(half))
    c[64:64 + half, C_FREQ] = freqs
    c[96:96 + half, C_FREQ] = freqs
    c[0:FH, C_HOT:C_HOT + FH] = np.eye(FH)
    c[0:FH, C_M8:C_M8 + P] = -FDH ** 0.5
    return c


def decay_table():
    gamma = 1 - 2.0 ** (-5 - np.arange(RH))
    gap = np.arange(S)[None, :] - np.arange(P)[:, None]
    t = np.where(gap[:, None, :] >= 0, gamma[None, :, None] ** np.maximum(gap, 0)[:, None, :], 0) * RDK ** -0.5
    return t.astype(np.float32)


def rope_table():
    half = RDK // 2
    inv = np.float32(10000.0) ** (-np.arange(0, RDK, 2, dtype=np.float32) / np.float32(RDK))
    ang = (np.arange(S, dtype=np.float32)[None, :] * inv[:, None]).astype(np.float64)
    t = np.zeros((P, 2, S))
    t[0:half, 0] = t[half:, 0] = np.cos(ang)
    t[0:half, 1], t[half:, 1] = -np.sin(ang), np.sin(ang)
    return t.astype(np.float32)


def col_panels(w):
    k, n = w.shape
    return w.reshape(KD, P, n // P, P).transpose(2, 1, 0, 3).reshape(n // P, P, PANEL)


def tok_panels(w):
    return w.reshape(KD // 2, 2, P, S).transpose(0, 2, 1, 3).reshape(KD // 2, P, PANEL)


def ffn_panels(w_in, w_out):
    a, b = col_panels(w_in[:, :F]), col_panels(w_in[:, F:])
    both = np.stack([a, b], 1).reshape(2 * KF, P, PANEL)
    whole = w_out[:KT_MAJOR * P].reshape(KT_MAJOR, P, PANEL)
    rest = w_out[KT_MAJOR * P:].reshape(KF - KT_MAJOR, P, KD, P).transpose(2, 0, 1, 3)
    rest = rest.reshape(-1, UNITS, P, P).transpose(0, 2, 1, 3).reshape(-1, P, PANEL)
    return [both, whole, rest]


def first_layer(a, l):
    w = a["w_in"][l]
    rq, rk, rv, rgw, fq, fk, fv = (w[:, i * 512:(i + 1) * 512] for i in range(7))
    gr, gf = w[:, 3592:4616], w[:, 4616:5640]
    crq, crk, cgr, cfq, cfk = map(col_panels, (rq, rk, gr, fq, fk))
    ret = np.stack([crq, crk, cgr[0::2], cgr[1::2]], 1).reshape(-1, P, PANEL)
    fox = np.stack([cfq, cfk], 1).reshape(-1, P, PANEL)
    wo = np.concatenate([a["w_o_ret"][l].reshape(RH, P, KD, P), a["w_o_fox"][l].reshape(FH // 2, P, KD, P)])
    wo = wo.transpose(2, 1, 0, 3).reshape(KD, P, PANEL)
    mrg = np.stack([col_panels(gf), wo], 1).reshape(-1, P, PANEL)
    return [*ffn_panels(a["w_ffn1_in"][l], a["w_ffn1_out"][l]), tok_panels(rv), tok_panels(fv), col_panels(rgw),
            ret, fox, mrg, col_panels(a["w_out"][l]), *ffn_panels(a["w_ffn2_in"][l], a["w_ffn2_out"][l])]


def second_layer(a, l):
    w = a["w_in_2"][l]
    cuts = np.cumsum((256, 128, 128, 256, 256, 256, 256, 128, 32, 256, 256, 256))
    a_q, a_k, a_v, b_b, b_c, b_x, c_q, c_kv, c_kr, d_q, d_k, d_v, gate_w = np.split(w, cuts, axis=1)
    tokens = np.concatenate([a_v, d_v, np.zeros((D, S - TM_COLS), np.float32)], 1)
    a_q = a_q.reshape(D, SWH, SDH)[:, [0, 2, 1, 3]].reshape(D, SWH * SDH)
    half = M_ROPE // 2

    def spread(rope):
        gap = np.zeros((*rope.shape[:-1], half), np.float32)
        return np.concatenate([rope[..., :half], gap, rope[..., half:]], -1)

    uq = a["mla_w_uq_2"][l].reshape(2, P, MH, M_NOPE + M_ROPE)
    uq = np.concatenate([uq[..., :M_NOPE], spread(uq[..., M_NOPE:]), np.zeros((2, P, MH, P - MLA_K), np.float32)], -1)
    uq = uq.transpose(1, 2, 0, 3).reshape(1, P, PANEL)
    ukv = a["mla_w_ukv_2"][l].reshape(KVR, MH, M_NOPE + M_V)
    k_rope = spread(c_kr).reshape(KD, P, KR_W).transpose(1, 0, 2).reshape(P, KD * KR_W)
    up = np.concatenate([ukv[..., :M_NOPE].reshape(P, -1), ukv[..., M_NOPE:].reshape(P, -1), k_rope,
                         np.zeros((P, PANEL - KR_AT - KD * KR_W), np.float32)], 1)[None]
    conv = np.stack([col_panels(b_c), col_panels(b_x), col_panels(b_b)], 1).reshape(-1, P, PANEL)
    return [tok_panels(tokens), col_panels(c_q), col_panels(c_kv), col_panels(a_k), col_panels(a_q), col_panels(d_q),
            col_panels(d_k), uq, up, conv, col_panels(gate_w), col_panels(a["w_out_2"][l])]


def columns(v):
    return v.reshape(-1, P).T


def kernel(**inputs):
    import concourse.bacc as bacc
    from concourse.bass_utils import run_bass_kernel_spmd

    a = {k: np.asarray(v) for k, v in inputs.items()}
    panels = [p for l in range(DEPTH) for p in first_layer(a, l)]
    panels += [p for l in range(DEPTH) for p in second_layer(a, l)]
    stream = np.concatenate(panels)
    assert len(stream) == N_PANELS
    vec = np.zeros((P, N_VEC), np.float32)
    norms = [a[k][l] for l in range(DEPTH) for k in ("norm_ffn1", "norm_mix", "norm_ffn2")]
    norms += [a["norm_final"], a["norm_pre_2"][0], a["norm_pre_2"][1]]
    for i, g in enumerate(norms):
        vec[:, i * KD:(i + 1) * KD] = columns(g)
    vec[:, V_RET:V_RET + DEPTH * RH] = columns(a["ret_norm"])
    vec[:, V_GRP:V_GRP + DEPTH * KD] = columns(a["group_norm_2"])
    vec[:, V_POST:V_POST + DEPTH * KD] = columns(a["norm_post_2"])
    vec[:, V_QN:V_QN + DEPTH * 2] = columns(a["mla_q_norm_2"])
    vec[:, V_KVN:V_KVN + DEPTH] = columns(a["mla_kv_norm_2"])
    vec[:, V_CW:V_CW + DEPTH * 6] = a["conv_w_2"].reshape(DEPTH, CONV_K, 2, P).transpose(3, 0, 2, 1).reshape(P, -1)
    vec[:, V_CB:V_CB + DEPTH * 2] = columns(a["conv_b_2"])
    vec[:, V_SINK:V_SINK + DEPTH * SWH] = a["attn_sinks_2"].reshape(1, -1)
    vec[0:FH, V_BF:V_BF + DEPTH] = a["b_forget"].T
    ff = a["w_in"][:, :, 3584:3592].reshape(DEPTH, KD, P, FH).transpose(2, 0, 1, 3).reshape(P, DEPTH, KD * FH)
    arrays = {
        "stream": stream,
        "x_t": np.ascontiguousarray(a["x"][0].T.reshape(KD, P, S).transpose(1, 0, 2)),
        "vec": vec, "const": table_of_constants(), "decay": decay_table(), "rope": rope_table(),
        "ff_w": np.ascontiguousarray(ff),
        "pos": np.ascontiguousarray(np.broadcast_to(a["positions_2"][0].astype(np.int32), (P, S))),
    }
    nc = bacc.Bacc("TRN2", target_bir_lowering=False, num_devices=1)
    args = [nc.dram_tensor(k, v.shape, mybir.dt.from_np(v.dtype), kind="ExternalInput").ap() for k, v in arrays.items()]
    out = nc.dram_tensor("out", [KD, P, S], F32, kind="ExternalOutput").ap()
    build(nc, *args, out)
    r = run_bass_kernel_spmd(nc, [arrays], core_ids=[0])
    return r.results[0]["out"].reshape(D, S).T[None].copy()
```

```python
from contextlib import ExitStack

import numpy as np
import concourse.bass as bass
import concourse.mybir as mybir

F32 = mybir.dt.float32
F32R = mybir.dt.float32r
I32 = mybir.dt.int32
BF16 = mybir.dt.bfloat16
ALU = mybir.AluOpType
ACT = mybir.ActivationFunctionType
AX_X = mybir.AxisListType.X

P = 128
D, S, DEPTH, F = 1024, 512, 2, 2816
KD = D // P
TT = S // P
KF = F // P
RH, RDK = 4, 128
FH, FDH = 8, 64
FF_W = FDH + FH
FF_COLS = KD * FF_W + P - FF_W
MH, M_NOPE, M_ROPE, M_V, QR, KVR = 4, 64, 32, 64, 256, 128
MLA_K = 112
SWH, SDH = 4, 64
BH, BDH = 4, 64
CONV_W, CONV_K = 256, 3
GROUP = 256
TM_COLS = SDH * 2 + BH * BDH
KR_AT = MH * (M_NOPE + M_V)
KR_W = 48
EPS = 1e-6
NEG = -1e31

UNITS = 8
PANEL = UNITS * P
RAW_SLOTS, SPLIT_SLOTS = 4, 2
KT_MAJOR = 16

FFN_IN = 2 * KF
FFN_PANELS = FFN_IN + KF
AT_RV = FFN_PANELS
AT_FV = AT_RV + KD // 2
AT_RG = AT_FV + KD // 2
AT_RET = AT_RG + RH
AT_FOX = AT_RET + 4 * RH
AT_MERGE = AT_FOX + FH
AT_WOUT = AT_MERGE + 2 * KD
AT_FFN2 = AT_WOUT + KD
LAYER1 = AT_FFN2 + FFN_PANELS
BT_TM = 0
BT_CQ = BT_TM + KD // 2
BT_CKV = BT_CQ + 2
BT_AK = BT_CKV + 1
BT_AQ = BT_AK + 1
BT_DQ = BT_AQ + 2
BT_DK = BT_DQ + 2
BT_UQ = BT_DK + 2
BT_UKV = BT_UQ + 1
BT_CONV = BT_UKV + 1
BT_GATE = BT_CONV + 6
BT_WOUT = BT_GATE + KD
LAYER2 = BT_WOUT + KD
SECOND = DEPTH * LAYER1
N_PANELS = SECOND + DEPTH * LAYER2
NORMS = 3 * DEPTH + 1 + DEPTH + 1
FINAL = 3 * DEPTH

V_RET = NORMS * KD
V_GRP = V_RET + DEPTH * RH
V_POST = V_GRP + DEPTH * KD
V_QN = V_POST + DEPTH * KD
V_KVN = V_QN + DEPTH * 2
V_CW = V_KVN + DEPTH
V_CB = V_CW + DEPTH * 6
V_BF = V_CB + DEPTH * 2
V_SINK = V_BF + DEPTH
N_VEC = V_SINK + DEPTH * SWH
C_ID, C_ONE, C_NONE, C_NTRI, C_CAUSAL, C_SWA, C_SWA0, C_STRICT, C_KEEP = (
    0, 128, 256, 384, 512, 640, 896, 1152, 1280)
C_FREQ, C_HOT = 1408, 1409
N_CONST = C_HOT + FH


class Steps:

    def __init__(self, sem, *names, started=0):
        self.sem, self.names, self.n, self.started = sem, names, len(names), started

    def at(self, round_, name):
        return self.sem, round_ * self.n + (self.names.index(name) + 1 + self.started)

    def before(self, round_):
        return self.sem, round_ * self.n + self.started


def build(nc, stream, x_in, vec, const, decay, rope, ff_w, pos, out):
    ctx = ExitStack()
    with ctx:
        def sb(name, shape, dt=F32, stack=ctx):
            return stack.enter_context(nc.sbuf_tensor(name, shape, dt))

        def sem(name):
            return ctx.enter_context(nc.semaphore(name))

        bank = [ctx.enter_context(nc.psum_tensor(f"bank{i}", [P, S], F32)) for i in range(8)]

        x = sb("x", [P, KD, S])
        xh = sb("xh", [P, KD, S], F32R)
        xl = sb("xl", [P, KD, S], F32R)
        sq = sb("sq", [P, S])
        ssq = sb("ssq", [P, S])
        diag = sb("diag", [P, S])
        rstd = sb("rstd", [P, S])
        std_col = sb("std_col", [P, TT])
        rstd_col = sb("rstd_col", [P, TT])
        raw = sb("raw", [P, RAW_SLOTS, PANEL])
        wh = sb("wh", [P, SPLIT_SLOTS, PANEL], F32R)
        wl = sb("wl", [P, SPLIT_SLOTS, PANEL], F32R)
        vecs = sb("vecs", [P, N_VEC])
        cst = sb("cst", [P, N_CONST])
        eps = sb("eps", [P, 1])
        one = sb("one", [P, 1])
        start_d = sb("start_d", [P, 1])
        start_a = sb("start_a", [P, 1])
        cos2 = sb("cos2", [P, S])
        sin2 = sb("sin2", [P, S])
        ident, ones = cst[:, C_ID:C_ID + P], cst[:, C_ONE:C_ONE + P]
        masks = sb("masks", [P, C_KEEP - C_CAUSAL], BF16)
        ident16 = sb("ident16", [P, P], BF16)
        causal = masks[:, 0:P]

        ffn = ExitStack()
        uh = sb("uh", [P, KF, S], F32R, ffn)
        ul = sb("ul", [P, KF, S], F32R, ffn)
        ta = sb("ta", [P, S], F32, ffn)
        tb = sb("tb", [P, S], F32, ffn)
        sa = sb("sa", [P, S], F32, ffn)
        u32 = sb("u32", [P, S], F32, ffn)
        ffn.close()
        init = ExitStack()
        x0 = sb("x0", [P, KD, S], F32, init)
        posi = sb("posi", [P, S], I32, init)
        ang = sb("ang", [P, S], F32, init)
        turn = sb("turn", [P, S], F32, init)
        init.close()
        mix = ExitStack()
        yrh = sb("yrh", [P, RH, S], F32R, mix)
        yrl = sb("yrl", [P, RH, S], F32R, mix)
        yfh = sb("yfh", [P, FH // 2, S], F32R, mix)
        yfl = sb("yfl", [P, FH // 2, S], F32R, mix)
        gate_r = sb("gate_r", [P, KD, S], F32, mix)
        heads = ExitStack()
        dec = sb("dec", [P, RH, S], F32, heads)
        rp = sb("rp", [P, 2, S], F32, heads)
        v_fox = sb("v_fox", [P, TT, S], F32, heads)
        cum = sb("cum", [P, S], F32, heads)
        fq = sb("fq", [P, 2, S], F32, heads)
        fk = sb("fk", [P, 2, S], F32, heads)
        ff_mem = ExitStack()
        ffraw = sb("ffraw", [P, FF_COLS], F32, ff_mem)
        ffh = sb("ffh", [P, FF_COLS], F32R, ff_mem)
        ffl = sb("ffl", [P, FF_COLS], F32R, ff_mem)
        ff_mem.close()
        ret_mem = ExitStack()
        pt = sb("pt", [P, 10 * P], F32, ret_mem)
        kr = sb("kr", [P, S], F32, ret_mem)
        qr = sb("qr", [P, S], F32, ret_mem)
        tq = sb("tq", [P, S], F32, ret_mem)
        tk = sb("tk", [P, S], F32, ret_mem)
        hsum = sb("hsum", [P, TT], F32, ret_mem)
        hstd = sb("hstd", [P, TT], F32, ret_mem)
        hinv = sb("hinv", [P, TT], F32, ret_mem)
        v_ret = sb("v_ret", [P, TT, S], F32, ret_mem)
        rgs = sb("rgs", [P, RH, S], F32, ret_mem)
        ret_mem.close()
        tg = yn = tk
        y32 = tq
        m1, sw = diag, ssq
        fox_mem = ExitStack()
        fp = sb("fp", [P, 2, 10 * P], F32, fox_mem)
        fpt = sb("fpt", [P, 10 * P], F32, fox_mem)
        fo = sb("fo", [P, TT, P], F32, fox_mem)
        fmx = sb("fmx", [P, 2, TT], F32, fox_mem)
        fnm = sb("fnm", [P, 2, TT], F32, fox_mem)
        fsum = sb("fsum", [P, 2, TT], F32, fox_mem)
        finv = sb("finv", [P, 2, TT], F32, fox_mem)
        fox_mem.close()
        fz, fa = fq[:, 0, :], fq[:, 1, :]
        heads.close()
        merge_mem = ExitStack()
        mh = sb("mh", [P, KD, S], F32R, merge_mem)
        ml = sb("ml", [P, KD, S], F32R, merge_mem)
        sr = sb("sr", [P, S], F32, merge_mem)
        sf = sb("sf", [P, S], F32, merge_mem)
        tgf = sb("tgf", [P, S], F32, merge_mem)
        mr = sb("mr", [P, S], F32, merge_mem)
        mf = sb("mf", [P, S], F32, merge_mem)
        mg = sb("mg", [P, S], F32, merge_mem)
        merge_mem.close()
        mix.close()
        hyb = ExitStack()
        y_swa = sb("y_swa", [P, TT, GROUP], F32, hyb)
        y_mla = sb("y_mla", [P, TT, GROUP], F32, hyb)
        y_sb = sb("y_sb", [P, TT, GROUP], F32, hyb)
        y_conv = sb("y_conv", [P, 2, S], F32, hyb)
        qkv_mem = ExitStack()
        vtm = sb("vtm", [P, TT, TM_COLS], F32, qkv_mem)
        cqh = sb("cqh", [P, 2, S], F32R, qkv_mem)
        cql = sb("cql", [P, 2, S], F32R, qkv_mem)
        ckh = sb("ckh", [P, S], F32R, qkv_mem)
        ckl = sb("ckl", [P, S], F32R, qkv_mem)
        aq = sb("aq", [P, 2, S], F32, qkv_mem)
        ak = sb("ak", [P, S], F32, qkv_mem)
        dq = sb("dq", [P, 2, S], F32, qkv_mem)
        dk = sb("dk", [P, 2, S], F32, qkv_mem)
        mq = sb("mq", [P, MH, S], F32, qkv_mem)
        mk = sb("mk", [P, MH, S], F32, qkv_mem)
        vm = sb("vm", [P, TT, MH * M_V], F32, qkv_mem)
        lat_mem = ExitStack()
        cq = sb("cq", [P, 2, S], F32, lat_mem)
        ckv = sb("ckv", [P, S], F32, lat_mem)
        qsq = sb("qsq", [P, 2, S], F32, lat_mem)
        ksq = sb("ksq", [P, S], F32, lat_mem)
        qin = sb("qin", [P, S], F32, lat_mem)
        kin = sb("kin", [P, S], F32, lat_mem)
        cn = sb("cn", [P, S], F32, lat_mem)
        t1 = sb("t1", [P, S], F32, lat_mem)
        t2 = sb("t2", [P, S], F32, lat_mem)
        msw = sb("msw", [P, S], F32, lat_mem)
        krs = sb("krs", [P, S], F32, lat_mem)
        kx = sb("kx", [P, S], F32, lat_mem)
        cgs = sb("cgs", [P, S], F32, lat_mem)
        cxs = sb("cxs", [P, S], F32, lat_mem)
        cu = sb("cu", [P, CONV_K - 1 + S], F32, lat_mem)
        cy = sb("cy", [P, S], F32, lat_mem)
        lat_mem.close()
        att_mem = ExitStack()
        pr = sb("pr", [P, 2, 10 * P], F32, att_mem)
        prt = sb("prt", [P, 10 * P], F32, att_mem)
        smx = sb("smx", [P, 2, TT], F32, att_mem)
        snm = sb("snm", [P, 2, TT], F32, att_mem)
        ssum = sb("ssum", [P, 2, TT], F32, att_mem)
        sinv = sb("sinv", [P, 2, TT], F32, att_mem)
        esk = sb("esk", [P, 2, TT], F32, att_mem)
        lsg = sb("lsg", [P, 2, 10 * P], F32, att_mem)
        spl = sb("spl", [P, 2, 10 * P], F32, att_mem)
        att_mem.close()
        grp_mem = ExitStack()
        yt = sb("yt", [P, KD, S], F32, grp_mem)
        bsq = sb("bsq", [P, 2, S], F32, grp_mem)
        bstd = sb("bstd", [P, S], F32, grp_mem)
        binv = sb("binv", [P, S], F32, grp_mem)
        gt = sb("gt", [P, S], F32, grp_mem)
        gs = sb("gs", [P, S], F32, grp_mem)
        yg = sb("yg", [P, S], F32, grp_mem)
        gsq = sb("gsq", [P, TT, GROUP], F32, grp_mem)
        gsum = sb("gsum", [P, 3, TT], F32, grp_mem)
        gstd = sb("gstd", [P, 3, TT], F32, grp_mem)
        ginv = sb("ginv", [P, 3, TT], F32, grp_mem)
        grp_mem.close()
        qkv_mem.close()
        out_mem = ExitStack()
        ygh = sb("ygh", [P, KD, S], F32R, out_mem)
        ygl = sb("ygl", [P, KD, S], F32R, out_mem)
        z = sb("z", [P, KD, S], F32, out_mem)
        out_mem.close()
        hyb.close()

        raw_in = [sem(f"raw_in{i}") for i in range(RAW_SLOTS)]
        split_hi, split_lo = sem("split_hi"), sem("split_lo")
        panel_done = sem("panel_done")
        loaded = sem("loaded")
        tab_in = sem("tab_in")
        tab_free = sem("tab_free")
        memsets = sem("memsets")
        one_set = sem("one_set")
        mask_set = sem("mask_set")
        stored = sem("stored")
        prep = Steps(sem("prep_dve"), "X", "XH", "XL", "ACC")
        prep_sq = Steps(sem("prep_act"), "SQ")
        chain_pe = Steps(sem("chain_pe"), "COL", "BC")
        chain_sd = Steps(sem("chain_act"), "SD")
        chain = Steps(sem("chain_dve"), "RC", "DG", "RB")
        fin = Steps(sem("ffn_in_dve"), "A", "B", "U", "UL")
        fin_act = Steps(sem("ffn_in_act"), "SILU", "UH")
        fout = Steps(sem("ffn_out_pe"), *range(KD))
        tm = Steps(sem("tm_dve"), *[f"RV{i}" for i in range(TT)], *[f"FV{i}" for i in range(TT)])
        ffs = Steps(sem("forget_dve"), "H", "L", "Z", "ZB", "LF", "C")
        ffs_pe = Steps(sem("forget_pe"), "FF")
        ffs_act = Steps(sem("forget_act"), "ABS", "EXP", "LN")
        rg = Steps(sem("rg_dve"), "T", started=1)
        rg_act = Steps(sem("rg_act"), "S", started=1)
        ret_sc, ret_pv, ret_tr = (Steps(sem(f"ret_{k}_pe"), "P") for k in ("scores", "values", "turned"))
        ret = Steps(sem("ret_dve"), "Q", "QC", "QS", "QR", "K", "KC", "KS", "KR", "G0", "P0", "P1", "P2", "P3", "G1")
        ret_n = Steps(sem("ret_norm_dve"), "RC", "N0", "N1", "N2", "N3")
        ret_y = Steps(sem("ret_out_dve"), "Y", "YL")
        ret_sw = Steps(sem("ret_swap_act"), "Q0", "Q1", "K0", "K1")
        ret_sq = Steps(sem("ret_norm_act"), "S0", "S1", "S2", "S3", "SD")
        ret_h = Steps(sem("ret_out_act"), "YH")
        fx_set = sem("fox_set_dve")
        fx_s, fx_v = ([Steps(sem(f"fox_{k}_{e}_pe"), "P") for e in "ab"] for k in ("scores", "values"))
        fx_t = [Steps(sem(f"fox_turned_{e}_pe"), "T0", "T1", "T2") for e in "ab"]
        fx_y = Steps(sem("fox_out_pe"), "TR")
        fx_q = Steps(sem("fox_qk_dve"), "CA", "CB", "QA", "QB", "KA", "KB")
        fx_m = [Steps(sem(f"fox_max_{e}_dve"), "M", "N") for e in "ab"]
        fx_o = [Steps(sem(f"fox_values_{e}_dve"), "E", "R", "O") for e in "ab"]
        fx_l = Steps(sem("fox_out_dve"), "YL")
        fx_x = [Steps(sem(f"fox_exp_{e}_act"), "X") for e in "ab"]
        fx_c = [Steps(sem(f"fox_turned_{e}_act"), "E0", "E2") for e in "ab"]
        fx_h = Steps(sem("fox_out_act"), "YH")
        mrg_d = Steps(sem("merge_dve"), "G", "R", "F", "M", "L")
        mrg_a = Steps(sem("merge_act"), "SR", "SF", "MH")

        trig = Steps(sem("trig_dve"), "F", "A", *[f"{w}{i}" for w in "sc" for i in range(6)], "NEG")
        trig_act = Steps(sem("trig_act"), "SIN", "COS")
        pj = Steps(sem("proj_dve"), "T0", "T1", "T2", "T3", "Q0", "Q1", "KV", "AK", "A0", "A1", "D0", "D1", "E0", "E1")
        lat_pe = Steps(sem("latent_pe"), "Q", "K")
        lat = Steps(sem("latent_dve"), "SUM", "IQ", "IK", "N0", "L0", "N1", "L1", "NK", "LK")
        lat_act = Steps(sem("latent_act"), "S0", "S1", "SK", "DQ", "DK", "H0", "H1", "HK")
        mla = Steps(sem("mla_q_dve"), "Z", *[f"{w}{h}" for h in range(MH) for w in "CSR"])
        mla_act = Steps(sem("mla_q_act"), *[f"{w}{h}" for h in range(MH) for w in "PVW"])
        kv = Steps(sem("mla_kv_dve"), "V0", "V1", "KS", "KC", "KM", "KR")
        kv_act = Steps(sem("mla_kv_act"), "N0", "N1", "N2", "N3", "X", "Y0", "Y1", "C1", "C2", "C3")
        conv = Steps(sem("conv_dve"), "C", "X", "U", "A", "B", "D", "G", "Y")
        mla_sc = Steps(sem("mla_scores_pe"), "SC")
        mla_mx = Steps(sem("mla_max_dve"), "M", "N")
        mla_ex = Steps(sem("mla_exp_act"), "X")
        mla_pe = Steps(sem("mla_values_pe"), "T0", "T1", "T2", "V")
        mla_dve = Steps(sem("mla_values_dve"), "E", "R", "O")
        mla_ev = Steps(sem("mla_values_act"), "E0", "E2")
        swa_sc = Steps(sem("swa_scores_pe"), "SC")
        swa_mx = Steps(sem("swa_max_dve"), "M", "S", "N")
        swa_ex = Steps(sem("swa_exp_act"), "X", "K")
        swa_pe = Steps(sem("swa_values_pe"), "T0", "T1", "V")
        swa_dve = Steps(sem("swa_values_dve"), "E", "Q", "R", "O")
        swa_ev = Steps(sem("swa_values_act"), "E0")
        sb_sc = Steps(sem("stick_scores_pe"), "Z")
        sb_ln = Steps(sem("stick_log_act"), "AB", "EX", "LN")
        sb_keep = Steps(sem("stick_log_dve"), "SP", "LS", "K")
        sb_pe = Steps(sem("stick_values_pe"), "A", "V")
        sb_dve = Steps(sem("stick_values_dve"), "T")
        sb_act = Steps(sem("stick_values_act"), "P", "O")
        gn_pe = Steps(sem("group_pe"), "B", "T0", "T1", "T2")
        gn = Steps(sem("group_dve"), "SUM", "I0", "N0", "I1", "N1", "I2", "N2", "A0", "A1", "C0", "C1", "IB", "B0", "B1",
                   "D0", "D1")
        gn_act = Steps(sem("group_act"), "Q0", "Q1", "S0", "S1", "S2", "DB", "D0", "D1", "D2")
        gate = Steps(sem("gate_dve"), "G", "Y", "L")
        gate_act = Steps(sem("gate_act"), "S", "H")
        z_act = Steps(sem("z_act"), "Z", "Q")
        z_sum = Steps(sem("z_dve"), "A")
        post_pe = Steps(sem("post_pe"), "COL", "BC")
        post_sd = Steps(sem("post_act"), "SD")
        post = Steps(sem("post_dve"), "RC", "DG", "RB", *[f"Z{d}" for d in range(KD)])

        SETS = (((2, 0), (3, 0), (2, 128), (4, 0)), ((1, 0), (5, 0), (1, 128), (0, 0)))
        HEAD_AT = SETS[0]
        FIRST_BLOCK = (0, 1, 3, 6)
        STICK_AT = (0, 512, 1024, 896)

        OFF = (0, 512, 896, 1152)

        block = ctx.enter_context(nc.Block())

        @block.sync
        def _(sp):
            loads = [(x0[:], x_in), (vecs[:], vec), (cst[:], const), (posi[:], pos)]
            for dst, src in loads:
                sp.dma_start(dst, src).then_inc(loaded, 16)
            for n in range(RAW_SLOTS):
                sp.dma_start(raw[:, n, :], stream[n]).then_inc(raw_in[n], 16)
            with sp.Fori(1, N_PANELS // RAW_SLOTS) as g:
                for n in range(RAW_SLOTS):
                    sp.wait_ge(split_lo, g * RAW_SLOTS + (n + 1 - RAW_SLOTS))
                    sp.dma_start(raw[:, n, :], stream[g * RAW_SLOTS + n]).then_inc(raw_in[n], 16)
            for d in range(KD):
                sp.wait_ge(*prep.at((NORMS - 1) * KD + d, "X"))
                sp.dma_start(out[d], x[:, d, :]).then_inc(stored, 16)
            sp.wait_ge(stored, 16 * KD)

        @block.gpsimd
        def _(pool):
            def split(n, g, first=False):
                slot = n % SPLIT_SLOTS
                pool.wait_ge(raw_in[n], 16 * (g + 1))
                if not (first and n < SPLIT_SLOTS):
                    pool.wait_ge(panel_done, g * RAW_SLOTS + (n + 1 - SPLIT_SLOTS))
                pool.tensor_tensor(wh[:, slot, :], raw[:, n, :], one[:].to_broadcast([P, PANEL]), ALU.mult).then_inc(split_hi, 1)
                pool.wait_ge(split_hi, g * RAW_SLOTS + (n + 1))
                pool.tensor_tensor(wl[:, slot, :], raw[:, n, :], wh[:, slot, :].bitcast(F32),
                                   ALU.subtract).then_inc(split_lo, 1)

            pool.memset(one[:], 1.0).then_inc(one_set, 1)
            pool.wait_ge(one_set, 1)
            for n in range(RAW_SLOTS):
                split(n, 0, True)
            with pool.Fori(1, N_PANELS // RAW_SLOTS) as g:
                for n in range(RAW_SLOTS):
                    split(n, g)

        @block.tensor
        def _(pe):
            def mm3(o, w, rhs_h, rhs_l, first, last):
                s, c = w
                pe.matmul(o, wh[:, s, c], rhs_h, start=first, stop=False)
                pe.matmul(o, wh[:, s, c], rhs_l, start=False, stop=False)
                return pe.matmul(o, wl[:, s, c], rhs_h, start=False, stop=last)

            def unit(u):
                return slice(u * P, (u + 1) * P)

            def panel_ready(idx):
                pe.wait_ge(split_lo, idx + 1)

            def x_ready(n, d):
                pe.wait_ge(*prep.at(n * KD + d, "XL"))

            def col_panel(o, slot, idx, norm=None):
                panel_ready(idx)
                for k in range(KD):
                    if norm is not None:
                        x_ready(norm, k)
                    last = mm3(o, (slot, unit(k)), xh[:, k, :], xl[:, k, :], k == 0, k == KD - 1)
                last.then_inc(panel_done, 1)

            def chain_col(n, b):
                pe.wait_ge(*prep.at(n * KD + KD - 1, "ACC"))
                for t in range(TT):
                    last = pe.matmul(bank[b][:, t:t + 1], ssq[:, t * P:(t + 1) * P], ones[:, 0:1],
                                     start=True, stop=True)
                last.then_inc(chain_pe.sem, 1)

            def chain_bc(n, b):
                pe.wait_ge(*chain.at(n, "DG"))
                pe.matmul(bank[b][:], ones, diag[:], start=True, stop=True).then_inc(chain_pe.sem, 1)

            def ffn_in(f, n, idx):
                def pair(j, at, it, first):
                    q = 2 * (j % 2)
                    if first:
                        pe.wait_ge(*prep.at(n * KD + 4 + q + 1, "X"))
                    else:
                        pe.wait_ge(*fin.at(it - 2, "B"))
                    col_panel(bank[q][:], 0, at, n if first and j == 0 else None)
                    if first and j == 0:
                        chain_col(n, 4)
                    col_panel(bank[q + 1][:], 1, at + 1)
                    if first and j == 0:
                        chain_bc(n, 5)

                for j in range(2):
                    pair(j, idx + 2 * j, None, True)
                with pe.Fori(1, KF // 2) as i:
                    for j in range(2):
                        pair(j, idx + i * 4 + 2 * j, f * KF + i * 2 + j, False)

            def ffn_out(f, idx):
                ob = [bank[i] for i in (4, 5, 6, 7, 0, 1, 2, 3)]

                def k_panel(slot, p_idx, it, kt, first):
                    panel_ready(p_idx)
                    pe.wait_ge(*fin.at(it, "UL"))
                    for d in range(KD):
                        if first and d == 4:
                            pe.wait_ge(*fin.at(f * KF + KF - 1, "B"))
                        last = mm3(ob[d][:], (slot, unit(d)), uh[:, kt, :], ul[:, kt, :], first, False)
                    last.then_inc(panel_done, 1)

                for kt in range(2):
                    k_panel(kt % 2, idx + kt, f * KF + kt, kt, kt == 0)
                with pe.Fori(1, KT_MAJOR // 2) as i:
                    for q in range(2):
                        k_panel(q, idx + i * 2 + q, f * KF + i * 2 + q, i * 2 + q, False)
                rest = KF - KT_MAJOR
                pe.wait_ge(*fin.at(f * KF + KF - 1, "UL"))
                for u in range(KD * rest):
                    p, d, kt = u // UNITS, u // rest, KT_MAJOR + u % rest
                    if u % UNITS == 0:
                        panel_ready(idx + KT_MAJOR + p)
                    last = mm3(ob[d][:], (p % 2, unit(u % UNITS)), uh[:, kt, :], ul[:, kt, :], False, kt == KF - 1)
                    if u % UNITS == UNITS - 1:
                        last.then_inc(panel_done, 1)
                    elif kt == KF - 1:
                        last.then_inc(fout.sem, 1)

            def token_major(idx, banks, cols, norm=None):
                for p in range(KD // 2):
                    panel_ready(idx + p)
                    for kk in range(2):
                        k = 2 * p + kk
                        if norm is not None:
                            x_ready(norm, k)
                        for t in range(TT):
                            o = bank[banks[t]][:, 0:cols]
                            w = slice(kk * S, kk * S + cols)
                            tok = slice(t * P, (t + 1) * P)
                            pe.matmul(o, xh[:, k, tok], wh[:, p % 2, w], start=k == 0, stop=False)
                            pe.matmul(o, xl[:, k, tok], wh[:, p % 2, w], start=False, stop=False)
                            last = pe.matmul(o, xh[:, k, tok], wl[:, p % 2, w], start=False, stop=k == KD - 1)
                    last.then_inc(panel_done, 1)
                    if norm is not None and p == 0:
                        chain_col(norm, 0)
                    if norm is not None and p == 2:
                        chain_bc(norm, 1)

            def ret_turn(it):
                pe.wait_ge(*ret_n.at(it, "N3"))
                for t in range(TT):
                    last = pe.transpose(bank[5][:, t * P:(t + 1) * P], yn[:, t * P:(t + 1) * P], ident)
                last.then_inc(ret_tr.sem, 1)

            def retention(l, idx):
                def head(h, first):
                    it = l * RH + h
                    at = idx + h * 4
                    if first:
                        pe.wait_ge(*rg.at(l * RH + RH - 1, "T"))
                    col_panel(bank[0][:], 0, at)
                    if not first:
                        ret_turn(it - 1)
                    col_panel(bank[1][:], 1, at + 1)
                    col_panel(bank[2][:], 0, at + 2)
                    pe.wait_ge(*ret.at(it, "KR"))
                    if not first:
                        pe.wait_ge(*ret_y.at(it - 1, "Y"))
                    for i in range(TT):
                        last = pe.matmul(bank[4 + i][:, 0:S - i * P], kr[:, i * P:(i + 1) * P], qr[:, i * P:S],
                                         start=True, stop=True)
                    last.then_inc(ret_sc.sem, 1)
                    if not first:
                        pe.wait_ge(*ret.at(it - 1, "G1"))
                    col_panel(bank[3][:], 1, at + 3)
                    pe.wait_ge(*ret.at(it, "P3"))
                    for t in range(TT):
                        for i in range(t + 1):
                            last = pe.matmul(bank[4][:, t * P:(t + 1) * P],
                                             pt[:, OFF[i] + (t - i) * P:OFF[i] + (t - i + 1) * P],
                                             v_ret[:, i, bass.ds(h * RDK, RDK)], start=i == 0, stop=i == t)
                    last.then_inc(ret_pv.sem, 1)

                head(0, True)
                with pe.Fori(1, RH) as h:
                    head(h, False)

            def fox_scores(it, e):
                for qt in range(TT):
                    b, c = HEAD_AT[qt]
                    n = (qt + 1) * P
                    pe.matmul(bank[b][:, c:c + n], fq[:, e, qt * P:n], fk[:, e, 0:n], start=True, stop=False)
                    last = pe.matmul(bank[b][:, c + n - P:c + n], ident16[:], causal, start=False, stop=True)
                last.then_inc(fx_s[e].sem, 1)

            def fox_values(it, e, v):
                pe.wait_ge(*fx_c[e].at(it, "E2"))
                pe.wait_ge(*fx_o[e].at(it, "E"))
                for qt in range(TT):
                    for j in range(qt + 1):
                        blk = FIRST_BLOCK[qt] + j
                        last = pe.matmul(bank[5][:, 2 * P + qt * FDH:2 * P + (qt + 1) * FDH],
                                         fpt[:, blk * P:(blk + 1) * P], v_fox[:, j, v(e)], start=j == 0, stop=j == qt)
                last.then_inc(fx_v[e].sem, 1)

            def fox_turn(it, b):
                pe.wait_ge(*fx_o[1].at(it, "O"))
                for t in range(TT):
                    last = pe.transpose(bank[b][:, t * P:(t + 1) * P], fo[:, t, :], ident)
                last.then_inc(fx_y.sem, 1)

            def forgetting(l, idx):
                pairs = FH // 2

                def pair(t2, first, last_pair):
                    it = l * pairs + t2

                    def v(e):
                        return bass.ds(t2 * P + e * FDH, FDH)

                    col_panel(bank[0][:], 0, idx + t2 * 2 + 2)
                    if not first:
                        fox_turn(it - 1, 1)
                    pe.wait_ge(*fx_x[0].at(it, "X"))
                    transposes(fp[:, 0, :], fx_t[0].sem)
                    fox_scores(it, 1)
                    fox_values(it, 0, v)
                    if not first:
                        pe.wait_ge(*fx_l.at(it - 1, "YL"))
                    col_panel(bank[1][:], 1, idx + t2 * 2 + 3)
                    pe.wait_ge(*fx_x[1].at(it, "X"))
                    pe.wait_ge(*fx_o[0].at(it, "O"))
                    transposes(fp[:, 1, :], fx_t[1].sem)
                    if not last_pair:
                        pe.wait_ge(*fx_q.at(it + 1, "KB"))
                        fox_scores(it + 1, 0)
                    fox_values(it, 1, v)

                pe.wait_ge(*ret.at(l * RH + RH - 1, "G1"))
                col_panel(bank[0][:], 0, idx)
                ret_turn(l * RH + RH - 1)
                col_panel(bank[1][:], 1, idx + 1)
                pe.wait_ge(*ret_y.at(l * RH + RH - 1, "Y"))
                pe.wait_ge(*fx_q.at(l * pairs, "KB"))
                fox_scores(l * pairs, 0)
                pair(0, True, False)
                with pe.Fori(1, pairs - 1) as t2:
                    pair(t2, False, False)
                pair(pairs - 1, False, True)

            def transposes(p_, sem_):
                for b, blocks in ((6, (6, 7, 8, 9)), (7, (0, 3, 4, 5)), (5, (1, 2))):
                    for j, blk in enumerate(blocks):
                        last = pe.transpose(bank[b][:, j * P:(j + 1) * P], p_[:, blk * P:(blk + 1) * P], ident)
                    last.then_inc(sem_, 1)

            def merge(l, idx):
                banks = ((0, 3, 4), (1, 6, 7))

                def branch(o, slot, n, u0, yh, yl, before_last=None):
                    for k in range(n):
                        if before_last and k == n - 1:
                            before_last()
                        last = mm3(o[:], (slot, unit(u0 + k)), yh[:, k, :], yl[:, k, :], k == 0, k == n - 1)
                    return last

                def tile(d, q, it):
                    g, r, f = (bank[b] for b in banks[q])
                    pe.wait_ge(*mrg_d.at(it - 2, "F"))
                    col_panel(g[:], 0, idx + d * 2)
                    panel_ready(idx + d * 2 + 1)
                    branch(r, 1, RH, 0, yrh, yrl)
                    branch(f, 1, FH // 2, RH, yfh, yfl).then_inc(panel_done, 1)

                end = l * (FH // 2) + FH // 2 - 1
                for q in range(2):
                    _, r, f = (bank[b] for b in banks[q])
                    panel_ready(idx + 2 + q)
                    branch(r, q, RH, 0, yrh, yrl)
                    if q == 0:
                        fox_turn(end, 2)
                    branch(f, q, FH // 2, RH, yfh, yfl, None if q else lambda: pe.wait_ge(*fx_l.at(end, "YL")))\
                        .then_inc(panel_done, 1)
                with pe.Fori(1, KD // 2) as i:
                    for q in range(2):
                        tile(i * 2 + q, q, l * KD + i * 2 + q)

            def mix_out(l, n, idx):
                for d in range(KD):
                    if d >= 2:
                        pe.wait_ge(*prep.at(n * KD + d - 2, "X"))
                    panel_ready(idx + d)
                    for k in range(KD):
                        if d == 0:
                            pe.wait_ge(*mrg_d.at(l * KD + k, "L"))
                        last = mm3(bank[2 + 3 * (d % 2)][:], (d % 2, unit(k)), mh[:, k, :], ml[:, k, :],
                                   k == 0, k == KD - 1)
                    last.then_inc(panel_done, 1)

            def mla_scores(m, h):
                for qt in range(TT):
                    b, c = SETS[h % 2][qt]
                    n = (qt + 1) * P
                    pe.matmul(bank[b][:, c:c + n], mq[0:MLA_K, h, qt * P:n], mk[0:MLA_K, h, 0:n],
                              start=True, stop=False)
                    last = pe.matmul(bank[b][:, c + n - P:c + n], ident16[:], causal, start=False, stop=True)
                last.then_inc(mla_sc.sem, 1)

            def mla_transposes(p_, sem_, wait_bank6):
                for j, blk in enumerate((6, 7, 8, 9)):
                    last = pe.transpose(bank[6][:, j * P:(j + 1) * P], p_[:, blk * P:(blk + 1) * P], ident)
                last.then_inc(sem_, 1)
                for j, blk in enumerate((0, 3, 4, 5)):
                    last = pe.transpose(bank[7][:, j * P:(j + 1) * P], p_[:, blk * P:(blk + 1) * P], ident)
                last.then_inc(sem_, 1)
                wait_bank6()
                for j, blk in enumerate((1, 2)):
                    last = pe.transpose(bank[6][:, j * P:(j + 1) * P], p_[:, blk * P:(blk + 1) * P], ident)
                last.then_inc(sem_, 1)

            def mla_values(m, h):
                it = m * MH + h
                pe.wait_ge(*mla_ex.at(it, "X"))
                mla_transposes(pr[:, h % 2, :], mla_pe.sem, lambda: pe.wait_ge(*mla_ev.at(it, "E0")))
                pe.wait_ge(*mla_ev.at(it, "E2"))
                pe.wait_ge(*mla_dve.at(it, "E"))
                for qt in range(TT):
                    for j in range(qt + 1):
                        blk = FIRST_BLOCK[qt] + j
                        last = pe.matmul(bank[3 + 2 * (h % 2)][:, qt * M_V:(qt + 1) * M_V],
                                         prt[:, blk * P:(blk + 1) * P], vm[:, j, h * M_V:(h + 1) * M_V],
                                         start=j == 0, stop=j == qt)
                last.then_inc(mla_pe.sem, 1)

            SWA_SETS = ((2, 4, 3), (1, 0, 5))

            def swa_scores(m, h):
                rows = slice(SDH * (h // 2), SDH * (h // 2 + 1))
                for qt in range(TT):
                    o = bank[SWA_SETS[h % 2][qt // 2]]
                    c = 2 * P * (qt % 2)
                    mask = C_SWA if qt else C_SWA0
                    k0 = max(qt - 1, 0) * P
                    n = (qt + 1) * P - k0
                    pe.matmul(o[:, c:c + 2 * P], ident16[:], masks[:, mask - C_CAUSAL:mask - C_CAUSAL + 2 * P], start=True, stop=False)
                    last = pe.matmul(o[:, c + 2 * P - n:c + 2 * P], aq[rows, h % 2, qt * P:(qt + 1) * P],
                                     ak[rows, k0:k0 + n], start=False, stop=True)
                last.then_inc(swa_sc.sem, 1)

            def swa_values(m, h):
                it = m * SWH + h
                pe.wait_ge(*swa_ex.at(it, "X"))
                if h == 0:
                    pe.wait_ge(*mla_ev.at(m * MH + MH - 1, "E2"))
                    pe.wait_ge(*mla_dve.at(m * MH + MH - 1, "E"))
                for b, blocks in ((6, (4, 5, 6, 7)), (7, (1, 2, 3))):
                    for j, blk in enumerate(blocks):
                        last = pe.transpose(bank[b][:, j * P:(j + 1) * P], pr[:, h % 2, blk * P:(blk + 1) * P], ident)
                    last.then_inc(swa_pe.sem, 1)
                pe.wait_ge(*swa_ev.at(it, "E0"))
                pe.wait_ge(*swa_dve.at(it, "E"))
                for qt in range(TT):
                    for j in range(max(qt - 1, 0), qt + 1):
                        blk = 2 * qt + j - qt + 1
                        last = pe.matmul(bank[SWA_SETS[h % 2][2]][:, qt * SDH:(qt + 1) * SDH],
                                         prt[:, blk * P:(blk + 1) * P],
                                         vtm[:, j, SDH * (h // 2):SDH * (h // 2 + 1)],
                                         start=j == max(qt - 1, 0), stop=j == qt)
                last.then_inc(swa_pe.sem, 1)

            STICK = ((0, 0), (1, 0), (2, 0), (1, 384))
            STICK_BANKS = ((2, 3, 4), (1, 5, 0))

            def stick_scores(m, h):
                rows = slice(BDH * (h % 2), BDH * (h % 2 + 1))
                for j in range(TT):
                    b, c = STICK[j]
                    n = S - j * P
                    last = pe.matmul(bank[STICK_BANKS[h % 2][b]][:, c:c + n], dk[rows, h // 2, j * P:(j + 1) * P],
                                     dq[rows, h // 2, j * P:S], start=True, stop=True)
                last.then_inc(sb_sc.sem, 1)

            def stick_after(m, h):
                pe.wait_ge(*sb_keep.at(m * BH + h, "K"))
                for i in range(TT):
                    b, c = STICK[i]
                    o = bank[STICK_BANKS[h % 2][b]]
                    for j in range(i, TT):
                        n = S - j * P
                        at = STICK_AT[j]
                        tri = cst[:, C_NTRI:C_NTRI + P] if j == i else cst[:, C_NONE:C_NONE + P]
                        pe.matmul(o[:, c + (j - i) * P:c + S - i * P], tri, spl[:, h % 2, at:at + n],
                                  start=j == i, stop=False)
                    last = pe.matmul(o[:, c:c + P], ident16[:], masks[:, C_STRICT - C_CAUSAL:C_STRICT - C_CAUSAL + P], start=False, stop=True)
                last.then_inc(sb_pe.sem, 1)

            def stick_values(m, h):
                pe.wait_ge(*sb_act.at(m * BH + h, "P"))
                for qt in range(TT):
                    for j in range(qt + 1):
                        at = STICK_AT[j] + (qt - j) * P
                        last = pe.matmul(bank[6 + h % 2][:, qt * BDH:(qt + 1) * BDH], lsg[:, h % 2, at:at + P],
                                         vtm[:, j, 2 * SDH + h * BDH:2 * SDH + (h + 1) * BDH],
                                         start=j == 0, stop=j == qt)
                last.then_inc(sb_pe.sem, 1)

            def hybrid(m):
                q0 = SECOND + m * LAYER2
                n = FINAL + 1 + m
                token_major(q0 + BT_TM, (4, 5, 6, 7), TM_COLS, n)
                col_panel(bank[2][:], 0, q0 + BT_CQ)
                col_panel(bank[3][:], 1, q0 + BT_CQ + 1)
                pe.wait_ge(*chain.at(n, "RB"))
                col_panel(bank[0][:], 0, q0 + BT_CKV)
                col_panel(bank[1][:], 1, q0 + BT_AK)
                pe.wait_ge(*pj.at(m, "T1"))
                pe.wait_ge(*lat.at(m, "SUM"))
                pe.matmul(bank[4][:], ones, qsq[:, 0, :], start=True, stop=True).then_inc(lat_pe.sem, 1)
                pe.wait_ge(*lat_act.at(m, "SK"))
                pe.matmul(bank[5][:], ones, ksq[:], start=True, stop=True).then_inc(lat_pe.sem, 1)
                for i, (b, free) in enumerate(((2, "Q0"), (3, "Q1"), (0, "KV"), (1, "AK"), (2, "A0"), (3, "A1"))):
                    pe.wait_ge(*pj.at(m, free))
                    col_panel(bank[b][:], i % 2, q0 + BT_AQ + i)
                pe.wait_ge(*lat.at(m, "LK"))
                panel_ready(q0 + BT_UQ)
                for h in range(MH):
                    for k in range(2):
                        last = mm3(bank[4 + h][:], (0, unit(2 * h + k)), cqh[:, k, :], cql[:, k, :], k == 0, k == 1)
                last.then_inc(panel_done, 1)
                panel_ready(q0 + BT_UKV)
                for h in range(MH):
                    pe.wait_ge(*pj.at(m, ("D0", "D1", "E0", "E1")[h]))
                    mm3(bank[h][:], (1, slice(h * M_NOPE, h * M_NOPE + P)), ckh[:], ckl[:], True, True)
                for t in range(TT):
                    if t % 2 == 0:
                        pe.wait_ge(*mla.at(m, f"R{t // 2}"))
                    o = bank[4 + t // 2][:, (t % 2) * GROUP:(t % 2 + 1) * GROUP]
                    w = slice(MH * M_NOPE, MH * (M_NOPE + M_V))
                    tok = slice(t * P, (t + 1) * P)
                    pe.matmul(o, ckh[:, tok], wh[:, 1, w], start=True, stop=False)
                    pe.matmul(o, ckl[:, tok], wh[:, 1, w], start=False, stop=False)
                    pe.matmul(o, ckh[:, tok], wl[:, 1, w], start=False, stop=True)
                pe.wait_ge(*mla.at(m, "R2"))
                for k in range(KD):
                    c = KR_AT + k * KR_W
                    last = mm3(bank[6][:], (1, slice(c, c + P)), xh[:, k, :], xl[:, k, :], k == 0, k == KD - 1)
                last.then_inc(panel_done, 1)
                for i in range(2):
                    for j in range(3):
                        if i == 0:
                            pe.wait_ge(*kv_act.at(m, f"N{j}"))
                        elif j == 0:
                            pe.wait_ge(*kv.at(m, "V1"))
                        elif j == 1:
                            pe.wait_ge(*kv.at(m, "KS"))
                        else:
                            pe.wait_ge(*mla.at(m, "R3"))
                        c = 3 * i + j
                        col_panel(bank[(0, 1, 2, 5, 6, 7)[c]][:], c % 2, q0 + BT_CONV + c)
                pe.wait_ge(*kv_act.at(m, "C3"))
                pe.wait_ge(*kv.at(m, "KR"))
                pe.wait_ge(*conv.at(m * 2, "G"))
                mla_scores(m, 0)
                pe.wait_ge(*conv.at(m * 2 + 1, "Y"))
                for h in range(MH):
                    if h < MH - 1:
                        if h:
                            pe.wait_ge(*mla_dve.at(m * MH + h - 1, "O"))
                        mla_scores(m, h + 1)
                    else:
                        pe.wait_ge(*mla_dve.at(m * MH + h - 1, "O"))
                        swa_scores(m, 0)
                    mla_values(m, h)
                for h in range(SWH):
                    pe.wait_ge(*(swa_dve.at(m * SWH + h - 1, "O") if h else mla_dve.at(m * MH + MH - 1, "O")))
                    if h < SWH - 1:
                        swa_scores(m, h + 1)
                    else:
                        stick_scores(m, 0)
                    swa_values(m, h)
                for h in range(BH):
                    if h == 0:
                        pe.wait_ge(*swa_dve.at(m * SWH + SWH - 1, "O"))
                        pe.wait_ge(*swa_ev.at(m * SWH + SWH - 1, "E0"))
                    if h < BH - 1:
                        if h:
                            pe.wait_ge(*sb_dve.at(m * BH + h - 1, "T"))
                        stick_scores(m, h + 1)
                    stick_after(m, h)
                    if h >= 2:
                        pe.wait_ge(*sb_act.at(m * BH + h - 2, "O"))
                    stick_values(m, h)
                def turn(y, i):
                    pe.wait_ge(*gn.at(m, f"N{i}"))
                    for c in range(2):
                        for t in range(TT):
                            last = pe.transpose(bank[2 + 2 * i + c][:, t * P:(t + 1) * P], y[:, t, c * P:(c + 1) * P],
                                                ident)
                    last.then_inc(gn_pe.sem, 1)

                pe.wait_ge(*sb_dve.at(m * BH + BH - 1, "T"))
                pe.wait_ge(*gn.at(m, "SUM"))
                pe.matmul(bank[0][:], ones, bsq[:, 0, :], start=True, stop=True).then_inc(gn_pe.sem, 1)
                col_panel(bank[1][:], 0, q0 + BT_GATE)
                turn(y_swa, 0)
                turn(y_mla, 1)
                pe.wait_ge(*gn_act.at(m, "DB"))
                col_panel(bank[0][:], 1, q0 + BT_GATE + 1)
                pe.wait_ge(*sb_act.at(m * BH + BH - 1, "O"))
                turn(y_sb, 2)
                for d in range(2, KD):
                    pe.wait_ge(*gate.at(m * KD + d - 2, "G"))
                    col_panel(bank[(d + 1) % 2][:], d % 2, q0 + BT_GATE + d)
                for d in range(KD):
                    if d < 2:
                        pe.wait_ge(*gn.at(m, f"A{d}"))
                    else:
                        pe.wait_ge(*z_act.at(m * KD + d - 2, "Z"))
                    panel_ready(q0 + BT_WOUT + d)
                    for k in range(KD):
                        if d == 0:
                            pe.wait_ge(*gate.at(m * KD + k, "L"))
                        last = mm3(bank[2 + d % 2][:], (d % 2, unit(k)), ygh[:, k, :], ygl[:, k, :], k == 0, k == KD - 1)
                    last.then_inc(panel_done, 1)
                pe.wait_ge(*z_sum.at(m * KD + KD - 1, "A"))
                for t in range(TT):
                    last = pe.matmul(bank[4][:, t:t + 1], ssq[:, t * P:(t + 1) * P], ones[:, 0:1], start=True, stop=True)
                last.then_inc(post_pe.sem, 1)
                pe.wait_ge(*post.at(m, "DG"))
                pe.matmul(bank[5][:], ones, diag[:], start=True, stop=True).then_inc(post_pe.sem, 1)

            pe.wait_ge(loaded, 64)
            pe.wait_ge(mask_set, 2)
            with pe.Fori(0, DEPTH) as l:
                p0 = l * LAYER1
                ffn_in(l * 2, l * 3, p0)
                ffn_out(l * 2, p0 + FFN_IN)
                n = l * 3 + 1
                for t in range(TT):
                    pe.wait_ge(*prep.at(n * KD + t, "X"))
                token_major(p0 + AT_RV, (4, 5, 6, 7), S, n)
                pe.wait_ge(*chain.at(n, "RB"))
                token_major(p0 + AT_FV, (0, 1, 2, 3), S)
                pe.wait_ge(*tm.at(l, "RV3"))
                pe.wait_ge(*ffs.at(l, "L"))
                for k in range(KD):
                    c = slice(k * FF_W, k * FF_W + P)
                    pe.matmul(bank[4][:], ffh[:, c], xh[:, k, :], start=k == 0, stop=False)
                    pe.matmul(bank[4][:], ffh[:, c], xl[:, k, :], start=False, stop=False)
                    last = pe.matmul(bank[4][:], ffl[:, c], xh[:, k, :], start=False, stop=k == KD - 1)
                last.then_inc(ffs_pe.sem, 1)
                with pe.Fori(0, RH // 2) as i:
                    for q in range(2):
                        pe.wait_ge(*tm.at(l, "FV3"))
                        pe.wait_ge(*rg.before(l * RH + i * 2))
                        col_panel(bank[q][:], q, p0 + AT_RG + i * 2 + q)
                retention(l, p0 + AT_RET)
                forgetting(l, p0 + AT_FOX)
                merge(l, p0 + AT_MERGE)
                mix_out(l, n + 1, p0 + AT_WOUT)
                ffn_in(l * 2 + 1, l * 3 + 2, p0 + AT_FFN2)
                ffn_out(l * 2 + 1, p0 + AT_FFN2 + FFN_IN)

            chain_col(FINAL, 4)
            chain_bc(FINAL, 5)
            with pe.Fori(0, DEPTH) as m:
                hybrid(m)

        @block.scalar
        def _(act):
            def squares(n):
                with act.Fori(0, KD) as d:
                    act.wait_ge(*prep.at(n * KD + d, "X"))
                    act.activation(sq[:], x[:, d, :], ACT.Square).then_inc(prep_sq.sem, 1)

            def chain_std(n, b):
                act.wait_ge(*chain_pe.at(n, "COL"))
                act.activation(std_col[:], bank[b][:, 0:TT], ACT.Sqrt, bias=eps[:], scale=1.0 / D)\
                   .then_inc(chain_sd.sem, 1)

            def ffn_in(f, n):
                chain_std(n, 4)
                with act.Fori(0, KF) as j:
                    it = f * KF + j
                    act.wait_ge(*fin.at(it, "A"))
                    act.activation(sa[:], ta[:], ACT.Silu).then_inc(fin_act.sem, 1)
                    act.wait_ge(*fin.at(it, "U"))
                    act.activation(uh[:, j, :], u32[:], ACT.Copy).then_inc(fin_act.sem, 1)

            def ret_out(it, h):
                act.wait_ge(*ret_y.at(it, "Y"))
                act.activation(yrh[:, h, :], y32[:], ACT.Copy).then_inc(ret_h.sem, 1)

            def retention(l):
                def head(h, first):
                    it = l * RH + h
                    for src, name in ((tq, "Q"), (tk, "K")):
                        act.wait_ge(*ret.at(it, name))
                        if name == "K":
                            act.wait_ge(*ret.at(it, "QS"))
                        act.activation(sw[0:64, :], src[64:128, :], ACT.Copy).then_inc(ret_sw.sem, 1)
                        act.activation(sw[64:128, :], src[0:64, :], ACT.Copy).then_inc(ret_sw.sem, 1)
                        if name == "Q" and not first:
                            ret_out(it - 1, h - 1)
                    act.wait_ge(*ret_pv.at(it, "P"))
                    for t in range(TT):
                        act.activation(sw[:, t * P:(t + 1) * P], bank[4][:, t * P:(t + 1) * P], ACT.Square,
                                       accum_out=hsum[:, t:t + 1]).then_inc(ret_sq.sem, 1)
                    act.wait_ge(*ret_sq.at(it, "S3"))
                    act.activation(hstd[:], hsum[:], ACT.Sqrt, bias=eps[:], scale=1.0 / RDK).then_inc(ret_sq.sem, 1)

                head(0, True)
                with act.Fori(1, RH) as h:
                    head(h, False)
                ret_out(l * RH + RH - 1, RH - 1)

            def fox_probs(it, e):
                act.wait_ge(*fx_m[e].at(it, "N"))
                for qt in range(TT):
                    b, c = HEAD_AT[qt]
                    n = (qt + 1) * P
                    last = act.activation(fp[:, e, FIRST_BLOCK[qt] * P:FIRST_BLOCK[qt] * P + n], bank[b][:, c:c + n],
                                          ACT.Exp, bias=fnm[:, e, qt:qt + 1], scale=FDH ** -0.5,
                                          accum_out=fsum[:, e, qt:qt + 1])
                last.then_inc(fx_x[e].sem, 1)

            def fox_turned(it, e, first):
                act.wait_ge(*fx_t[e].at(it, "T0"))
                if e:
                    act.wait_ge(*fx_v[0].at(it, "P"))
                elif not first:
                    act.wait_ge(*fx_v[1].at(it - 1, "P"))
                act.activation(fpt[:, 6 * P:10 * P], bank[6][:], ACT.Copy).then_inc(fx_c[e].sem, 1)
                act.wait_ge(*fx_t[e].at(it, "T2"))
                act.activation(fpt[:, P:3 * P], bank[5][:, 0:2 * P], ACT.Copy).then_inc(fx_c[e].sem, 1)

            def fox_out(it, t2, b):
                act.wait_ge(*fx_y.at(it, "TR"))
                act.activation(yfh[:, t2, :], bank[b][:], ACT.Copy).then_inc(fx_h.sem, 1)

            def forgetting(l):
                pairs = FH // 2

                def pair(t2, first, last_pair):
                    it = l * pairs + t2
                    if not first:
                        fox_out(it - 1, t2 - 1, 1)
                    fox_turned(it, 0, first)
                    fox_probs(it, 1)
                    fox_turned(it, 1, first)
                    if not last_pair:
                        fox_probs(it + 1, 0)

                fox_probs(l * pairs, 0)
                pair(0, True, False)
                with act.Fori(1, pairs - 1) as t2:
                    pair(t2, False, False)
                pair(pairs - 1, False, True)
                fox_out(l * pairs + pairs - 1, pairs - 1, 2)

            def mla_probs(m, h):
                it = m * MH + h
                act.wait_ge(*mla_mx.at(it, "N"))
                for qt in range(TT):
                    b, c = SETS[h % 2][qt]
                    n = (qt + 1) * P
                    at = FIRST_BLOCK[qt] * P
                    last = act.activation(pr[:, h % 2, at:at + n], bank[b][:, c:c + n], ACT.Exp,
                                          bias=snm[:, h % 2, qt:qt + 1], scale=(M_NOPE + M_ROPE) ** -0.5,
                                          accum_out=ssum[:, h % 2, qt:qt + 1])
                last.then_inc(mla_ex.sem, 1)

            def swa_probs(m, h):
                it = m * SWH + h
                act.wait_ge(*swa_mx.at(it, "N"))
                for qt in range(TT):
                    o = bank[((2, 4), (1, 0))[h % 2][qt // 2]]
                    c = 2 * P * (qt % 2)
                    last = act.activation(pr[:, h % 2, qt * 2 * P:(qt + 1) * 2 * P], o[:, c:c + 2 * P], ACT.Exp,
                                          bias=snm[:, h % 2, qt:qt + 1], scale=SDH ** -0.5,
                                          accum_out=ssum[:, h % 2, qt:qt + 1])
                last.then_inc(swa_ex.sem, 1)
                act.activation(esk[:, h % 2, :], snm[:, h % 2, :], ACT.Exp,
                               bias=vecs[:, bass.ds(m * SWH + V_SINK + h, 1)]).then_inc(swa_ex.sem, 1)

            PIECES = ((0, 0, 512), (1, 512, 512), (2, 1024, 256))

            def stick_logs(m, h):
                it = m * BH + h
                buf = lsg[:, h % 2, :]
                act.wait_ge(*sb_sc.at(it, "Z"))
                for b, c, n in PIECES:
                    last = act.activation(buf[:, c:c + n], bank[((2, 3, 4), (1, 5, 0))[h % 2][b]][:, 0:n], ACT.Abs)
                last.then_inc(sb_ln.sem, 1)
                act.wait_ge(*sb_ln.at(it, "AB"))
                act.activation(buf, buf, ACT.Exp, scale=-1.0).then_inc(sb_ln.sem, 1)
                act.wait_ge(*sb_ln.at(it, "EX"))
                act.activation(buf, buf, ACT.Ln, bias=ones[:, 0:1]).then_inc(sb_ln.sem, 1)

            def hybrid(m):
                n = FINAL + 1 + m
                chain_std(n, 0)
                for i in range(2):
                    act.wait_ge(*pj.at(m, f"Q{i}"))
                    act.activation(qsq[:, i, :], cq[:, i, :], ACT.Square).then_inc(lat_act.sem, 1)
                act.wait_ge(*pj.at(m, "KV"))
                act.activation(ksq[:], ckv[:], ACT.Square).then_inc(lat_act.sem, 1)
                act.wait_ge(*lat_pe.at(m, "Q"))
                act.activation(qin[:], bank[4][:], ACT.Sqrt, bias=eps[:], scale=1.0 / QR).then_inc(lat_act.sem, 1)
                act.wait_ge(*lat_pe.at(m, "K"))
                act.activation(kin[:], bank[5][:], ACT.Sqrt, bias=eps[:], scale=1.0 / KVR).then_inc(lat_act.sem, 1)
                for name, dst in (("N0", cqh[:, 0, :]), ("N1", cqh[:, 1, :]), ("NK", ckh[:])):
                    act.wait_ge(*lat.at(m, name))
                    act.activation(dst, cn[:], ACT.Copy).then_inc(lat_act.sem, 1)
                act.wait_ge(panel_done, SECOND + m * LAYER2 + BT_UQ + 1)
                act.wait_ge(*mla.at(m, "Z"))
                for h in range(MH):
                    b = bank[4 + h]
                    act.activation(mq[0:M_NOPE, h, :], b[0:M_NOPE, :], ACT.Copy).then_inc(mla_act.sem, 1)
                    if h:
                        act.wait_ge(*mla.at(m, f"S{h - 1}"))
                    act.activation(msw[64:80, :], b[96:112, :], ACT.Copy).then_inc(mla_act.sem, 1)
                    act.activation(msw[96:112, :], b[64:80, :], ACT.Copy).then_inc(mla_act.sem, 1)
                act.wait_ge(panel_done, SECOND + m * LAYER2 + BT_UKV + 1)
                for h in range(MH):
                    act.activation(mk[0:M_NOPE, h, :], bank[h][0:M_NOPE, :], ACT.Copy).then_inc(kv_act.sem, 1)
                act.wait_ge(*kv.at(m, "KS"))
                act.wait_ge(*mla.at(m, f"S{MH - 1}"))
                act.activation(kx[64:112, :], krs[0:KR_W, :], ACT.Copy).then_inc(kv_act.sem, 1)
                act.activation(msw[64:80, :], krs[32:48, :], ACT.Copy).then_inc(kv_act.sem, 1)
                act.activation(msw[96:112, :], krs[0:16, :], ACT.Copy).then_inc(kv_act.sem, 1)
                act.wait_ge(*kv.at(m, "KR"))
                for h in range(1, MH):
                    act.activation(mk[64:112, h, :], mk[64:112, 0, :], ACT.Copy).then_inc(kv_act.sem, 1)
                mla_probs(m, 0)
                for h in range(MH):
                    it = m * MH + h
                    if h < MH - 1:
                        mla_probs(m, h + 1)
                    else:
                        swa_probs(m, 0)
                    act.wait_ge(*mla_pe.at(it, "T0"))
                    act.activation(prt[:, 6 * P:10 * P], bank[6][:], ACT.Copy).then_inc(mla_ev.sem, 1)
                    act.wait_ge(*mla_pe.at(it, "T2"))
                    act.activation(prt[:, P:3 * P], bank[6][:, 0:2 * P], ACT.Copy).then_inc(mla_ev.sem, 1)
                for h in range(SWH):
                    it = m * SWH + h
                    if h < SWH - 1:
                        swa_probs(m, h + 1)
                    act.wait_ge(*swa_pe.at(it, "T0"))
                    act.activation(prt[:, 4 * P:8 * P], bank[6][:], ACT.Copy).then_inc(swa_ev.sem, 1)
                stick_logs(m, 0)
                for h in range(BH):
                    it = m * BH + h
                    if h < BH - 1:
                        if h:
                            act.wait_ge(*sb_pe.at(it - 1, "V"))
                        stick_logs(m, h + 1)
                    act.wait_ge(*sb_dve.at(it, "T"))
                    act.activation(lsg[:, h % 2, :], lsg[:, h % 2, :], ACT.Exp).then_inc(sb_act.sem, 1)
                    act.wait_ge(*sb_pe.at(it, "V"))
                    act.activation(y_sb[:, :, h * BDH:(h + 1) * BDH],
                                   bank[6 + h % 2][:, 0:TT * BDH].rearrange("p (t c) -> p t c", c=BDH),
                                   ACT.Copy).then_inc(sb_act.sem, 1)
                for i in range(2):
                    act.activation(bsq[:, i, :], y_conv[:, i, :], ACT.Square).then_inc(gn_act.sem, 1)
                for i, y in enumerate((y_swa, y_mla, y_sb)):
                    if i == 0:
                        act.wait_ge(*swa_dve.at(m * SWH + SWH - 1, "O"))
                    else:
                        act.wait_ge(*gn_act.at(m, f"S{i - 1}"))
                    if i == 2:
                        act.wait_ge(*sb_act.at(m * BH + BH - 1, "O"))
                    for t in range(TT):
                        last = act.activation(gsq[:, t, :], y[:, t, :], ACT.Square, accum_out=gsum[:, i, t:t + 1])
                    last.then_inc(gn_act.sem, 1)
                act.wait_ge(*gn_pe.at(m, "B"))
                act.activation(bstd[:], bank[0][:], ACT.Sqrt, bias=eps[:], scale=1.0 / GROUP).then_inc(gn_act.sem, 1)
                for i in range(3):
                    act.wait_ge(*gn_act.at(m, f"S{i}"))
                    act.activation(gstd[:, i, :], gsum[:, i, :], ACT.Sqrt, bias=eps[:], scale=1.0 / GROUP)\
                       .then_inc(gn_act.sem, 1)
                for d in range(KD):
                    it = m * KD + d
                    act.wait_ge(*gate.at(it, "G"))
                    act.activation(gs[:], gt[:], ACT.Silu).then_inc(gate_act.sem, 1)
                    act.wait_ge(*gate.at(it, "Y"))
                    act.activation(ygh[:, d, :], yg[:], ACT.Copy).then_inc(gate_act.sem, 1)
                for d in range(KD):
                    it = m * KD + d
                    act.wait_ge(panel_done, SECOND + m * LAYER2 + BT_WOUT + d + 1)
                    act.activation(z[:, d, :], bank[2 + d % 2][:], ACT.Copy).then_inc(z_act.sem, 1)
                    act.wait_ge(*z_act.at(it, "Z"))
                    if d:
                        act.wait_ge(*z_sum.at(it - 1, "A"))
                    act.activation(sq[:], z[:, d, :], ACT.Square).then_inc(z_act.sem, 1)
                act.wait_ge(*post_pe.at(m, "COL"))
                act.activation(std_col[:], bank[4][:, 0:TT], ACT.Sqrt, bias=eps[:], scale=1.0 / D)\
                   .then_inc(post_sd.sem, 1)
                squares(n + 1)

            act.wait_ge(loaded, 64)
            act.wait_ge(memsets, 1)
            act.activation(start_a[:], eps[:], ACT.Copy).then_inc(rg_act.sem, 1)
            squares(0)
            act.wait_ge(*trig.at(0, "s5"))
            act.activation(sin2[64:112, :], ang[64:112, :], ACT.Sin).then_inc(trig_act.sem, 1)
            act.wait_ge(*trig.at(0, "c5"))
            act.activation(cos2[64:112, :], turn[64:112, :], ACT.Sin).then_inc(trig_act.sem, 1)
            with act.Fori(0, DEPTH) as l:
                ffn_in(l * 2, l * 3)
                squares(l * 3 + 1)
                act.wait_ge(*prep.at((l * 3 + 1) * KD + KD - 1, "X"))
                act.dma_start(dec[:], decay).then_inc(tab_in, 16)
                act.dma_start(rp[:], rope).then_inc(tab_in, 16)
                act.dma_start(ffraw[:], ff_w[l]).then_inc(tab_in, 16)
                chain_std(l * 3 + 1, 0)
                act.wait_ge(*ffs.at(l, "ZB"))
                act.activation(fa[0:FF_W], fz[0:FF_W], ACT.Abs).then_inc(ffs_act.sem, 1)
                act.wait_ge(*ffs_act.at(l, "ABS"))
                act.activation(fa[0:FF_W], fa[0:FF_W], ACT.Exp, scale=-1.0).then_inc(ffs_act.sem, 1)
                act.wait_ge(*ffs_act.at(l, "EXP"))
                act.activation(fa[0:FF_W], fa[0:FF_W], ACT.Ln, bias=ones[0:FF_W, 0:1]).then_inc(ffs_act.sem, 1)
                with act.Fori(0, RH) as h:
                    act.wait_ge(*rg.at(l * RH + h, "T"))
                    act.activation(rgs[:, h, :], tg[:], ACT.Silu).then_inc(rg_act.sem, 1)
                retention(l)
                forgetting(l)
                with act.Fori(0, KD) as d:
                    it = l * KD + d
                    act.wait_ge(*mrg_d.at(it, "G"))
                    act.activation(sr[:], gate_r[:, d, :], ACT.Sigmoid).then_inc(mrg_a.sem, 1)
                    act.activation(sf[:], tgf[:], ACT.Sigmoid).then_inc(mrg_a.sem, 1)
                    act.wait_ge(*mrg_d.at(it, "M"))
                    act.activation(mh[:, d, :], mg[:], ACT.Copy).then_inc(mrg_a.sem, 1)
                squares(l * 3 + 2)
                ffn_in(l * 2 + 1, l * 3 + 2)
                squares(l * 3 + 3)
            chain_std(FINAL, 4)
            squares(FINAL + 1)
            with act.Fori(0, DEPTH) as m:
                hybrid(m)

        @block.vector
        def _(dve):
            def prepare(n, d, g):
                gain = vecs[:, bass.ds(g * KD + d, 1)]
                dve.wait_ge(*prep.at(n * KD + d, "X"))
                dve.tensor_scalar(xh[:, d, :], x[:, d, :], gain, None, ALU.mult).then_inc(prep.sem, 1)
                dve.wait_ge(*prep.at(n * KD + d, "XH"))
                dve.scalar_tensor_tensor(out=xl[:, d, :], in0=x[:, d, :], scalar=gain,
                                         in1=xh[:, d, :].bitcast(F32), op0=ALU.mult,
                                         op1=ALU.subtract).then_inc(prep.sem, 1)

            def add_squares(n, d, first):
                dve.wait_ge(*prep_sq.at(n * KD + d, "SQ"))
                if first:
                    dve.tensor_copy(ssq[:], sq[:]).then_inc(prep.sem, 1)
                else:
                    dve.tensor_tensor(ssq[:], ssq[:], sq[:], ALU.add).then_inc(prep.sem, 1)

            def norm_chain(n, b):
                dve.wait_ge(*chain_sd.at(n, "SD"))
                dve.reciprocal(rstd_col[:], std_col[:]).then_inc(chain.sem, 1)
                dve.wait_ge(*chain.at(n, "RC"))
                for t in range(TT):
                    last = dve.tensor_scalar(diag[:, t * P:(t + 1) * P], ident, rstd_col[:, t:t + 1], None, ALU.mult)
                last.then_inc(chain.sem, 1)
                dve.wait_ge(*chain_pe.at(n, "BC"))
                dve.tensor_copy(rstd[:], bank[b][:]).then_inc(chain.sem, 1)

            def scaled(dst, src, st):
                dve.tensor_tensor(dst, src, rstd[:], ALU.mult).then_inc(st.sem, 1)

            def ffn_in(f, n, idx):
                norm_chain(n, 5)
                with dve.Fori(0, KF // 2) as i:
                    dve.wait_ge(*chain.at(n, "RB"))
                    for q in range(2):
                        it = f * KF + i * 2 + q
                        at = idx + i * 4 + 2 * q
                        dve.wait_ge(panel_done, at + 1)
                        scaled(ta[:], bank[2 * q][:], fin)
                        dve.wait_ge(panel_done, at + 2)
                        scaled(tb[:], bank[2 * q + 1][:], fin)
                        dve.wait_ge(*fin_act.at(it, "SILU"))
                        dve.wait_ge(*fin.at(it, "B"))
                        dve.tensor_tensor(u32[:], sa[:], tb[:], ALU.mult).then_inc(fin.sem, 1)
                        dve.wait_ge(*fin_act.at(it, "UH"))
                        dve.tensor_tensor(ul[:, i * 2 + q, :], u32[:], uh[:, i * 2 + q, :].bitcast(F32),
                                          ALU.subtract).then_inc(fin.sem, 1)

            def ffn_out(f, n, idx):
                rest = KF - KT_MAJOR
                steps = 0
                for d in range(KD):
                    done = (d + 1) * rest
                    if done % UNITS == 0:
                        dve.wait_ge(panel_done, idx + KT_MAJOR + done // UNITS)
                    else:
                        dve.wait_ge(fout.sem, f * (KD - 2) + steps + 1)
                        steps += 1
                    dve.scalar_tensor_tensor(out=x[:, d, :], in0=bank[(4 + d) % 8][:], scalar=0.5,
                                             in1=x[:, d, :], op0=ALU.mult, op1=ALU.add).then_inc(prep.sem, 1)
                    prepare(n, d, n)
                    add_squares(n, d, d == 0)

            def ret_norm(it):
                dve.wait_ge(*ret_sq.at(it, "SD"))
                dve.reciprocal(hinv[:], hstd[:]).then_inc(ret_n.sem, 1)
                dve.wait_ge(*ret_n.at(it, "RC"))
                for t in range(TT):
                    dve.tensor_scalar(yn[:, t * P:(t + 1) * P], bank[4][:, t * P:(t + 1) * P],
                                      hinv[:, t:t + 1], None, ALU.mult).then_inc(ret_n.sem, 1)

            def ret_out(it, l, h):
                dve.wait_ge(*ret_tr.at(it, "P"))
                dve.scalar_tensor_tensor(out=y32[:], in0=bank[5][:], scalar=vecs[:, bass.ds(l * RH + h + V_RET, 1)],
                                         in1=rgs[:, h, :], op0=ALU.mult, op1=ALU.mult).then_inc(ret_y.sem, 1)
                dve.wait_ge(*ret_h.at(it, "YH"))
                dve.tensor_tensor(yrl[:, h, :], y32[:], yrh[:, h, :].bitcast(F32), ALU.subtract).then_inc(ret_y.sem, 1)

            def retention(l, idx):
                def rotated(it, dst, src, name):
                    dve.wait_ge(*ret.at(it, name))
                    dve.tensor_tensor(m1[:], src[:], rp[:, 0, :], ALU.mult).then_inc(ret.sem, 1)
                    dve.wait_ge(*ret_sw.at(it, name + "1"))
                    dve.tensor_tensor(dst[:], sw[:], rp[:, 1, :], ALU.mult).then_inc(ret.sem, 1)
                    dve.wait_ge(*ret.at(it, name + "S"))
                    dve.tensor_tensor(dst[:], dst[:], m1[:], ALU.add).then_inc(ret.sem, 1)

                def head(h, first):
                    it = l * RH + h
                    at = idx + h * 4
                    if first:
                        dve.wait_ge(*rg_act.before((l + 1) * RH))
                    else:
                        ret_norm(it - 1)
                    dve.wait_ge(panel_done, at + 1)
                    scaled(tq[:], bank[0][:], ret)
                    rotated(it, qr, tq, "Q")
                    if not first:
                        dve.wait_ge(*ret.at(it, "QR"))
                        ret_out(it - 1, l, h - 1)
                    dve.wait_ge(panel_done, at + 2)
                    scaled(tk[:], bank[1][:], ret)
                    dve.wait_ge(*ret.at(it, "QR"))
                    rotated(it, kr, tk, "K")
                    dve.wait_ge(panel_done, at + 3)
                    scaled(gate_r[:, h * 2, :], bank[2][:], ret)
                    dve.wait_ge(*ret_sc.at(it, "P"))
                    for i in range(TT):
                        dve.tensor_tensor(pt[:, OFF[i]:OFF[i] + S - i * P], bank[4 + i][:, 0:S - i * P],
                                          dec[:, h, 0:S - i * P], ALU.mult).then_inc(ret.sem, 1)
                    dve.wait_ge(panel_done, at + 4)
                    scaled(gate_r[:, h * 2 + 1, :], bank[3][:], ret)

                head(0, True)
                with dve.Fori(1, RH) as h:
                    head(h, False)
                ret_norm(l * RH + RH - 1)

            def fox_load(it, t2, idx):
                for e, rows in enumerate((slice(FDH, FF_W), slice(0, FH))):
                    dve.tensor_scalar(fk[rows, e, :], cum[rows, :], cst[rows, bass.ds(t2 * 2 + C_HOT + e, 1)],
                                      None, ALU.mult).then_inc(fx_q.sem, 1)
                for k, dst in enumerate((fq, fk)):
                    dve.wait_ge(panel_done, idx + t2 * 2 + k + 1)
                    for e in range(2):
                        rows = slice(e * FDH, (e + 1) * FDH)
                        dve.tensor_tensor(dst[rows, e, :], bank[k][rows, :], rstd[rows, :], ALU.mult)\
                           .then_inc(fx_q.sem, 1)

            def fox_max(it, e):
                dve.wait_ge(*fx_s[e].at(it, "P"))
                for qt in range(TT):
                    b, c = HEAD_AT[qt]
                    last = dve.tensor_reduce(fmx[:, e, qt:qt + 1], bank[b][:, c:c + (qt + 1) * P], AX_X, ALU.max)
                last.then_inc(fx_m[e].sem, 1)
                dve.wait_ge(*fx_m[e].at(it, "M"))
                dve.tensor_scalar(fnm[:, e, :], fmx[:, e, :], -FDH ** -0.5, None, ALU.mult).then_inc(fx_m[e].sem, 1)

            def fox_turned(it, e, first):
                dve.wait_ge(*fx_t[e].at(it, "T1"))
                if e:
                    dve.wait_ge(*fx_v[0].at(it, "P"))
                elif not first:
                    dve.wait_ge(*fx_v[1].at(it - 1, "P"))
                dve.tensor_copy(fpt[:, 0:P], bank[7][:, 0:P])
                dve.tensor_copy(fpt[:, 3 * P:6 * P], bank[7][:, P:4 * P]).then_inc(fx_o[e].sem, 1)
                dve.wait_ge(*fx_x[e].at(it, "X"))
                dve.reciprocal(finv[:, e, :], fsum[:, e, :]).then_inc(fx_o[e].sem, 1)

            def fox_normed(it, e):
                dve.wait_ge(*fx_o[e].at(it, "R"))
                dve.wait_ge(*fx_v[e].at(it, "P"))
                dve.tensor_tensor(fo[:, :, e * FDH:(e + 1) * FDH],
                                  bank[5][:, 2 * P:2 * P + TT * FDH].rearrange("p (t c) -> p t c", c=FDH),
                                  finv[:, e, :].rearrange("p (t c) -> p t c", c=1).to_broadcast([P, TT, FDH]),
                                  ALU.mult).then_inc(fx_o[e].sem, 1)

            def fox_out(it, t2, b):
                dve.wait_ge(*fx_h.at(it, "YH"))
                dve.tensor_tensor(yfl[:, t2, :], bank[b][:], yfh[:, t2, :].bitcast(F32), ALU.subtract)\
                   .then_inc(fx_l.sem, 1)

            def forgetting(l, idx):
                pairs = FH // 2

                def pair(t2, first, last_pair):
                    it = l * pairs + t2
                    fox_turned(it, 0, first)
                    if not first:
                        fox_out(it - 1, t2 - 1, 1)
                    fox_max(it, 1)
                    fox_normed(it, 0)
                    if not last_pair:
                        fox_load(it + 1, t2 + 1, idx)
                    fox_turned(it, 1, first)
                    if not last_pair:
                        fox_max(it + 1, 0)
                    fox_normed(it, 1)

                ret_out(l * RH + RH - 1, l, RH - 1)
                dve.wait_ge(fx_set, l * 4 + 4)
                fox_load(l * pairs, 0, idx)
                fox_max(l * pairs, 0)
                pair(0, True, False)
                with dve.Fori(1, pairs - 1) as t2:
                    pair(t2, False, False)
                pair(pairs - 1, False, True)
                fox_out(l * pairs + pairs - 1, pairs - 1, 2)

            def merge(l, idx):
                def tile(d, q, gate_at, out_at):
                    it = l * KD + d
                    g, r, f = (bank[b] for b in ((0, 3, 4), (1, 6, 7))[q])
                    dve.wait_ge(panel_done, gate_at + 1)
                    scaled(tgf[:], g[:], mrg_d)
                    dve.wait_ge(panel_done, out_at + 1)
                    dve.wait_ge(*mrg_a.at(it, "SF"))
                    dve.tensor_tensor(mr[:], r[:], sr[:], ALU.mult).then_inc(mrg_d.sem, 1)
                    dve.tensor_tensor(mf[:], f[:], sf[:], ALU.mult).then_inc(mrg_d.sem, 1)
                    dve.wait_ge(*mrg_d.at(it, "F"))
                    dve.tensor_tensor(mg[:], mr[:], mf[:], ALU.add).then_inc(mrg_d.sem, 1)
                    dve.wait_ge(*mrg_a.at(it, "MH"))
                    dve.tensor_tensor(ml[:, d, :], mg[:], mh[:, d, :].bitcast(F32), ALU.subtract)\
                       .then_inc(mrg_d.sem, 1)

                for q in range(2):
                    tile(q, q, idx + q, idx + 2 + q)
                with dve.Fori(1, KD // 2) as i:
                    for q in range(2):
                        tile(i * 2 + q, q, idx + i * 4 + 2 * q, idx + i * 4 + 2 * q + 1)

            def angles():
                R = slice(64, 112)
                a, b, p_ = ang[R, :], turn[R, :], rstd[R, :]
                full = 2 * np.pi
                c1 = 6.28125
                c2 = float(np.float32(full - c1))
                c3 = float(full - c1 - c2)
                dve.tensor_copy(p_, posi[R, :]).then_inc(trig.sem, 1)
                dve.wait_ge(*trig.at(0, "F"))
                dve.tensor_scalar(b, p_, cst[R, C_FREQ:C_FREQ + 1], None, ALU.mult).then_inc(trig.sem, 1)
                for w, dst, shift in (("s", a, 0.0), ("c", b, 0.25)):
                    dve.wait_ge(*trig.at(0, "A" if w == "s" else "s5"))
                    dve.tensor_scalar(p_, b, 1 / full, shift, ALU.mult, ALU.add).then_inc(trig.sem, 1)
                    dve.wait_ge(*trig.at(0, w + "0"))
                    dve.tensor_scalar(p_, p_, 12582912.0, 12582912.0, ALU.add, ALU.subtract).then_inc(trig.sem, 1)
                    dve.wait_ge(*trig.at(0, w + "1"))
                    src = b
                    for i, c in enumerate((c1, c2, c3)):
                        dve.scalar_tensor_tensor(out=dst, in0=p_, scalar=-c, in1=src, op0=ALU.mult, op1=ALU.add)\
                           .then_inc(trig.sem, 1)
                        dve.wait_ge(*trig.at(0, w + str(i + 2)))
                        src = dst
                    if w == "s":
                        dve.tensor_scalar(dst, dst, np.pi, -np.pi, ALU.min, ALU.max).then_inc(trig.sem, 1)
                    else:
                        dve.tensor_scalar(dst, dst, np.pi / 2, np.pi, ALU.add, ALU.min).then_inc(trig.sem, 1)
                dve.wait_ge(*trig_act.at(0, "COS"))
                dve.tensor_scalar(sin2[64:96, :], sin2[64:96, :], -1.0, None, ALU.mult).then_inc(trig.sem, 1)

            def mla_max(m, h):
                it = m * MH + h
                dve.wait_ge(*mla_sc.at(it, "SC"))
                for qt in range(TT):
                    b, c = SETS[h % 2][qt]
                    last = dve.tensor_reduce(smx[:, h % 2, qt:qt + 1], bank[b][:, c:c + (qt + 1) * P], AX_X, ALU.max)
                last.then_inc(mla_mx.sem, 1)
                dve.wait_ge(*mla_mx.at(it, "M"))
                dve.tensor_scalar(snm[:, h % 2, :], smx[:, h % 2, :], -(M_NOPE + M_ROPE) ** -0.5, None, ALU.mult)\
                   .then_inc(mla_mx.sem, 1)

            def swa_max(m, h):
                it = m * SWH + h
                dve.wait_ge(*swa_sc.at(it, "SC"))
                for i, b in enumerate(((2, 4), (1, 0))[h % 2]):
                    last = dve.tensor_reduce(smx[:, h % 2, 2 * i:2 * i + 2],
                                             bank[b][:].rearrange("p (t k) -> p t k", k=2 * P), AX_X, ALU.max)
                last.then_inc(swa_mx.sem, 1)
                dve.wait_ge(*swa_mx.at(it, "M"))
                dve.tensor_scalar(smx[:, h % 2, :], smx[:, h % 2, :], SDH ** -0.5,
                                  vecs[:, bass.ds(m * SWH + V_SINK + h, 1)], ALU.mult, ALU.max).then_inc(swa_mx.sem, 1)
                dve.wait_ge(*swa_mx.at(it, "S"))
                dve.tensor_scalar(snm[:, h % 2, :], smx[:, h % 2, :], -1.0, None, ALU.mult).then_inc(swa_mx.sem, 1)

            def normalised(dst, h, b, st):
                dve.tensor_tensor(dst[:, :, h * SDH:(h + 1) * SDH],
                                  bank[b][:, 0:TT * SDH].rearrange("p (t c) -> p t c", c=SDH),
                                  sinv[:, h % 2, :].rearrange("p (t c) -> p t c", c=1).to_broadcast([P, TT, SDH]),
                                  ALU.mult).then_inc(st.sem, 1)

            PIECES = ((0, 0, 512), (1, 512, 512), (2, 1024, 256))

            def stick_log_sums(m, h):
                it = m * BH + h
                banks = ((2, 3, 4), (1, 5, 0))[h % 2]
                dve.wait_ge(*sb_ln.at(it, "LN"))
                for b, c, n in PIECES:
                    last = dve.scalar_tensor_tensor(out=spl[:, h % 2, c:c + n], in0=bank[banks[b]][:, 0:n], scalar=0.0,
                                                    in1=lsg[:, h % 2, c:c + n], op0=ALU.max, op1=ALU.add)
                last.then_inc(sb_keep.sem, 1)
                dve.wait_ge(*sb_keep.at(it, "SP"))
                for b, c, n in PIECES:
                    last = dve.scalar_tensor_tensor(out=lsg[:, h % 2, c:c + n], in0=bank[banks[b]][:, 0:n], scalar=0.0,
                                                    in1=lsg[:, h % 2, c:c + n], op0=ALU.min, op1=ALU.subtract)
                last.then_inc(sb_keep.sem, 1)
                for c in STICK_AT:
                    last = dve.tensor_tensor(spl[:, h % 2, c:c + P], spl[:, h % 2, c:c + P],
                                             cst[:, C_KEEP:C_KEEP + P], ALU.mult)
                last.then_inc(sb_keep.sem, 1)

            def hybrid(m):
                q0 = SECOND + m * LAYER2
                n = FINAL + 1 + m
                norm_chain(n, 1)
                dve.wait_ge(panel_done, q0 + BT_TM + KD // 2)
                for t in range(TT):
                    dve.tensor_scalar(vtm[:, t, :], bank[4 + t][:, 0:TM_COLS], rstd_col[:, t:t + 1], None, ALU.mult)\
                       .then_inc(pj.sem, 1)
                dve.wait_ge(*chain.at(n, "RB"))
                for i, (dst, b) in enumerate(((cq[:, 0, :], 2), (cq[:, 1, :], 3), (ckv[:], 0))):
                    dve.wait_ge(panel_done, q0 + BT_CQ + i + 1)
                    scaled(dst, bank[b][:], pj)
                dve.wait_ge(*lat_act.at(m, "S1"))
                dve.tensor_tensor(qsq[:, 0, :], qsq[:, 0, :], qsq[:, 1, :], ALU.add).then_inc(lat.sem, 1)
                for i, (dst, b) in enumerate(((ak[:], 1), (aq[:, 0, :], 2), (aq[:, 1, :], 3))):
                    dve.wait_ge(panel_done, q0 + BT_AK + i + 1)
                    scaled(dst, bank[b][:], pj)
                dve.wait_ge(*lat_act.at(m, "DK"))
                dve.reciprocal(qin[:], qin[:]).then_inc(lat.sem, 1)
                dve.reciprocal(kin[:], kin[:]).then_inc(lat.sem, 1)
                for i, (src, g, inv, high, low) in enumerate((
                        (cq[:, 0, :], m * 2 + V_QN, qin, cqh[:, 0, :], cql[:, 0, :]),
                        (cq[:, 1, :], m * 2 + V_QN + 1, qin, cqh[:, 1, :], cql[:, 1, :]),
                        (ckv[:], m + V_KVN, kin, ckh[:], ckl[:]))):
                    dve.wait_ge(*lat.at(m, ("IK", "L0", "L1")[i]))
                    dve.scalar_tensor_tensor(out=cn[:], in0=src, scalar=vecs[:, bass.ds(g, 1)], in1=inv[:],
                                             op0=ALU.mult, op1=ALU.mult).then_inc(lat.sem, 1)
                    dve.wait_ge(*lat_act.at(m, ("H0", "H1", "HK")[i]))
                    dve.tensor_tensor(low, cn[:], high.bitcast(F32), ALU.subtract).then_inc(lat.sem, 1)
                for i, (dst, b) in enumerate(((dq, 0), (dq, 1), (dk, 2), (dk, 3))):
                    dve.wait_ge(panel_done, q0 + BT_DQ + i + 1)
                    if dst is dq:
                        dve.scalar_tensor_tensor(out=dq[:, i, :], in0=bank[b][:], scalar=BDH ** -0.5, in1=rstd[:],
                                                 op0=ALU.mult, op1=ALU.mult).then_inc(pj.sem, 1)
                    else:
                        scaled(dk[:, i - 2, :], bank[b][:], pj)
                R = slice(64, 112)
                dve.memset(msw[R, :], 0.0).then_inc(mla.sem, 1)
                for h in range(MH):
                    dve.wait_ge(*mla_act.at(m, f"W{h}"))
                    if h:
                        dve.wait_ge(*mla.at(m, f"R{h - 1}"))
                    dve.tensor_tensor(t1[R, :], bank[4 + h][R, :], cos2[R, :], ALU.mult).then_inc(mla.sem, 1)
                    dve.tensor_tensor(t2[R, :], msw[R, :], sin2[R, :], ALU.mult).then_inc(mla.sem, 1)
                    dve.wait_ge(*mla.at(m, f"S{h}"))
                    dve.tensor_tensor(mq[R, h, :], t1[R, :], t2[R, :], ALU.add).then_inc(mla.sem, 1)
                dve.wait_ge(panel_done, q0 + BT_UKV + 1)
                for i in range(2):
                    dve.tensor_copy(vm[:, 2 * i:2 * i + 2, :], bank[4 + i][:].rearrange("p (t c) -> p t c", t=2))\
                       .then_inc(kv.sem, 1)
                dve.tensor_tensor(krs[0:KR_W, :], bank[6][0:KR_W, :], rstd[0:KR_W, :], ALU.mult).then_inc(kv.sem, 1)
                dve.wait_ge(*kv_act.at(m, "Y1"))
                dve.wait_ge(*mla.at(m, f"R{MH - 1}"))
                dve.tensor_tensor(t1[R, :], kx[R, :], cos2[R, :], ALU.mult).then_inc(kv.sem, 1)
                dve.tensor_tensor(t2[R, :], msw[R, :], sin2[R, :], ALU.mult).then_inc(kv.sem, 1)
                dve.wait_ge(*kv.at(m, "KM"))
                dve.tensor_tensor(mk[R, 0, :], t1[R, :], t2[R, :], ALU.add).then_inc(kv.sem, 1)
                for i in range(2):
                    it = m * 2 + i
                    banks = (0, 1, 2) if i == 0 else (5, 6, 7)
                    at = q0 + BT_CONV + 3 * i
                    if i:
                        dve.wait_ge(*conv.at(it - 1, "Y"))
                    else:
                        dve.memset(cu[:, 0:CONV_K - 1], 0.0)
                    dve.wait_ge(panel_done, at + 1)
                    scaled(cgs[:], bank[banks[0]][:], conv)
                    dve.wait_ge(panel_done, at + 2)
                    scaled(cxs[:], bank[banks[1]][:], conv)
                    dve.wait_ge(*conv.at(it, "X"))
                    dve.tensor_tensor(cu[:, CONV_K - 1:], cgs[:], cxs[:], ALU.mult).then_inc(conv.sem, 1)
                    dve.wait_ge(*conv.at(it, "U"))
                    w = m * 6 + V_CW + 3 * i
                    dve.tensor_scalar(cy[:], cu[:, 0:S], vecs[:, bass.ds(w, 1)], vecs[:, bass.ds(m * 2 + V_CB + i, 1)],
                                      ALU.mult, ALU.add).then_inc(conv.sem, 1)
                    for j, name in ((1, "A"), (2, "B")):
                        dve.wait_ge(*conv.at(it, name))
                        dve.scalar_tensor_tensor(out=cy[:], in0=cu[:, j:j + S], scalar=vecs[:, bass.ds(w + j, 1)],
                                                 in1=cy[:], op0=ALU.mult, op1=ALU.add).then_inc(conv.sem, 1)
                    dve.wait_ge(panel_done, at + 3)
                    scaled(cgs[:], bank[banks[2]][:], conv)
                    dve.wait_ge(*conv.at(it, "G"))
                    dve.tensor_tensor(y_conv[:, i, :], cgs[:], cy[:], ALU.mult).then_inc(conv.sem, 1)
                mla_max(m, 0)
                for h in range(MH):
                    it = m * MH + h
                    if h < MH - 1:
                        mla_max(m, h + 1)
                    else:
                        swa_max(m, 0)
                    dve.wait_ge(*mla_pe.at(it, "T1"))
                    dve.tensor_copy(prt[:, 0:P], bank[7][:, 0:P])
                    dve.tensor_copy(prt[:, 3 * P:6 * P], bank[7][:, P:4 * P]).then_inc(mla_dve.sem, 1)
                    dve.reciprocal(sinv[:, h % 2, :], ssum[:, h % 2, :]).then_inc(mla_dve.sem, 1)
                    dve.wait_ge(*mla_dve.at(it, "R"))
                    dve.wait_ge(*mla_pe.at(it, "V"))
                    normalised(y_mla, h, 3 + 2 * (h % 2), mla_dve)
                for h in range(SWH):
                    it = m * SWH + h
                    if h < SWH - 1:
                        swa_max(m, h + 1)
                    dve.wait_ge(*swa_pe.at(it, "T1"))
                    dve.tensor_copy(prt[:, P:4 * P], bank[7][:, 0:3 * P]).then_inc(swa_dve.sem, 1)
                    dve.wait_ge(*swa_ex.at(it, "K"))
                    dve.tensor_tensor(ssum[:, h % 2, :], ssum[:, h % 2, :], esk[:, h % 2, :], ALU.add).then_inc(swa_dve.sem, 1)
                    dve.wait_ge(*swa_dve.at(it, "Q"))
                    dve.reciprocal(sinv[:, h % 2, :], ssum[:, h % 2, :]).then_inc(swa_dve.sem, 1)
                    dve.wait_ge(*swa_dve.at(it, "R"))
                    dve.wait_ge(*swa_pe.at(it, "V"))
                    normalised(y_swa, h, 3 + 2 * (h % 2), swa_dve)
                stick_log_sums(m, 0)
                for h in range(BH):
                    it = m * BH + h
                    banks = ((2, 3, 4), (1, 5, 0))[h % 2]
                    if h < BH - 1:
                        stick_log_sums(m, h + 1)
                    dve.wait_ge(*sb_pe.at(it, "A"))
                    for b, c, n_ in PIECES:
                        last = dve.tensor_tensor(lsg[:, h % 2, c:c + n_], lsg[:, h % 2, c:c + n_],
                                                 bank[banks[b]][:, 0:n_], ALU.add)
                    last.then_inc(sb_dve.sem, 1)
                dve.wait_ge(*gn_act.at(m, "Q1"))
                dve.tensor_tensor(bsq[:, 0, :], bsq[:, 0, :], bsq[:, 1, :], ALU.add).then_inc(gn.sem, 1)
                for i, y in enumerate((y_swa, y_mla, y_sb)):
                    dve.wait_ge(*gn_act.at(m, f"D{i}"))
                    dve.reciprocal(ginv[:, i, :], gstd[:, i, :]).then_inc(gn.sem, 1)
                    dve.wait_ge(*gn.at(m, f"I{i}"))
                    dve.tensor_tensor(y[:], y[:], ginv[:, i, :].rearrange("p (t c) -> p t c", c=1)
                                      .to_broadcast([P, TT, GROUP]), ALU.mult).then_inc(gn.sem, 1)

                def gained(i, d, src):
                    dve.tensor_scalar(yt[:, d, :], src, vecs[:, bass.ds(m * KD + V_GRP + d, 1)], None, ALU.mult)\
                       .then_inc(gn.sem, 1)

                for i, d in ((0, 0), (1, 4)):
                    dve.wait_ge(*gn_pe.at(m, f"T{i}"))
                    for c in range(2):
                        gained(i, d + c, bank[2 + 2 * i + c][:])
                dve.reciprocal(binv[:], bstd[:]).then_inc(gn.sem, 1)
                dve.wait_ge(*gn.at(m, "IB"))
                for c in range(2):
                    dve.scalar_tensor_tensor(out=yt[:, 2 + c, :], in0=y_conv[:, c, :],
                                             scalar=vecs[:, bass.ds(m * KD + V_GRP + 2 + c, 1)], in1=binv[:],
                                             op0=ALU.mult, op1=ALU.mult).then_inc(gn.sem, 1)
                dve.wait_ge(*gn_pe.at(m, "T2"))
                for c in range(2):
                    gained(2, 6 + c, bank[6 + c][:])
                dve.wait_ge(*gn.at(m, "D1"))
                for d in range(KD):
                    it = m * KD + d
                    dve.wait_ge(panel_done, q0 + BT_GATE + d + 1)
                    scaled(gt[:], bank[(d + 1) % 2][:], gate)
                    dve.wait_ge(*gate_act.at(it, "S"))
                    dve.tensor_tensor(yg[:], yt[:, d, :], gs[:], ALU.mult).then_inc(gate.sem, 1)
                    dve.wait_ge(*gate_act.at(it, "H"))
                    dve.tensor_tensor(ygl[:, d, :], yg[:], ygh[:, d, :].bitcast(F32), ALU.subtract)\
                       .then_inc(gate.sem, 1)
                for d in range(KD):
                    dve.wait_ge(*z_act.at(m * KD + d, "Q"))
                    if d == 0:
                        dve.tensor_copy(ssq[:], sq[:]).then_inc(z_sum.sem, 1)
                    else:
                        dve.wait_ge(*z_sum.at(m * KD + d - 1, "A"))
                        dve.tensor_tensor(ssq[:], ssq[:], sq[:], ALU.add).then_inc(z_sum.sem, 1)
                dve.wait_ge(*post_sd.at(m, "SD"))
                dve.reciprocal(rstd_col[:], std_col[:]).then_inc(post.sem, 1)
                dve.wait_ge(*post.at(m, "RC"))
                for t in range(TT):
                    last = dve.tensor_scalar(diag[:, t * P:(t + 1) * P], ident, rstd_col[:, t:t + 1], None, ALU.mult)
                last.then_inc(post.sem, 1)
                dve.wait_ge(*post_pe.at(m, "BC"))
                dve.tensor_copy(rstd[:], bank[5][:]).then_inc(post.sem, 1)
                dve.wait_ge(*post.at(m, "RB"))
                for d in range(KD):
                    dve.scalar_tensor_tensor(out=z[:, d, :], in0=z[:, d, :],
                                             scalar=vecs[:, bass.ds(m * KD + V_POST + d, 1)], in1=rstd[:],
                                             op0=ALU.mult, op1=ALU.mult).then_inc(post.sem, 1)
                    dve.wait_ge(*post.at(m, f"Z{d}"))
                    dve.tensor_tensor(x[:, d, :], x[:, d, :], z[:, d, :], ALU.add).then_inc(prep.sem, 1)
                    prepare(n + 1, d, n + 1)
                    add_squares(n + 1, d, d == 0)

            dve.memset(eps[:], EPS).then_inc(memsets, 1)
            dve.memset(start_d[:], 0.0).then_inc(rg.sem, 1)
            dve.wait_ge(loaded, 64)
            for d in range(KD):
                dve.tensor_copy(x[:, d, :], x0[:, d, :]).then_inc(prep.sem, 1)
                prepare(0, d, 0)
                add_squares(0, d, d == 0)
            dve.tensor_copy(ident16[:], ident).then_inc(mask_set, 1)
            dve.tensor_copy(masks[:], cst[:, C_CAUSAL:C_KEEP]).then_inc(mask_set, 1)
            angles()
            with dve.Fori(0, DEPTH) as l:
                p0 = l * LAYER1
                ffn_in(l * 2, l * 3, p0)
                n = l * 3 + 1
                ffn_out(l * 2, n, p0 + FFN_IN)
                dve.wait_ge(tab_in, l * 48 + 48)
                dve.tensor_copy(ffh[:], ffraw[:]).then_inc(ffs.sem, 1)
                dve.wait_ge(*ffs.at(l, "H"))
                dve.tensor_tensor(ffl[:], ffraw[:], ffh[:].bitcast(F32), ALU.subtract).then_inc(ffs.sem, 1)
                norm_chain(n, 1)
                for dst, at, banks in ((v_ret, AT_RV, (4, 5, 6, 7)), (v_fox, AT_FV, (0, 1, 2, 3))):
                    dve.wait_ge(panel_done, p0 + at + KD // 2)
                    for t in range(TT):
                        dve.tensor_scalar(dst[:, t, :], bank[banks[t]][:], rstd_col[:, t:t + 1], None, ALU.mult)\
                           .then_inc(tm.sem, 1)
                dve.wait_ge(*ffs_pe.at(l, "FF"))
                dve.wait_ge(*chain.at(n, "RB"))
                dve.tensor_tensor(fz[0:FF_W], bank[4][0:FF_W, :], rstd[0:FF_W, :], ALU.mult).then_inc(ffs.sem, 1)
                dve.wait_ge(*ffs.at(l, "Z"))
                dve.tensor_scalar(fz[0:FF_W], fz[0:FF_W], vecs[0:FF_W, bass.ds(l + V_BF, 1)], None, ALU.add)\
                   .then_inc(ffs.sem, 1)
                dve.wait_ge(*ffs_act.at(l, "LN"))
                dve.scalar_tensor_tensor(out=fz[0:FF_W], in0=fz[0:FF_W], scalar=0.0, in1=fa[0:FF_W],
                                         op0=ALU.min, op1=ALU.subtract).then_inc(ffs.sem, 1)
                dve.wait_ge(*ffs.at(l, "LF"))
                dve.tensor_tensor_scan(cum[0:FF_W, :], ones[0:FF_W, 0:1].to_broadcast([FF_W, S]), fz[0:FF_W], 0.0,
                                       ALU.mult, ALU.add).then_inc(ffs.sem, 1)
                dve.wait_ge(*ffs.at(l, "C"))
                for e, rows in enumerate((slice(FDH, P), slice(0, FDH))):
                    dve.memset(fq[rows, e, :], -FDH ** 0.5).then_inc(fx_set, 1)
                    dve.memset(fk[rows, e, :], 0.0).then_inc(fx_set, 1)
                with dve.Fori(0, RH // 2) as i:
                    for q in range(2):
                        dve.wait_ge(panel_done, p0 + AT_RG + i * 2 + q + 1)
                        dve.wait_ge(*rg_act.before(l * RH + i * 2 + q))
                        scaled(tg[:], bank[q][:], rg)
                retention(l, p0 + AT_RET)
                forgetting(l, p0 + AT_FOX)
                merge(l, p0 + AT_MERGE)
                n2 = l * 3 + 2
                for d in range(KD):
                    dve.wait_ge(panel_done, p0 + AT_WOUT + d + 1)
                    dve.tensor_tensor(x[:, d, :], bank[2 + 3 * (d % 2)][:], x[:, d, :], ALU.add).then_inc(prep.sem, 1)
                    prepare(n2, d, n2)
                    add_squares(n2, d, d == 0)
                ffn_in(l * 2 + 1, n2, p0 + AT_FFN2)
                ffn_out(l * 2 + 1, l * 3 + 3, p0 + AT_FFN2 + FFN_IN)
            norm_chain(FINAL, 5)
            dve.wait_ge(*chain.at(FINAL, "RB"))
            for d in range(KD):
                dve.scalar_tensor_tensor(out=x[:, d, :], in0=x[:, d, :],
                                         scalar=vecs[:, FINAL * KD + d:FINAL * KD + d + 1],
                                         in1=rstd[:], op0=ALU.mult, op1=ALU.mult).then_inc(prep.sem, 1)
                prepare(FINAL + 1, d, FINAL + 1)
                add_squares(FINAL + 1, d, d == 0)
            with dve.Fori(0, DEPTH) as m:
                hybrid(m)


def table_of_constants():
    c = np.zeros((P, N_CONST), np.float32)
    i, j = np.arange(P)[:, None], np.arange(P)[None, :]
    c[:, C_ID:C_ID + P] = i == j
    c[:, C_ONE:C_ONE + P] = 1
    c[:, C_NONE:C_NONE + P] = -1
    c[:, C_NTRI:C_NTRI + P] = -1.0 * (i > j)
    c[:, C_CAUSAL:C_CAUSAL + P] = np.where(j <= i, 0, NEG)
    c[:, C_SWA:C_SWA + P] = np.where(j > i, 0, NEG)
    c[:, C_SWA + P:C_SWA + 2 * P] = np.where(j <= i, 0, NEG)
    c[:, C_SWA0:C_SWA0 + P] = NEG
    c[:, C_SWA0 + P:C_SWA0 + 2 * P] = np.where(j <= i, 0, NEG)
    c[:, C_STRICT:C_STRICT + P] = np.where(j > i, 0, NEG)
    c[:, C_KEEP:C_KEEP + P] = j > i
    half = M_ROPE // 2
    freqs = np.float32(10000.0) ** (-np.arange(half, dtype=np.float32) / np.float32(half))
    c[64:64 + half, C_FREQ] = freqs
    c[96:96 + half, C_FREQ] = freqs
    c[0:FH, C_HOT:C_HOT + FH] = c[FDH:FF_W, C_HOT:C_HOT + FH] = np.eye(FH)
    return c


def decay_table():
    gamma = 1 - 2.0 ** (-5 - np.arange(RH))
    gap = np.arange(S)[None, :] - np.arange(P)[:, None]
    t = np.where(gap[:, None, :] >= 0, gamma[None, :, None] ** np.maximum(gap, 0)[:, None, :], 0) * RDK ** -0.5
    return t.astype(np.float32)


def rope_table():
    half = RDK // 2
    inv = np.float32(10000.0) ** (-np.arange(0, RDK, 2, dtype=np.float32) / np.float32(RDK))
    ang = (np.arange(S, dtype=np.float32)[None, :] * inv[:, None]).astype(np.float64)
    t = np.zeros((P, 2, S))
    t[0:half, 0] = t[half:, 0] = np.cos(ang)
    t[0:half, 1], t[half:, 1] = -np.sin(ang), np.sin(ang)
    return t.astype(np.float32)


def col_panels(w):
    k, n = w.shape
    return w.reshape(KD, P, n // P, P).transpose(2, 1, 0, 3).reshape(n // P, P, PANEL)


def tok_panels(w):
    return w.reshape(KD // 2, 2, P, S).transpose(0, 2, 1, 3).reshape(KD // 2, P, PANEL)


def ffn_panels(w_in, w_out):
    a, b = col_panels(w_in[:, :F]), col_panels(w_in[:, F:])
    both = np.stack([a, b], 1).reshape(2 * KF, P, PANEL)
    whole = w_out[:KT_MAJOR * P].reshape(KT_MAJOR, P, PANEL)
    rest = w_out[KT_MAJOR * P:].reshape(KF - KT_MAJOR, P, KD, P).transpose(2, 0, 1, 3)
    rest = rest.reshape(-1, UNITS, P, P).transpose(0, 2, 1, 3).reshape(-1, P, PANEL)
    return [both, whole, rest]


def first_layer(a, l):
    w = a["w_in"][l]
    rq, rk, rv, rgw, fq, fk, fv = (w[:, i * 512:(i + 1) * 512] for i in range(7))
    gr, gf = w[:, 3592:4616], w[:, 4616:5640]
    crq, crk, cgr, cfq, cfk = map(col_panels, (rq, rk, gr, fq, fk))
    ret = np.stack([crq, crk, cgr[0::2], cgr[1::2]], 1).reshape(-1, P, PANEL)
    fox = np.stack([cfq, cfk], 1).reshape(-1, P, PANEL)
    wo = np.concatenate([a["w_o_ret"][l].reshape(RH, P, KD, P), a["w_o_fox"][l].reshape(FH // 2, P, KD, P)])
    wo = wo.transpose(2, 1, 0, 3).reshape(KD, P, PANEL)
    mrg = np.stack([col_panels(gf), wo], 1).reshape(-1, P, PANEL)
    mrg[[1, 2]] = mrg[[2, 1]]
    return [*ffn_panels(a["w_ffn1_in"][l], a["w_ffn1_out"][l]), tok_panels(rv), tok_panels(fv), col_panels(rgw),
            ret, fox, mrg, col_panels(a["w_out"][l]), *ffn_panels(a["w_ffn2_in"][l], a["w_ffn2_out"][l])]


def second_layer(a, l):
    w = a["w_in_2"][l]
    cuts = np.cumsum((256, 128, 128, 256, 256, 256, 256, 128, 32, 256, 256, 256))
    a_q, a_k, a_v, b_b, b_c, b_x, c_q, c_kv, c_kr, d_q, d_k, d_v, gate_w = np.split(w, cuts, axis=1)
    tokens = np.concatenate([a_v, d_v, np.zeros((D, S - TM_COLS), np.float32)], 1)
    a_q = a_q.reshape(D, SWH, SDH)[:, [0, 2, 1, 3]].reshape(D, SWH * SDH)
    half = M_ROPE // 2

    def spread(rope):
        gap = np.zeros((*rope.shape[:-1], half), np.float32)
        return np.concatenate([rope[..., :half], gap, rope[..., half:]], -1)

    uq = a["mla_w_uq_2"][l].reshape(2, P, MH, M_NOPE + M_ROPE)
    uq = np.concatenate([uq[..., :M_NOPE], spread(uq[..., M_NOPE:]), np.zeros((2, P, MH, P - MLA_K), np.float32)], -1)
    uq = uq.transpose(1, 2, 0, 3).reshape(1, P, PANEL)
    ukv = a["mla_w_ukv_2"][l].reshape(KVR, MH, M_NOPE + M_V)
    k_rope = spread(c_kr).reshape(KD, P, KR_W).transpose(1, 0, 2).reshape(P, KD * KR_W)
    up = np.concatenate([ukv[..., :M_NOPE].reshape(P, -1), ukv[..., M_NOPE:].reshape(P, -1), k_rope,
                         np.zeros((P, PANEL - KR_AT - KD * KR_W), np.float32)], 1)[None]
    conv = np.stack([col_panels(b_c), col_panels(b_x), col_panels(b_b)], 1).reshape(-1, P, PANEL)
    return [tok_panels(tokens), col_panels(c_q), col_panels(c_kv), col_panels(a_k), col_panels(a_q), col_panels(d_q),
            col_panels(d_k), uq, up, conv, col_panels(gate_w), col_panels(a["w_out_2"][l])]


def columns(v):
    return v.reshape(-1, P).T


def kernel(**inputs):
    import concourse.bacc as bacc
    from concourse.bass_utils import run_bass_kernel_spmd

    a = {k: np.asarray(v) for k, v in inputs.items()}
    panels = [p for l in range(DEPTH) for p in first_layer(a, l)]
    panels += [p for l in range(DEPTH) for p in second_layer(a, l)]
    stream = np.concatenate(panels)
    assert len(stream) == N_PANELS
    vec = np.zeros((P, N_VEC), np.float32)
    norms = [a[k][l] for l in range(DEPTH) for k in ("norm_ffn1", "norm_mix", "norm_ffn2")]
    norms += [a["norm_final"], a["norm_pre_2"][0], a["norm_pre_2"][1]]
    for i, g in enumerate(norms):
        vec[:, i * KD:(i + 1) * KD] = columns(g)
    vec[:, V_RET:V_RET + DEPTH * RH] = columns(a["ret_norm"])
    vec[:, V_GRP:V_GRP + DEPTH * KD] = columns(a["group_norm_2"])
    vec[:, V_POST:V_POST + DEPTH * KD] = columns(a["norm_post_2"])
    vec[:, V_QN:V_QN + DEPTH * 2] = columns(a["mla_q_norm_2"])
    vec[:, V_KVN:V_KVN + DEPTH] = columns(a["mla_kv_norm_2"])
    vec[:, V_CW:V_CW + DEPTH * 6] = a["conv_w_2"].reshape(DEPTH, CONV_K, 2, P).transpose(3, 0, 2, 1).reshape(P, -1)
    vec[:, V_CB:V_CB + DEPTH * 2] = columns(a["conv_b_2"])
    vec[:, V_SINK:V_SINK + DEPTH * SWH] = a["attn_sinks_2"].reshape(1, -1)
    vec[0:FH, V_BF:V_BF + DEPTH] = vec[FDH:FF_W, V_BF:V_BF + DEPTH] = a["b_forget"].T
    w_ff = a["w_in"][:, :, 3584:3592].reshape(DEPTH, KD, P, FH).transpose(0, 2, 1, 3)
    ff = np.zeros((DEPTH, P, FF_COLS), np.float32)
    by_tile = ff[:, :, :KD * FF_W].reshape(DEPTH, P, KD, FF_W)
    by_tile[..., 0:FH] = by_tile[..., FDH:] = w_ff
    arrays = {
        "stream": stream,
        "x_t": np.ascontiguousarray(a["x"][0].T.reshape(KD, P, S).transpose(1, 0, 2)),
        "vec": vec, "const": table_of_constants(), "decay": decay_table(), "rope": rope_table(),
        "ff_w": ff,
        "pos": np.ascontiguousarray(np.broadcast_to(a["positions_2"][0].astype(np.int32), (P, S))),
    }
    nc = bacc.Bacc("TRN2", target_bir_lowering=False, num_devices=1)
    args = [nc.dram_tensor(k, v.shape, mybir.dt.from_np(v.dtype), kind="ExternalInput").ap() for k, v in arrays.items()]
    out = nc.dram_tensor("out", [KD, P, S], F32, kind="ExternalOutput").ap()
    build(nc, *args, out)
    r = run_bass_kernel_spmd(nc, [arrays], core_ids=[0])
    return r.results[0]["out"].reshape(D, S).T[None].copy()
```

```python
from contextlib import ExitStack

import numpy as np
import concourse.bass as bass
import concourse.mybir as mybir

F32 = mybir.dt.float32
F32R = mybir.dt.float32r
I32 = mybir.dt.int32
BF16 = mybir.dt.bfloat16
ALU = mybir.AluOpType
ACT = mybir.ActivationFunctionType
AX_X = mybir.AxisListType.X

P = 128
D, S, DEPTH, F = 1024, 512, 2, 2816
KD = D // P
TT = S // P
KF = F // P
RH, RDK = 4, 128
FH, FDH = 8, 64
FF_W = FDH + FH
FF_COLS = KD * FF_W + P - FF_W
MH, M_NOPE, M_ROPE, M_V, QR, KVR = 4, 64, 32, 64, 256, 128
MLA_K = 112
SWH, SDH = 4, 64
BH, BDH = 4, 64
CONV_W, CONV_K = 256, 3
GROUP = 256
TM_COLS = SDH * 2 + BH * BDH
KR_AT = MH * (M_NOPE + M_V)
KR_W = 48
EPS = 1e-6
NEG = -1e31

UNITS = 8
PANEL = UNITS * P
RAW_SLOTS, SPLIT_SLOTS = 4, 2
X_PARTS = 4
KT_MAJOR = 16

FFN_IN = 2 * KF
FFN_PANELS = FFN_IN + KF
AT_RV = FFN_PANELS
AT_FV = AT_RV + KD // 2
AT_RG = AT_FV + KD // 2
AT_RET = AT_RG + RH
AT_FOX = AT_RET + 4 * RH
AT_MERGE = AT_FOX + FH
AT_WOUT = AT_MERGE + 2 * KD
AT_FFN2 = AT_WOUT + KD
LAYER1 = AT_FFN2 + FFN_PANELS
BT_TM = 0
BT_CQ = BT_TM + KD // 2
BT_CKV = BT_CQ + 2
BT_AK = BT_CKV + 1
BT_AQ = BT_AK + 1
BT_UQ = BT_AQ + 2
BT_DQ = BT_UQ + 1
BT_UKV = BT_DQ + 2
BT_DK = BT_UKV + 1
BT_CONV = BT_DK + 2
BT_GATE = BT_CONV + 6
BT_WOUT = BT_GATE + KD
LAYER2 = BT_WOUT + KD
SECOND = DEPTH * LAYER1
N_PANELS = SECOND + DEPTH * LAYER2
NORMS = 3 * DEPTH + 1 + DEPTH + 1
FINAL = 3 * DEPTH

V_RET = NORMS * KD
V_GRP = V_RET + DEPTH * RH
V_POST = V_GRP + DEPTH * KD
V_QN = V_POST + DEPTH * KD
V_KVN = V_QN + DEPTH * 2
V_CW = V_KVN + DEPTH
V_CB = V_CW + DEPTH * 6
V_BF = V_CB + DEPTH * 2
V_SINK = V_BF + DEPTH
N_VEC = V_SINK + DEPTH * SWH
C_ID, C_ONE, C_NONE, C_NTRI, C_CAUSAL, C_SWA, C_SWA0, C_STRICT, C_KEEP = (
    0, 128, 256, 384, 512, 640, 896, 1152, 1280)
C_FREQ, C_HOT = 1408, 1409
N_CONST = C_HOT + FH


class Steps:

    def __init__(self, sem, *names, started=0):
        self.sem, self.names, self.n, self.started = sem, names, len(names), started

    def at(self, round_, name):
        return self.sem, round_ * self.n + (self.names.index(name) + 1 + self.started)

    def before(self, round_):
        return self.sem, round_ * self.n + self.started


def build(nc, stream, x_in, vec, const, decay, rope, ff_w, pos, out):
    ctx = ExitStack()
    with ctx:
        def sb(name, shape, dt=F32, stack=ctx):
            return stack.enter_context(nc.sbuf_tensor(name, shape, dt))

        def sem(name):
            return ctx.enter_context(nc.semaphore(name))

        bank = [ctx.enter_context(nc.psum_tensor(f"bank{i}", [P, S], F32)) for i in range(8)]

        x = sb("x", [P, KD, S])
        xh = sb("xh", [P, KD, S], F32R)
        xl = sb("xl", [P, KD, S], F32R)
        sq = sb("sq", [P, S])
        ssq = sb("ssq", [P, S])
        diag = sb("diag", [P, S])
        rstd = sb("rstd", [P, S])
        std_col = sb("std_col", [P, TT])
        rstd_col = sb("rstd_col", [P, TT])
        raw = sb("raw", [P, RAW_SLOTS, PANEL])
        wh = sb("wh", [P, SPLIT_SLOTS, PANEL], F32R)
        wl = sb("wl", [P, SPLIT_SLOTS, PANEL], F32R)
        vecs = sb("vecs", [P, N_VEC])
        cst = sb("cst", [P, N_CONST])
        eps = sb("eps", [P, 1])
        one = sb("one", [P, 1])
        start_d = sb("start_d", [P, 1 + KD])
        root = sb("root", [P, 1])
        start_a = sb("start_a", [P, 1])
        cos2 = sb("cos2", [P, S])
        sin2 = sb("sin2", [P, S])
        ident, ones = cst[:, C_ID:C_ID + P], cst[:, C_ONE:C_ONE + P]
        masks = sb("masks", [P, C_KEEP - C_CAUSAL], BF16)
        ident16 = sb("ident16", [P, P], BF16)
        causal = masks[:, 0:P]

        ffn = ExitStack()
        uh = sb("uh", [P, KF, S], F32R, ffn)
        ul = sb("ul", [P, KF, S], F32R, ffn)
        ta = sb("ta", [P, S], F32, ffn)
        tb = sb("tb", [P, S], F32, ffn)
        sa = sb("sa", [P, S], F32, ffn)
        u32 = sb("u32", [P, S], F32, ffn)
        posi = sb("posi", [P, S], I32, ffn)
        ang = sb("ang", [P, S], F32, ffn)
        turn = sb("turn", [P, S], F32, ffn)
        whole = sb("whole", [P, S], F32, ffn)
        ffn.close()
        mix = ExitStack()
        yrh = sb("yrh", [P, RH, S], F32R, mix)
        yrl = sb("yrl", [P, RH, S], F32R, mix)
        yfh = sb("yfh", [P, FH // 2, S], F32R, mix)
        yfl = sb("yfl", [P, FH // 2, S], F32R, mix)
        gate_r = sb("gate_r", [P, KD, S], F32, mix)
        heads = ExitStack()
        dec = sb("dec", [P, RH, S], F32, heads)
        rp = sb("rp", [P, 2, S], F32, heads)
        v_fox = sb("v_fox", [P, TT, S], F32, heads)
        cum = sb("cum", [P, S], F32, heads)
        fq = sb("fq", [P, 2, S], F32, heads)
        fk = sb("fk", [P, 2, S], F32, heads)
        ff_mem = ExitStack()
        ffraw = sb("ffraw", [P, FF_COLS], F32, ff_mem)
        ffh = sb("ffh", [P, FF_COLS], F32R, ff_mem)
        ffl = sb("ffl", [P, FF_COLS], F32R, ff_mem)
        ff_mem.close()
        ret_mem = ExitStack()
        pt = sb("pt", [P, 10 * P], F32, ret_mem)
        kr = sb("kr", [P, S], F32, ret_mem)
        qr = sb("qr", [P, S], F32, ret_mem)
        tq = sb("tq", [P, S], F32, ret_mem)
        tk = sb("tk", [P, S], F32, ret_mem)
        hsum = sb("hsum", [P, TT], F32, ret_mem)
        hstd = sb("hstd", [P, TT], F32, ret_mem)
        hinv = sb("hinv", [P, TT], F32, ret_mem)
        v_ret = sb("v_ret", [P, TT, S], F32, ret_mem)
        rgs = sb("rgs", [P, RH, S], F32, ret_mem)
        ret_mem.close()
        tg = yn = tk
        y32 = tq
        m1, sw = diag, ssq
        fox_mem = ExitStack()
        fp = sb("fp", [P, 2, 10 * P], F32, fox_mem)
        fpt = sb("fpt", [P, 10 * P], F32, fox_mem)
        fo = sb("fo", [P, TT, P], F32, fox_mem)
        fmx = sb("fmx", [P, 2, TT], F32, fox_mem)
        fnm = sb("fnm", [P, 2, TT], F32, fox_mem)
        fsum = sb("fsum", [P, 2, TT], F32, fox_mem)
        finv = sb("finv", [P, 2, TT], F32, fox_mem)
        fox_mem.close()
        fz, fa = fq[:, 0, :], fq[:, 1, :]
        heads.close()
        merge_mem = ExitStack()
        mh = sb("mh", [P, KD, S], F32R, merge_mem)
        ml = sb("ml", [P, KD, S], F32R, merge_mem)
        sr = sb("sr", [P, S], F32, merge_mem)
        sf = sb("sf", [P, S], F32, merge_mem)
        tgf = sb("tgf", [P, S], F32, merge_mem)
        mr = sb("mr", [P, S], F32, merge_mem)
        mf = sb("mf", [P, S], F32, merge_mem)
        mg = sb("mg", [P, S], F32, merge_mem)
        merge_mem.close()
        mix.close()
        hyb = ExitStack()
        y_swa = sb("y_swa", [P, TT, GROUP], F32, hyb)
        y_mla = sb("y_mla", [P, TT, GROUP], F32, hyb)
        y_sb = sb("y_sb", [P, TT, GROUP], F32, hyb)
        y_conv = sb("y_conv", [P, 2, S], F32, hyb)
        qkv_mem = ExitStack()
        vtm = sb("vtm", [P, TT, TM_COLS], F32, qkv_mem)
        aq = sb("aq", [P, 2, S], F32, qkv_mem)
        ak = sb("ak", [P, S], F32, qkv_mem)
        dq = sb("dq", [P, 2, S], F32, qkv_mem)
        dk = sb("dk", [P, 2, S], F32, qkv_mem)
        mq = sb("mq", [P, MH, S], F32, qkv_mem)
        mk = sb("mk", [P, MH, S], F32, qkv_mem)
        vm = sb("vm", [P, TT, MH * M_V], F32, qkv_mem)
        cgs = sb("cgs", [P, S], F32, qkv_mem)
        cxs = sb("cxs", [P, S], F32, qkv_mem)
        cu = sb("cu", [P, CONV_K - 1 + S], F32, qkv_mem)
        cy = sb("cy", [P, S], F32, qkv_mem)
        lat_mem = ExitStack()
        cqh = sb("cqh", [P, 2, S], F32R, lat_mem)
        cql = sb("cql", [P, 2, S], F32R, lat_mem)
        ckh = sb("ckh", [P, S], F32R, lat_mem)
        ckl = sb("ckl", [P, S], F32R, lat_mem)
        cq = sb("cq", [P, 2, S], F32, lat_mem)
        ckv = sb("ckv", [P, S], F32, lat_mem)
        qsq = sb("qsq", [P, 2, S], F32, lat_mem)
        ksq = sb("ksq", [P, S], F32, lat_mem)
        lstd = sb("lstd", [P, 2, TT], F32, lat_mem)
        linv = sb("linv", [P, 2, TT], F32, lat_mem)
        diag_q = sb("diag_q", [P, S], F32, lat_mem)
        diag_k = sb("diag_k", [P, S], F32, lat_mem)
        cn = sb("cn", [P, 2, S], F32, lat_mem)
        t1 = sb("t1", [P, S], F32, lat_mem)
        t2 = sb("t2", [P, S], F32, lat_mem)
        msw = sb("msw", [P, S], F32, lat_mem)
        krs = sb("krs", [P, S], F32, lat_mem)
        kx = sb("kx", [P, S], F32, lat_mem)
        lat_mem.close()
        lsg = sb("lsg", [P, 2, 10 * P], F32, qkv_mem)
        spl = sb("spl", [P, 2, 10 * P], F32, qkv_mem)
        pr, prt = lsg, spl[:, 0, :]
        smx = sb("smx", [P, 2, TT], F32, qkv_mem)
        snm = sb("snm", [P, 2, TT], F32, qkv_mem)
        ssum = sb("ssum", [P, 2, TT], F32, qkv_mem)
        sinv = sb("sinv", [P, 2, TT], F32, qkv_mem)
        esk = sb("esk", [P, 2, TT], F32, qkv_mem)
        gsum = sb("gsum", [P, 4, TT], F32, qkv_mem)
        gates = sb("gates", [P, KD, S], F32, qkv_mem)
        qkv_mem.close()
        out_mem = ExitStack()
        z = sb("z", [P, KD, S], F32, out_mem)
        yg = sb("yg", [P, 2, S], F32, out_mem)
        gstd = sb("gstd", [P, 4, TT], F32, out_mem)
        ginv = sb("ginv", [P, 4, TT], F32, out_mem)
        ygh = sb("ygh", [P, KD, S], F32R, out_mem)
        ygl = sb("ygl", [P, KD, S], F32R, out_mem)
        out_mem.close()
        hyb.close()

        raw_in = [sem(f"raw_in{i}") for i in range(RAW_SLOTS)]
        split_hi, split_lo = sem("split_hi"), sem("split_lo")
        panel_done = sem("panel_done")
        x_part = [sem(f"x_part{i}") for i in range(X_PARTS)]
        vec_in, const_in, pos_in = sem("vec_in"), sem("const_in"), sem("pos_in")
        tab_in = sem("tab_in")
        memsets = sem("memsets")
        one_set = sem("one_set")
        mask_set = sem("mask_set")
        stored = sem("stored")
        resid = Steps(sem("residual_dve"), "X")
        prep = Steps(sem("prep_dve"), "XH", "XL")
        acc = Steps(sem("squares_dve"), "ACC")
        prep_sq = Steps(sem("prep_act"), "SQ")
        hyb_sq = Steps(sem("norm_squares_pe"), "U")
        hyb_act = Steps(sem("norm_operand_act"), "XH", "SQ")
        hyb_xl = Steps(sem("norm_operand_dve"), "XL")
        chain_col_pe = Steps(sem("chain_col_pe"), "COL")
        chain_bc_pe = Steps(sem("chain_bc_pe"), "BC")
        chain_sd = Steps(sem("chain_act"), "SD")
        chain = Steps(sem("chain_dve"), "RC", "DG", "RB")
        fin = Steps(sem("ffn_in_dve"), "A", "B", "U", "UL")
        fin_act = Steps(sem("ffn_in_act"), "SILU", "UH")
        fout = Steps(sem("ffn_out_pe"), *range(KD))
        tm = Steps(sem("tm_dve"), *[f"RV{i}" for i in range(TT)], *[f"FV{i}" for i in range(TT)])
        ffs = Steps(sem("forget_dve"), "H", "L", "Z", "ZB", "LF", "C")
        ffs_pe = Steps(sem("forget_pe"), "FF")
        ffs_act = Steps(sem("forget_act"), "ABS", "EXP", "LN")
        rg = Steps(sem("rg_dve"), "T", started=1)
        rg_act = Steps(sem("rg_act"), "S", started=1)
        ret_sc, ret_pv, ret_tr = (Steps(sem(f"ret_{k}_pe"), "P") for k in ("scores", "values", "turned"))
        ret = Steps(sem("ret_dve"), "Q", "QC", "QS", "QR", "K", "KC", "KS", "KR", "G0", "P0", "P1", "P2", "P3", "G1")
        ret_n = Steps(sem("ret_norm_dve"), "RC", "N0", "N1", "N2", "N3")
        ret_y = Steps(sem("ret_out_dve"), "Y", "YL")
        ret_sw = Steps(sem("ret_swap_act"), "Q0", "Q1", "K0", "K1")
        ret_sq = Steps(sem("ret_norm_act"), "S0", "S1", "S2", "S3", "SD")
        ret_h = Steps(sem("ret_out_act"), "YH")
        fx_set = sem("fox_set_dve")
        fx_s, fx_v = ([Steps(sem(f"fox_{k}_{e}_pe"), "P") for e in "ab"] for k in ("scores", "values"))
        fx_t = [Steps(sem(f"fox_turned_{e}_pe"), "T0", "T1", "T2") for e in "ab"]
        fx_y = Steps(sem("fox_out_pe"), "TR")
        fx_q = Steps(sem("fox_qk_dve"), "CA", "CB", "QA", "QB", "KA", "KB")
        fx_m = [Steps(sem(f"fox_max_{e}_dve"), "M", "N") for e in "ab"]
        fx_o = [Steps(sem(f"fox_values_{e}_dve"), "E", "R", "O") for e in "ab"]
        fx_l = Steps(sem("fox_out_dve"), "YL")
        fx_x = [Steps(sem(f"fox_exp_{e}_act"), "X") for e in "ab"]
        fx_c = [Steps(sem(f"fox_turned_{e}_act"), "E0", "E2") for e in "ab"]
        fx_h = Steps(sem("fox_out_act"), "YH")
        mrg_d = Steps(sem("merge_dve"), "G", "R", "F", "M", "L")
        mrg_a = Steps(sem("merge_act"), "SR", "SF", "MH")

        trig = Steps(sem("trig_dve"), "F", "A", *[f"{w}{i}" for w in "sc" for i in range(7)])
        trig_act = Steps(sem("trig_act"), "SIN0", "SIN1", "COS")
        pj = Steps(sem("proj_dve"), "T0", "T1", "T2", "T3", "Q0", "Q1", "KV", "AK", "A0", "A1", "D0", "D1", "E0", "E1")
        lat_pe = Steps(sem("latent_pe"), "COL", "BC")
        lat = Steps(sem("latent_dve"), "SUM", "I", "GQ", "GK", "N0", "N1", "L0", "NK", "L1", "LK")
        lat_act = Steps(sem("latent_act"), "S0", "S1", "SK", "DQ", "DK", "H0", "H1", "HK")
        mla = Steps(sem("mla_q_dve"), "Z", *[f"{w}{h}" for h in range(MH) for w in "CSR"])
        mla_act = Steps(sem("mla_q_act"), *[f"{w}{h}" for h in range(MH) for w in "PVW"])
        kv = Steps(sem("mla_kv_dve"), "V0", "V1", "KS", "KC", "KM", "KR")
        kv_act = Steps(sem("mla_kv_act"), "N0", "N1", "N2", "N3", "X", "Y0", "Y1", "C1", "C2", "C3")
        conv = Steps(sem("conv_dve"), "C", "X", "U", "A", "B", "D", "G", "Y")
        mla_sc = Steps(sem("mla_scores_pe"), "SC")
        mla_mx = Steps(sem("mla_max_dve"), "M", "N")
        mla_ex = Steps(sem("mla_exp_act"), "X")
        mla_pe = Steps(sem("mla_values_pe"), "T0", "T1", "T2", "V")
        mla_dve = Steps(sem("mla_values_dve"), "E", "R", "O")
        mla_ev = Steps(sem("mla_values_act"), "E0", "E2")
        swa_sc = Steps(sem("swa_scores_pe"), "SC")
        swa_mx = Steps(sem("swa_max_dve"), "M", "S", "N")
        swa_ex = Steps(sem("swa_exp_act"), "X", "K")
        swa_pe = Steps(sem("swa_values_pe"), "T0", "T1", "V")
        swa_dve = Steps(sem("swa_values_dve"), "E", "Q", "R", "O")
        swa_ev = Steps(sem("swa_values_act"), "E0")
        sb_sc = Steps(sem("stick_scores_pe"), "Z")
        sb_ln = Steps(sem("stick_log_act"), "AB", "EX", "LN")
        sb_keep = Steps(sem("stick_log_dve"), "SP", "LS", "K")
        sb_pe = Steps(sem("stick_values_pe"), "A", "V")
        sb_dve = Steps(sem("stick_values_dve"), "T")
        sb_act = Steps(sem("stick_values_act"), "P", "O")
        gn_pe = Steps(sem("group_pe"), "COL", "T0", "T1", "T2", "BC")
        gn = Steps(sem("group_dve"), "SUM", "I0", "C", "N0", "N1", "I1", "N2", "DG", "B0", "B1")
        gn_act = Steps(sem("group_act"), "S1", "Q0", "Q1", "S0", "D0", "S2", "D1")
        gate_in = Steps(sem("gate_in_dve"), "G")
        gate_s = Steps(sem("gate_silu_act"), "S")
        gate_y = Steps(sem("gated_dve"), "Y")
        gate_h = Steps(sem("gated_hi_act"), "H")
        gate_l = Steps(sem("gated_lo_dve"), "L")
        z_act = Steps(sem("z_act"), "Q", "Z")
        sqrt_set = sem("sqrt_set_act")
        z_sum = Steps(sem("z_dve"), "A")
        post_pe = Steps(sem("post_pe"), "COL", "BC")
        post_sd = Steps(sem("post_act"), "SD")
        post = Steps(sem("post_dve"), "RC", "DG", *[f"Z{d}" for d in range(KD)])

        HEAD_AT = ((2, 0), (3, 0), (2, 128), (4, 0))
        HEAD_OUT = 2 * P
        FIRST_BLOCK = (0, 1, 3, 6)
        STICK_AT = (0, 512, 1024, 896)

        SWA_BANKS = (2, 3)
        STICK = ((0, 0), (1, 0), (2, 0), (1, 384))
        STICK_BANKS = ((2, 3, 4), (1, 5, 0))
        PIECES = ((0, 0, 512), (1, 512, 512), (2, 1024, 256))
        FILL_BANK = (0, 1, 0, 1, 0, 1, 0, 1, 7, 7, 7, 7, 7, 2)
        CONV_TILES = 3 * (CONV_W // P)
        READY = (0, 1, 4, 5, 6, 7, 2, 3)
        AHEAD = 1
        GROUP_BANKS = ((3, 4), (0, 1), (5, 6))
        OUT_BANKS = (7, 2)

        OFF = (0, 512, 896, 1152)

        block = ctx.enter_context(nc.Block())

        @block.sync
        def _(sp):
            sp.dma_start(raw[:, 0, :], stream[0]).then_inc(raw_in[0], 16)
            sp.dma_start(vecs[:], vec).then_inc(vec_in, 16)
            for i in range(X_PARTS):
                d = slice(i * KD // X_PARTS, (i + 1) * KD // X_PARTS)
                sp.dma_start(x[:, d, :], x_in[:, d, :]).then_inc(x_part[i], 16)
                if i == 1:
                    sp.dma_start(raw[:, 1, :], stream[1]).then_inc(raw_in[1], 16)
            sp.dma_start(cst[:], const).then_inc(const_in, 16)
            for n in range(2, RAW_SLOTS):
                sp.dma_start(raw[:, n, :], stream[n]).then_inc(raw_in[n], 16)
            sp.dma_start(posi[:], pos).then_inc(pos_in, 16)
            with sp.Fori(1, N_PANELS // RAW_SLOTS) as g:
                for n in range(RAW_SLOTS):
                    sp.wait_ge(split_lo, g * RAW_SLOTS + (n + 1 - RAW_SLOTS))
                    sp.dma_start(raw[:, n, :], stream[g * RAW_SLOTS + n]).then_inc(raw_in[n], 16)
            for d in range(KD):
                sp.wait_ge(*resid.at((NORMS - 1) * KD + d, "X"))
                sp.dma_start(out[d], x[:, d, :]).then_inc(stored, 16)
            sp.wait_ge(stored, 16 * KD)

        @block.gpsimd
        def _(pool):
            def split(n, g, first=False):
                slot = n % SPLIT_SLOTS
                pool.wait_ge(raw_in[n], 16 * (g + 1))
                if not (first and n < SPLIT_SLOTS):
                    pool.wait_ge(panel_done, g * RAW_SLOTS + (n + 1 - SPLIT_SLOTS))
                pool.tensor_tensor(wh[:, slot, :], raw[:, n, :], one[:].to_broadcast([P, PANEL]), ALU.mult)\
                    .then_inc(split_hi, 1)
                pool.wait_ge(split_hi, g * RAW_SLOTS + (n + 1))
                pool.tensor_tensor(wl[:, slot, :], raw[:, n, :], wh[:, slot, :].bitcast(F32),
                                   ALU.subtract).then_inc(split_lo, 1)

            pool.memset(one[:], 1.0).then_inc(one_set, 1)
            pool.wait_ge(one_set, 1)
            for n in range(RAW_SLOTS):
                split(n, 0, True)
            with pool.Fori(1, N_PANELS // RAW_SLOTS) as g:
                for n in range(RAW_SLOTS):
                    split(n, g)

        @block.tensor
        def _(pe):
            def mm3(o, w, rhs_h, rhs_l, first, last):
                s, c = w
                pe.matmul(o, wh[:, s, c], rhs_h, start=first, stop=False)
                pe.matmul(o, wh[:, s, c], rhs_l, start=False, stop=False)
                return pe.matmul(o, wl[:, s, c], rhs_h, start=False, stop=last)

            def unit(u):
                return slice(u * P, (u + 1) * P)

            def panel_ready(idx):
                pe.wait_ge(split_lo, idx + 1)

            def x_ready(n, d):
                pe.wait_ge(*prep.at(n * KD + d, "XL"))

            def col_panel(o, slot, idx, norm=None):
                panel_ready(idx)
                for k in range(KD):
                    if norm is not None:
                        x_ready(norm, k)
                    last = mm3(o, (slot, unit(k)), xh[:, k, :], xl[:, k, :], k == 0, k == KD - 1)
                last.then_inc(panel_done, 1)

            def chain_col(n, b):
                pe.wait_ge(*acc.at(n * KD + KD - 1, "ACC"))
                for t in range(TT):
                    last = pe.matmul(bank[b][:, t:t + 1], ssq[:, t * P:(t + 1) * P], ones[:, 0:1],
                                     start=True, stop=True)
                last.then_inc(chain_col_pe.sem, 1)

            def chain_bc(n, b):
                pe.wait_ge(*chain.at(n, "DG"))
                pe.matmul(bank[b][:], ones, diag[:], start=True, stop=True).then_inc(chain_bc_pe.sem, 1)

            def ffn_in(f, n, idx):
                def pair(j, at, it, first):
                    q = 2 * (j % 2)
                    a, b = (bank[4], bank[5]) if first and j == 0 else (bank[q], bank[q + 1])
                    if first:
                        pe.wait_ge(*resid.at(n * KD + (1 if j == 0 else KD - 1), "X"))
                    else:
                        pe.wait_ge(*fin.at(it - 2, "B"))
                    col_panel(a[:], 0, at, n if first and j == 0 else None)
                    if first and j == 1:
                        chain_bc(n, 7)
                    col_panel(b[:], 1, at + 1)
                    if first and j == 0:
                        pe.wait_ge(const_in, 16)
                        chain_col(n, 6)

                for j in range(2):
                    pair(j, idx + 2 * j, None, True)
                with pe.Fori(1, KF // 2) as i:
                    for j in range(2):
                        pair(j, idx + i * 4 + 2 * j, f * KF + i * 2 + j, False)

            def ffn_out(f, idx):
                ob = [bank[i] for i in (4, 5, 6, 7, 0, 1, 2, 3)]

                def k_panel(slot, p_idx, it, kt, first):
                    panel_ready(p_idx)
                    pe.wait_ge(*fin.at(it, "UL"))
                    for d in range(KD):
                        if first and d == 4:
                            pe.wait_ge(*fin.at(f * KF + KF - 1, "B"))
                        last = mm3(ob[d][:], (slot, unit(d)), uh[:, kt, :], ul[:, kt, :], first, False)
                    last.then_inc(panel_done, 1)

                for kt in range(2):
                    k_panel(kt % 2, idx + kt, f * KF + kt, kt, kt == 0)
                with pe.Fori(1, KT_MAJOR // 2) as i:
                    for q in range(2):
                        k_panel(q, idx + i * 2 + q, f * KF + i * 2 + q, i * 2 + q, False)
                rest = KF - KT_MAJOR
                pe.wait_ge(*fin.at(f * KF + KF - 1, "UL"))
                for u in range(KD * rest):
                    p, d, kt = u // UNITS, u // rest, KT_MAJOR + u % rest
                    if u % UNITS == 0:
                        panel_ready(idx + KT_MAJOR + p)
                    last = mm3(ob[d][:], (p % 2, unit(u % UNITS)), uh[:, kt, :], ul[:, kt, :], False, kt == KF - 1)
                    if u % UNITS == UNITS - 1:
                        last.then_inc(panel_done, 1)
                    elif kt == KF - 1:
                        last.then_inc(fout.sem, 1)

            def token_major(idx, banks, cols, ready=None, after_tile=None, after_panel=None):
                for p in range(KD // 2):
                    panel_ready(idx + p)
                    for kk in range(2):
                        k = 2 * p + kk
                        if ready:
                            ready(k)
                        for t in range(TT):
                            o = bank[banks[t]][:, 0:cols]
                            w = slice(kk * S, kk * S + cols)
                            tok = slice(t * P, (t + 1) * P)
                            pe.matmul(o, xh[:, k, tok], wh[:, p % 2, w], start=k == 0, stop=False)
                            pe.matmul(o, xl[:, k, tok], wh[:, p % 2, w], start=False, stop=False)
                            last = pe.matmul(o, xh[:, k, tok], wl[:, p % 2, w], start=False, stop=k == KD - 1)
                        if kk == 1:
                            last.then_inc(panel_done, 1)
                        if after_tile:
                            after_tile(k)
                    if after_panel:
                        after_panel(p)

            def ret_turn(it):
                pe.wait_ge(*ret_n.at(it, "N3"))
                for t in range(TT):
                    last = pe.transpose(bank[5][:, t * P:(t + 1) * P], yn[:, t * P:(t + 1) * P], ident)
                last.then_inc(ret_tr.sem, 1)

            def retention(l, idx):
                def head(h, first):
                    it = l * RH + h
                    at = idx + h * 4
                    if first:
                        pe.wait_ge(*rg.at(l * RH + RH - 1, "T"))
                    col_panel(bank[0][:], 0, at)
                    if not first:
                        ret_turn(it - 1)
                    col_panel(bank[1][:], 1, at + 1)
                    col_panel(bank[2][:], 0, at + 2)
                    pe.wait_ge(*ret.at(it, "KR"))
                    if not first:
                        pe.wait_ge(*ret_y.at(it - 1, "Y"))
                    for i in range(TT):
                        last = pe.matmul(bank[4 + i][:, 0:S - i * P], kr[:, i * P:(i + 1) * P], qr[:, i * P:S],
                                         start=True, stop=True)
                    last.then_inc(ret_sc.sem, 1)
                    if not first:
                        pe.wait_ge(*ret.at(it - 1, "G1"))
                    col_panel(bank[3][:], 1, at + 3)
                    pe.wait_ge(*ret.at(it, "P3"))
                    for t in range(TT):
                        for i in range(t + 1):
                            last = pe.matmul(bank[4][:, t * P:(t + 1) * P],
                                             pt[:, OFF[i] + (t - i) * P:OFF[i] + (t - i + 1) * P],
                                             v_ret[:, i, bass.ds(h * RDK, RDK)], start=i == 0, stop=i == t)
                    last.then_inc(ret_pv.sem, 1)

                head(0, True)
                with pe.Fori(1, RH) as h:
                    head(h, False)

            def fox_scores(it, e):
                for qt in range(TT):
                    b, c = HEAD_AT[qt]
                    n = (qt + 1) * P
                    pe.matmul(bank[b][:, c:c + n], fq[:, e, qt * P:n], fk[:, e, 0:n], start=True, stop=False)
                    last = pe.matmul(bank[b][:, c + n - P:c + n], ident16[:], causal, start=False, stop=True)
                last.then_inc(fx_s[e].sem, 1)

            def fox_values(it, e, v):
                pe.wait_ge(*fx_c[e].at(it, "E2"))
                pe.wait_ge(*fx_o[e].at(it, "E"))
                for qt in range(TT):
                    for j in range(qt + 1):
                        blk = FIRST_BLOCK[qt] + j
                        last = pe.matmul(bank[5][:, 2 * P + qt * FDH:2 * P + (qt + 1) * FDH],
                                         fpt[:, blk * P:(blk + 1) * P], v_fox[:, j, v(e)], start=j == 0, stop=j == qt)
                last.then_inc(fx_v[e].sem, 1)

            def fox_turn(it, b):
                pe.wait_ge(*fx_o[1].at(it, "O"))
                for t in range(TT):
                    last = pe.transpose(bank[b][:, t * P:(t + 1) * P], fo[:, t, :], ident)
                last.then_inc(fx_y.sem, 1)

            def forgetting(l, idx):
                pairs = FH // 2

                def pair(t2, first, last_pair):
                    it = l * pairs + t2

                    def v(e):
                        return bass.ds(t2 * P + e * FDH, FDH)

                    col_panel(bank[0][:], 0, idx + t2 * 2 + 2)
                    if not first:
                        fox_turn(it - 1, 1)
                    pe.wait_ge(*fx_x[0].at(it, "X"))
                    transposes(fp[:, 0, :], fx_t[0].sem)
                    fox_scores(it, 1)
                    fox_values(it, 0, v)
                    if not first:
                        pe.wait_ge(*fx_l.at(it - 1, "YL"))
                    col_panel(bank[1][:], 1, idx + t2 * 2 + 3)
                    pe.wait_ge(*fx_x[1].at(it, "X"))
                    pe.wait_ge(*fx_o[0].at(it, "O"))
                    transposes(fp[:, 1, :], fx_t[1].sem)
                    if not last_pair:
                        pe.wait_ge(*fx_q.at(it + 1, "KB"))
                        fox_scores(it + 1, 0)
                    fox_values(it, 1, v)

                pe.wait_ge(*ret.at(l * RH + RH - 1, "G1"))
                col_panel(bank[0][:], 0, idx)
                ret_turn(l * RH + RH - 1)
                col_panel(bank[1][:], 1, idx + 1)
                pe.wait_ge(*ret_y.at(l * RH + RH - 1, "Y"))
                pe.wait_ge(*fx_q.at(l * pairs, "KB"))
                pe.wait_ge(mask_set, 2)
                fox_scores(l * pairs, 0)
                pair(0, True, False)
                with pe.Fori(1, pairs - 1) as t2:
                    pair(t2, False, False)
                pair(pairs - 1, False, True)

            def transposes(p_, sem_):
                for b, blocks in ((6, (6, 7, 8, 9)), (7, (0, 3, 4, 5)), (5, (1, 2))):
                    for j, blk in enumerate(blocks):
                        last = pe.transpose(bank[b][:, j * P:(j + 1) * P], p_[:, blk * P:(blk + 1) * P], ident)
                    last.then_inc(sem_, 1)

            def merge(l, idx):
                banks = ((0, 3, 4), (1, 6, 7))

                def branch(o, slot, n, u0, yh, yl, before_last=None):
                    for k in range(n):
                        if before_last and k == n - 1:
                            before_last()
                        last = mm3(o[:], (slot, unit(u0 + k)), yh[:, k, :], yl[:, k, :], k == 0, k == n - 1)
                    return last

                def tile(d, q, it):
                    g, r, f = (bank[b] for b in banks[q])
                    pe.wait_ge(*mrg_d.at(it - 2, "F"))
                    col_panel(g[:], 0, idx + d * 2)
                    panel_ready(idx + d * 2 + 1)
                    branch(r, 1, RH, 0, yrh, yrl)
                    branch(f, 1, FH // 2, RH, yfh, yfl).then_inc(panel_done, 1)

                end = l * (FH // 2) + FH // 2 - 1
                for q in range(2):
                    _, r, f = (bank[b] for b in banks[q])
                    panel_ready(idx + 2 + q)
                    branch(r, q, RH, 0, yrh, yrl)
                    if q == 0:
                        fox_turn(end, 2)
                    branch(f, q, FH // 2, RH, yfh, yfl, None if q else lambda: pe.wait_ge(*fx_l.at(end, "YL")))\
                        .then_inc(panel_done, 1)
                with pe.Fori(1, KD // 2) as i:
                    for q in range(2):
                        tile(i * 2 + q, q, l * KD + i * 2 + q)

            def mix_out(l, n, idx):
                for d in range(KD):
                    if d >= 2:
                        pe.wait_ge(*resid.at(n * KD + d - 2, "X"))
                    panel_ready(idx + d)
                    for k in range(KD):
                        if d == 0:
                            pe.wait_ge(*mrg_d.at(l * KD + k, "L"))
                        last = mm3(bank[2 + 3 * (d % 2)][:], (d % 2, unit(k)), mh[:, k, :], ml[:, k, :],
                                   k == 0, k == KD - 1)
                    last.then_inc(panel_done, 1)

            def mla_scores(m, h):
                for qt in range(TT):
                    b, c = HEAD_AT[qt]
                    n = (qt + 1) * P
                    pe.matmul(bank[b][:, c:c + n], mq[0:MLA_K, h, qt * P:n], mk[0:MLA_K, h, 0:n],
                              start=True, stop=False)
                    last = pe.matmul(bank[b][:, c + n - P:c + n], ident16[:], causal, start=False, stop=True)
                last.then_inc(mla_sc.sem, 1)

            def mla_values(m, h):
                it = m * MH + h
                pe.wait_ge(*mla_ev.at(it, "E2"))
                pe.wait_ge(*mla_dve.at(it, "E"))
                for qt in range(TT):
                    for j in range(qt + 1):
                        blk = FIRST_BLOCK[qt] + j
                        last = pe.matmul(bank[5][:, HEAD_OUT + qt * M_V:HEAD_OUT + (qt + 1) * M_V],
                                         prt[:, blk * P:(blk + 1) * P], vm[:, j, h * M_V:(h + 1) * M_V],
                                         start=j == 0, stop=j == qt)
                last.then_inc(mla_pe.sem, 1)

            def swa_scores(m, h):
                rows = slice(SDH * (h // 2), SDH * (h // 2 + 1))
                for qt in range(TT):
                    o = bank[SWA_BANKS[qt // 2]]
                    c = 2 * P * (qt % 2)
                    mask = (C_SWA if qt else C_SWA0) - C_CAUSAL
                    k0 = max(qt - 1, 0) * P
                    n = (qt + 1) * P - k0
                    pe.matmul(o[:, c:c + 2 * P], ident16[:], masks[:, mask:mask + 2 * P], start=True, stop=False)
                    last = pe.matmul(o[:, c + 2 * P - n:c + 2 * P], aq[rows, h % 2, qt * P:(qt + 1) * P],
                                     ak[rows, k0:k0 + n], start=False, stop=True)
                last.then_inc(swa_sc.sem, 1)

            def swa_turn(m, h):
                for b, blocks in ((6, (4, 5, 6, 7)), (7, (1, 2, 3))):
                    for j, blk in enumerate(blocks):
                        last = pe.transpose(bank[b][:, j * P:(j + 1) * P], pr[:, h % 2, blk * P:(blk + 1) * P], ident)
                    last.then_inc(swa_pe.sem, 1)

            def swa_values(m, h):
                it = m * SWH + h
                pe.wait_ge(*swa_ev.at(it, "E0"))
                pe.wait_ge(*swa_dve.at(it, "E"))
                for qt in range(TT):
                    for j in range(max(qt - 1, 0), qt + 1):
                        blk = 2 * qt + j - qt + 1
                        last = pe.matmul(bank[5][:, HEAD_OUT + qt * SDH:HEAD_OUT + (qt + 1) * SDH],
                                         prt[:, blk * P:(blk + 1) * P],
                                         vtm[:, j, SDH * (h // 2):SDH * (h // 2 + 1)],
                                         start=j == max(qt - 1, 0), stop=j == qt)
                last.then_inc(swa_pe.sem, 1)

            def stick_scores(m, h):
                rows = slice(BDH * (h % 2), BDH * (h % 2 + 1))
                for j in range(TT):
                    b, c = STICK[j]
                    n = S - j * P
                    last = pe.matmul(bank[STICK_BANKS[h % 2][b]][:, c:c + n], dk[rows, h // 2, j * P:(j + 1) * P],
                                     dq[rows, h // 2, j * P:S], start=True, stop=True)
                last.then_inc(sb_sc.sem, 1)

            def stick_after(m, h):
                pe.wait_ge(*sb_keep.at(m * BH + h, "K"))
                for i in range(TT):
                    b, c = STICK[i]
                    o = bank[STICK_BANKS[h % 2][b]]
                    for j in range(i, TT):
                        n = S - j * P
                        at = STICK_AT[j]
                        tri = cst[:, C_NTRI:C_NTRI + P] if j == i else cst[:, C_NONE:C_NONE + P]
                        pe.matmul(o[:, c + (j - i) * P:c + S - i * P], tri, spl[:, h % 2, at:at + n],
                                  start=j == i, stop=False)
                    strict = C_STRICT - C_CAUSAL
                    last = pe.matmul(o[:, c:c + P], ident16[:], masks[:, strict:strict + P], start=False, stop=True)
                last.then_inc(sb_pe.sem, 1)

            def stick_values(m, h):
                pe.wait_ge(*sb_act.at(m * BH + h, "P"))
                for qt in range(TT):
                    for j in range(qt + 1):
                        at = STICK_AT[j] + (qt - j) * P
                        last = pe.matmul(bank[6][:, qt * BDH:(qt + 1) * BDH], lsg[:, h % 2, at:at + P],
                                         vtm[:, j, 2 * SDH + h * BDH:2 * SDH + (h + 1) * BDH],
                                         start=j == 0, stop=j == qt)
                last.then_inc(sb_pe.sem, 1)

            def fill(m, c):
                it = m * 2
                gate0 = m * KD
                free = (pj.at(m, "E0"), pj.at(m, "E1"), conv.at(it, "C"), conv.at(it, "X"), conv.at(it, "G"),
                        conv.at(it + 1, "C"), conv.at(it + 1, "X"), conv.at(it + 1, "G"),
                        swa_dve.at(m * SWH + SWH - 1, "E"), gate_in.at(gate0 + 2, "G"), gate_in.at(gate0 + 3, "G"),
                        gate_in.at(gate0 + 4, "G"), gn.at(m, "C"), sb_dve.at(m * BH + 2, "T"))
                pe.wait_ge(*free[c])
                col_panel(bank[FILL_BANK[c]][:], c % 2, SECOND + m * LAYER2 + BT_CONV + c)

            def hybrid(m):
                q0 = SECOND + m * LAYER2
                n = FINAL + 1 + m

                def sum_squares(k):
                    if k == 0:
                        return
                    for d in (k - 1, k) if k == KD - 1 else (k - 1,):
                        pe.wait_ge(*hyb_act.at(m * KD + d, "SQ"))
                        for t in range(TT):
                            last = pe.matmul(bank[0][:, t:t + 1], z[:, d, t * P:(t + 1) * P], ones[:, 0:1],
                                             start=d == t == 0, stop=d == KD - 1 and t == TT - 1)
                    if k == KD - 1:
                        last.then_inc(hyb_sq.sem, 1)

                token_major(q0 + BT_TM, (4, 5, 6, 7), TM_COLS, lambda k: pe.wait_ge(*hyb_xl.at(m * KD + k, "XL")),
                            after_tile=sum_squares)
                col_panel(bank[2][:], 0, q0 + BT_CQ)
                chain_bc(n, 1)
                col_panel(bank[3][:], 1, q0 + BT_CQ + 1)
                pe.wait_ge(*chain.at(n, "RB"))
                col_panel(bank[0][:], 0, q0 + BT_CKV)
                col_panel(bank[1][:], 1, q0 + BT_AK)
                pe.wait_ge(*pj.at(m, "T2"))
                pe.wait_ge(*lat.at(m, "SUM"))
                pe.wait_ge(*lat_act.at(m, "SK"))
                for i, src in enumerate((qsq[:, 0, :], ksq[:])):
                    for t in range(TT):
                        c = i * TT + t
                        last = pe.matmul(bank[4][:, c:c + 1], src[:, t * P:(t + 1) * P], ones[:, 0:1],
                                         start=True, stop=True)
                last.then_inc(lat_pe.sem, 1)
                pe.wait_ge(*pj.at(m, "Q0"))
                col_panel(bank[2][:], 0, q0 + BT_AQ)
                pe.wait_ge(*lat.at(m, "GK"))
                pe.matmul(bank[5][:], ones, diag_q[:], start=True, stop=True)
                pe.matmul(bank[6][:], ones, diag_k[:], start=True, stop=True).then_inc(lat_pe.sem, 1)
                pe.wait_ge(*pj.at(m, "Q1"))
                col_panel(bank[3][:], 1, q0 + BT_AQ + 1)
                pe.wait_ge(*lat.at(m, "LK"))
                panel_ready(q0 + BT_UQ)
                for h in range(MH):
                    for k in range(2):
                        last = mm3(bank[4 + h][:], (0, unit(2 * h + k)), cqh[:, k, :], cql[:, k, :], k == 0, k == 1)
                last.then_inc(panel_done, 1)
                for i, free in enumerate(("KV", "AK")):
                    pe.wait_ge(*pj.at(m, free))
                    col_panel(bank[i][:], 1 - i, q0 + BT_DQ + i)
                panel_ready(q0 + BT_UKV)
                for h in (2, 3, 0, 1):
                    pe.wait_ge(*pj.at(m, ("D0", "D1", "A0", "A1")[h]))
                    mm3(bank[h][:], (1, slice(h * M_NOPE, h * M_NOPE + P)), ckh[:], ckl[:], True, True)
                for t in range(TT):
                    if t % 2 == 0:
                        pe.wait_ge(*mla.at(m, f"R{t // 2}"))
                    o = bank[4 + t // 2][:, (t % 2) * GROUP:(t % 2 + 1) * GROUP]
                    w = slice(MH * M_NOPE, MH * (M_NOPE + M_V))
                    tok = slice(t * P, (t + 1) * P)
                    pe.matmul(o, ckh[:, tok], wh[:, 1, w], start=True, stop=False)
                    pe.matmul(o, ckl[:, tok], wh[:, 1, w], start=False, stop=False)
                    pe.matmul(o, ckh[:, tok], wl[:, 1, w], start=False, stop=True)
                pe.wait_ge(*mla.at(m, "R2"))
                for k in range(KD):
                    c = KR_AT + k * KR_W
                    last = mm3(bank[6][:], (1, slice(c, c + P)), xh[:, k, :], xl[:, k, :], k == 0, k == KD - 1)
                last.then_inc(panel_done, 1)
                for i in range(2):
                    pe.wait_ge(*kv_act.at(m, f"N{i}"))
                    col_panel(bank[i][:], i, q0 + BT_DK + i)
                pe.wait_ge(*kv_act.at(m, "C3"))
                pe.wait_ge(*kv.at(m, "KR"))
                mla_scores(m, 0)
                for h in range(MH):
                    it = m * MH + h
                    fill(m, h)
                    pe.wait_ge(*mla_ex.at(it, "X"))
                    if h:
                        pe.wait_ge(*mla_dve.at(it - 1, "O"))
                    transposes(pr[:, h % 2, :], mla_pe.sem)
                    if h < MH - 1:
                        mla_scores(m, h + 1)
                    else:
                        swa_scores(m, 0)
                    mla_values(m, h)
                for h in range(SWH):
                    it = m * SWH + h
                    fill(m, MH + h)
                    pe.wait_ge(*swa_ex.at(it, "X"))
                    swa_turn(m, h)
                    if h < SWH - 1:
                        swa_scores(m, h + 1)
                    else:
                        stick_scores(m, 0)
                    pe.wait_ge(*(swa_dve.at(it - 1, "O") if h else mla_dve.at(m * MH + MH - 1, "O")))
                    swa_values(m, h)
                for h in range(BH):
                    it = m * BH + h
                    if h == 0:
                        fill(m, MH + SWH)
                        pe.wait_ge(*swa_dve.at(m * SWH + SWH - 1, "O"))
                        pe.wait_ge(*gate_in.at(m * KD + 1, "G"))
                    if h < BH - 1:
                        if h:
                            pe.wait_ge(*sb_dve.at(it - 1, "T"))
                        stick_scores(m, h + 1)
                    stick_after(m, h)
                    if h < BH - 1:
                        fill(m, MH + SWH + 1 + h)
                    else:
                        pe.wait_ge(*gn.at(m, "SUM"))
                        pe.wait_ge(*gate_in.at(m * KD + KD - 3, "G"))
                        for t in range(TT):
                            last = pe.matmul(bank[7][:, t:t + 1], cgs[:, t * P:(t + 1) * P], ones[:, 0:1],
                                             start=True, stop=True)
                        last.then_inc(gn_pe.sem, 1)
                    if h:
                        pe.wait_ge(*sb_act.at(it - 1, "O"))
                    stick_values(m, h)

                def turn(y, i):
                    pe.wait_ge(*gn.at(m, f"N{i}"))
                    for c in range(2):
                        for t in range(TT):
                            last = pe.transpose(bank[GROUP_BANKS[i][c]][:, t * P:(t + 1) * P],
                                                y[:, t, c * P:(c + 1) * P], ident)
                    last.then_inc(gn_pe.sem, 1)

                fill(m, 12)
                pe.wait_ge(*sb_dve.at(m * BH + BH - 1, "T"))
                turn(y_swa, 0)
                turn(y_mla, 1)
                fill(m, 13)
                turn(y_sb, 2)
                pe.wait_ge(*gn.at(m, "DG"))
                pe.wait_ge(*gate_y.at(m * KD + 1, "Y"))
                pe.matmul(bank[3][:], ones, diag[:], start=True, stop=True).then_inc(gn_pe.sem, 1)
                for d in range(KD):
                    pe.wait_ge(*(gate_in.at(m * KD + KD - 2 + d, "G") if d < 2 else z_act.at(m * KD + d - 2, "Z")))
                    panel_ready(q0 + BT_WOUT + d)
                    for j, k in enumerate(READY):
                        if d == 0:
                            pe.wait_ge(*gate_l.at(m * KD + j, "L"))
                        last = mm3(bank[OUT_BANKS[d % 2]][:], (d % 2, unit(k)), ygh[:, k, :], ygl[:, k, :],
                                   j == 0, j == KD - 1)
                    last.then_inc(panel_done, 1)
                pe.wait_ge(*z_sum.at(m * KD + KD - 1, "A"))
                for t in range(TT):
                    last = pe.matmul(bank[4][:, t:t + 1], ssq[:, t * P:(t + 1) * P], ones[:, 0:1],
                                     start=True, stop=True)
                last.then_inc(post_pe.sem, 1)
                pe.wait_ge(*post.at(m, "DG"))
                pe.matmul(bank[3][:], ones, diag[:], start=True, stop=True).then_inc(post_pe.sem, 1)

            with pe.Fori(0, DEPTH) as l:
                p0 = l * LAYER1
                ffn_in(l * 2, l * 3, p0)
                ffn_out(l * 2, p0 + FFN_IN)
                n = l * 3 + 1
                for t in range(TT):
                    pe.wait_ge(*resid.at(n * KD + t, "X"))

                def chain_steps(p):
                    if p == 0:
                        chain_col(n, 0)
                    elif p == 2:
                        chain_bc(n, 1)

                token_major(p0 + AT_RV, (4, 5, 6, 7), S, lambda k: x_ready(n, k), after_panel=chain_steps)
                pe.wait_ge(*chain.at(n, "RB"))
                token_major(p0 + AT_FV, (0, 1, 2, 3), S)
                pe.wait_ge(*tm.at(l, "RV3"))
                pe.wait_ge(*ffs.at(l, "L"))
                for k in range(KD):
                    c = slice(k * FF_W, k * FF_W + P)
                    pe.matmul(bank[4][:], ffh[:, c], xh[:, k, :], start=k == 0, stop=False)
                    pe.matmul(bank[4][:], ffh[:, c], xl[:, k, :], start=False, stop=False)
                    last = pe.matmul(bank[4][:], ffl[:, c], xh[:, k, :], start=False, stop=k == KD - 1)
                last.then_inc(ffs_pe.sem, 1)
                with pe.Fori(0, RH // 2) as i:
                    for q in range(2):
                        pe.wait_ge(*tm.at(l, "FV3"))
                        pe.wait_ge(*rg.before(l * RH + i * 2))
                        col_panel(bank[q][:], q, p0 + AT_RG + i * 2 + q)
                retention(l, p0 + AT_RET)
                forgetting(l, p0 + AT_FOX)
                merge(l, p0 + AT_MERGE)
                mix_out(l, n + 1, p0 + AT_WOUT)
                ffn_in(l * 2 + 1, l * 3 + 2, p0 + AT_FFN2)
                ffn_out(l * 2 + 1, p0 + AT_FFN2 + FFN_IN)

            chain_col(FINAL, 6)
            chain_bc(FINAL, 7)
            with pe.Fori(0, DEPTH) as m:
                hybrid(m)

        @block.scalar
        def _(act):
            def squares(n):
                def tile(d, q, first):
                    act.wait_ge(*resid.at(n * KD + d, "X"))
                    if not first:
                        act.wait_ge(*acc.at(n * KD + d - 2, "ACC"))
                    act.activation((sq, diag)[q][:], x[:, d, :], ACT.Square).then_inc(prep_sq.sem, 1)

                for q in range(2):
                    tile(q, q, True)
                with act.Fori(1, KD // 2) as i:
                    for q in range(2):
                        tile(i * 2 + q, q, False)

            def chain_std(n, b, summed=None):
                act.wait_ge(*(summed or chain_col_pe.at(n, "COL")))
                act.activation(std_col[:], bank[b][:, 0:TT], ACT.Sqrt, bias=eps[:], scale=1.0 / D)\
                   .then_inc(chain_sd.sem, 1)

            def ffn_in(f, n):
                with act.Fori(0, KF) as j:
                    it = f * KF + j
                    act.wait_ge(*fin.at(it, "A"))
                    act.activation(sa[:], ta[:], ACT.Silu).then_inc(fin_act.sem, 1)
                    act.wait_ge(*fin.at(it, "U"))
                    act.activation(uh[:, j, :], u32[:], ACT.Copy).then_inc(fin_act.sem, 1)

            def ret_out(it, h):
                act.wait_ge(*ret_y.at(it, "Y"))
                act.activation(yrh[:, h, :], y32[:], ACT.Copy).then_inc(ret_h.sem, 1)

            def retention(l):
                def head(h, first):
                    it = l * RH + h
                    for src, name in ((tq, "Q"), (tk, "K")):
                        act.wait_ge(*ret.at(it, name))
                        if name == "K":
                            act.wait_ge(*ret.at(it, "QS"))
                        act.activation(sw[0:64, :], src[64:128, :], ACT.Copy).then_inc(ret_sw.sem, 1)
                        act.activation(sw[64:128, :], src[0:64, :], ACT.Copy).then_inc(ret_sw.sem, 1)
                        if name == "Q" and not first:
                            ret_out(it - 1, h - 1)
                    act.wait_ge(*ret_pv.at(it, "P"))
                    for t in range(TT):
                        act.activation(sw[:, t * P:(t + 1) * P], bank[4][:, t * P:(t + 1) * P], ACT.Square,
                                       accum_out=hsum[:, t:t + 1]).then_inc(ret_sq.sem, 1)
                    act.wait_ge(*ret_sq.at(it, "S3"))
                    act.activation(hstd[:], hsum[:], ACT.Sqrt, bias=eps[:], scale=1.0 / RDK).then_inc(ret_sq.sem, 1)

                head(0, True)
                with act.Fori(1, RH) as h:
                    head(h, False)
                ret_out(l * RH + RH - 1, RH - 1)

            def fox_probs(it, e):
                act.wait_ge(*fx_m[e].at(it, "N"))
                for qt in range(TT):
                    b, c = HEAD_AT[qt]
                    n = (qt + 1) * P
                    last = act.activation(fp[:, e, FIRST_BLOCK[qt] * P:FIRST_BLOCK[qt] * P + n], bank[b][:, c:c + n],
                                          ACT.Exp, bias=fnm[:, e, qt:qt + 1], scale=FDH ** -0.5,
                                          accum_out=fsum[:, e, qt:qt + 1])
                last.then_inc(fx_x[e].sem, 1)

            def fox_turned(it, e, first):
                act.wait_ge(*fx_t[e].at(it, "T0"))
                if e:
                    act.wait_ge(*fx_v[0].at(it, "P"))
                elif not first:
                    act.wait_ge(*fx_v[1].at(it - 1, "P"))
                act.activation(fpt[:, 6 * P:10 * P], bank[6][:], ACT.Copy).then_inc(fx_c[e].sem, 1)
                act.wait_ge(*fx_t[e].at(it, "T2"))
                act.activation(fpt[:, P:3 * P], bank[5][:, 0:2 * P], ACT.Copy).then_inc(fx_c[e].sem, 1)

            def fox_out(it, t2, b):
                act.wait_ge(*fx_y.at(it, "TR"))
                act.activation(yfh[:, t2, :], bank[b][:], ACT.Copy).then_inc(fx_h.sem, 1)

            def forgetting(l):
                pairs = FH // 2

                def pair(t2, first, last_pair):
                    it = l * pairs + t2
                    if not first:
                        fox_out(it - 1, t2 - 1, 1)
                    fox_turned(it, 0, first)
                    fox_probs(it, 1)
                    fox_turned(it, 1, first)
                    if not last_pair:
                        fox_probs(it + 1, 0)

                fox_probs(l * pairs, 0)
                pair(0, True, False)
                with act.Fori(1, pairs - 1) as t2:
                    pair(t2, False, False)
                pair(pairs - 1, False, True)
                fox_out(l * pairs + pairs - 1, pairs - 1, 2)

            def operands(m):
                n = FINAL + 1 + m
                for d in range(KD):
                    act.wait_ge(*resid.at(n * KD + d, "X"))
                    act.activation(xh[:, d, :], x[:, d, :], ACT.Copy, scale=vecs[:, bass.ds(n * KD + d, 1)])\
                       .then_inc(hyb_act.sem, 1)
                    act.activation(z[:, d, :], x[:, d, :], ACT.Square).then_inc(hyb_act.sem, 1)

            def mla_probs(m, h):
                it = m * MH + h
                act.wait_ge(*mla_mx.at(it, "N"))
                for qt in range(TT):
                    b, c = HEAD_AT[qt]
                    n = (qt + 1) * P
                    at = FIRST_BLOCK[qt] * P
                    last = act.activation(pr[:, h % 2, at:at + n], bank[b][:, c:c + n], ACT.Exp,
                                          bias=snm[:, h % 2, qt:qt + 1], scale=(M_NOPE + M_ROPE) ** -0.5,
                                          accum_out=ssum[:, h % 2, qt:qt + 1])
                last.then_inc(mla_ex.sem, 1)

            def swa_probs(m, h):
                it = m * SWH + h
                act.wait_ge(*swa_mx.at(it, "N"))
                for qt in range(TT):
                    o = bank[SWA_BANKS[qt // 2]]
                    c = 2 * P * (qt % 2)
                    last = act.activation(pr[:, h % 2, qt * 2 * P:(qt + 1) * 2 * P], o[:, c:c + 2 * P], ACT.Exp,
                                          bias=snm[:, h % 2, qt:qt + 1], scale=SDH ** -0.5,
                                          accum_out=ssum[:, h % 2, qt:qt + 1])
                last.then_inc(swa_ex.sem, 1)
                act.activation(esk[:, h % 2, :], snm[:, h % 2, :], ACT.Exp,
                               bias=vecs[:, bass.ds(m * SWH + V_SINK + h, 1)]).then_inc(swa_ex.sem, 1)

            def stick_logs(m, h):
                it = m * BH + h
                buf = lsg[:, h % 2, :]
                act.wait_ge(*sb_sc.at(it, "Z"))
                for b, c, n in PIECES:
                    last = act.activation(buf[:, c:c + n], bank[STICK_BANKS[h % 2][b]][:, 0:n], ACT.Abs)
                last.then_inc(sb_ln.sem, 1)
                act.wait_ge(*sb_ln.at(it, "AB"))
                act.activation(buf, buf, ACT.Exp, scale=-1.0).then_inc(sb_ln.sem, 1)
                act.wait_ge(*sb_ln.at(it, "EX"))
                act.activation(buf, buf, ACT.Ln, bias=ones[:, 0:1]).then_inc(sb_ln.sem, 1)

            def hybrid(m):
                n = FINAL + 1 + m
                chain_std(n, 0, hyb_sq.at(m, "U"))
                for i in range(2):
                    act.wait_ge(*pj.at(m, f"Q{i}"))
                    act.activation(qsq[:, i, :], cq[:, i, :], ACT.Square).then_inc(lat_act.sem, 1)
                act.wait_ge(*pj.at(m, "KV"))
                act.activation(ksq[:], ckv[:], ACT.Square).then_inc(lat_act.sem, 1)
                act.wait_ge(*lat_pe.at(m, "COL"))
                for i, n_ in enumerate((QR, KVR)):
                    act.activation(lstd[:, i, :], bank[4][:, i * TT:(i + 1) * TT], ACT.Sqrt, bias=eps[:],
                                   scale=1.0 / n_).then_inc(lat_act.sem, 1)
                for i, (name, dst) in enumerate((("N0", cqh[:, 0, :]), ("N1", cqh[:, 1, :]), ("NK", ckh[:]))):
                    act.wait_ge(*lat.at(m, name))
                    act.activation(dst, cn[:, i % 2, :], ACT.Copy).then_inc(lat_act.sem, 1)
                act.wait_ge(panel_done, SECOND + m * LAYER2 + BT_UQ + 1)
                act.wait_ge(*mla.at(m, "Z"))
                for h in range(MH):
                    b = bank[4 + h]
                    act.activation(mq[0:M_NOPE, h, :], b[0:M_NOPE, :], ACT.Copy).then_inc(mla_act.sem, 1)
                    if h:
                        act.wait_ge(*mla.at(m, f"S{h - 1}"))
                    act.activation(msw[64:80, :], b[96:112, :], ACT.Copy).then_inc(mla_act.sem, 1)
                    act.activation(msw[96:112, :], b[64:80, :], ACT.Copy).then_inc(mla_act.sem, 1)
                act.wait_ge(panel_done, SECOND + m * LAYER2 + BT_UKV + 1)
                for h in range(MH):
                    act.activation(mk[0:M_NOPE, h, :], bank[h][0:M_NOPE, :], ACT.Copy).then_inc(kv_act.sem, 1)
                act.wait_ge(*kv.at(m, "KS"))
                act.wait_ge(*mla.at(m, f"S{MH - 1}"))
                act.activation(kx[64:112, :], krs[0:KR_W, :], ACT.Copy).then_inc(kv_act.sem, 1)
                act.activation(msw[64:80, :], krs[32:48, :], ACT.Copy).then_inc(kv_act.sem, 1)
                act.activation(msw[96:112, :], krs[0:16, :], ACT.Copy).then_inc(kv_act.sem, 1)
                act.wait_ge(*kv.at(m, "KR"))
                for h in range(1, MH):
                    act.activation(mk[64:112, h, :], mk[64:112, 0, :], ACT.Copy).then_inc(kv_act.sem, 1)
                def group_squares(y, i):
                    for t in range(TT):
                        last = act.activation((sq, ssq)[t // 2][:, (t % 2) * GROUP:(t % 2 + 1) * GROUP], y[:, t, :],
                                              ACT.Square, accum_out=gsum[:, i, t:t + 1])
                    last.then_inc(gn_act.sem, 1)

                mla_probs(m, 0)
                for h in range(MH):
                    it = m * MH + h
                    act.wait_ge(*mla_pe.at(it, "T0"))
                    if h:
                        act.wait_ge(*mla_pe.at(it - 1, "V"))
                    act.activation(prt[:, 6 * P:10 * P], bank[6][:], ACT.Copy).then_inc(mla_ev.sem, 1)
                    act.wait_ge(*mla_pe.at(it, "T2"))
                    act.activation(prt[:, P:3 * P], bank[5][:, 0:2 * P], ACT.Copy).then_inc(mla_ev.sem, 1)
                    if h < MH - 1:
                        mla_probs(m, h + 1)
                    else:
                        swa_probs(m, 0)
                for h in range(SWH):
                    it = m * SWH + h
                    act.wait_ge(*swa_pe.at(it, "T0"))
                    act.wait_ge(*(swa_pe.at(it - 1, "V") if h else mla_pe.at(m * MH + MH - 1, "V")))
                    act.activation(prt[:, 4 * P:8 * P], bank[6][:], ACT.Copy).then_inc(swa_ev.sem, 1)
                    if h < SWH - 1:
                        swa_probs(m, h + 1)
                    if h == 0:
                        act.wait_ge(*mla_dve.at(m * MH + MH - 1, "O"))
                        group_squares(y_mla, 1)
                    elif h == 2:
                        act.wait_ge(*conv.at(m * 2 + 1, "Y"))
                        for i, dst in enumerate((cgs, cxs)):
                            act.activation(dst[:], y_conv[:, i, :], ACT.Square).then_inc(gn_act.sem, 1)
                stick_logs(m, 0)
                for h in range(BH):
                    it = m * BH + h
                    if h < BH - 1:
                        if h:
                            act.wait_ge(*sb_pe.at(it - 1, "V"))
                        stick_logs(m, h + 1)
                    if h == 0:
                        act.wait_ge(*swa_dve.at(m * SWH + SWH - 1, "O"))
                        act.wait_ge(*gn_act.at(m, "S1"))
                        group_squares(y_swa, 0)
                    act.wait_ge(*sb_dve.at(it, "T"))
                    act.activation(lsg[:, h % 2, :], lsg[:, h % 2, :], ACT.Exp).then_inc(sb_act.sem, 1)
                    if h == BH - 1:
                        act.wait_ge(*gn_act.at(m, "S0"))
                        act.activation(gstd[:, 0:2, :], gsum[:, 0:2, :], ACT.Sqrt, bias=eps[:], scale=1.0 / GROUP)\
                           .then_inc(gn_act.sem, 1)
                    act.wait_ge(*sb_pe.at(it, "V"))
                    act.activation(y_sb[:, :, h * BDH:(h + 1) * BDH],
                                   bank[6][:, 0:TT * BDH].rearrange("p (t c) -> p t c", c=BDH),
                                   ACT.Copy).then_inc(sb_act.sem, 1)
                act.wait_ge(*sb_act.at(m * BH + BH - 1, "O"))
                group_squares(y_sb, 2)
                act.wait_ge(*gn_act.at(m, "S2"))
                act.wait_ge(*gn.at(m, "C"))
                act.activation(gstd[:, 2:4, :], gsum[:, 2:4, :], ACT.Sqrt, bias=eps[:], scale=1.0 / GROUP)\
                   .then_inc(gn_act.sem, 1)

                def gate_hi(j):
                    act.wait_ge(*gate_y.at(m * KD + j, "Y"))
                    act.activation(ygh[:, READY[j], :], yg[:, j % 2, :], ACT.Copy).then_inc(gate_h.sem, 1)

                for d in range(KD):
                    act.wait_ge(*gate_in.at(m * KD + d, "G"))
                    act.activation(gates[:, d, :], gates[:, d, :], ACT.Silu).then_inc(gate_s.sem, 1)
                    if d == KD - 2:
                        gate_hi(0)
                        gate_hi(1)
                for j in range(2, KD):
                    gate_hi(j)
                act.activation(root[:], eps[:], ACT.Sqrt).then_inc(sqrt_set, 1)
                for d in range(KD):
                    it = m * KD + d
                    src = bank[OUT_BANKS[d % 2]][:]
                    act.wait_ge(panel_done, SECOND + m * LAYER2 + BT_WOUT + d + 1)
                    if d >= 2:
                        act.wait_ge(*z_sum.at(it - 2, "A"))
                    act.activation((sq, diag)[d % 2][:], src, ACT.Square).then_inc(z_act.sem, 1)
                    act.activation(z[:, d, :], src, ACT.Copy).then_inc(z_act.sem, 1)
                act.wait_ge(sqrt_set, m + (DEPTH + 1))
                act.wait_ge(*post_pe.at(m, "COL"))
                act.activation(std_col[:], bank[4][:, 0:TT], ACT.Sqrt, bias=eps[:], scale=1.0 / D)\
                   .then_inc(post_sd.sem, 1)
                operands(m + 1)

            act.wait_ge(memsets, 1)
            act.activation(start_a[:], eps[:], ACT.Copy).then_inc(rg_act.sem, 1)
            squares(0)
            act.wait_ge(const_in, 16)
            chain_std(0, 6)
            act.wait_ge(*trig.at(0, "s6"))
            act.activation(sin2[64:96, :], ang[64:96, :], ACT.Sin, scale=-1.0).then_inc(trig_act.sem, 1)
            act.activation(sin2[96:112, :], ang[96:112, :], ACT.Sin).then_inc(trig_act.sem, 1)
            act.wait_ge(*trig.at(0, "c6"))
            act.activation(cos2[64:112, :], turn[64:112, :], ACT.Sin).then_inc(trig_act.sem, 1)
            with act.Fori(0, DEPTH) as l:
                ffn_in(l * 2, l * 3)
                squares(l * 3 + 1)
                act.wait_ge(*resid.at((l * 3 + 1) * KD + KD - 1, "X"))
                act.dma_start(dec[:], decay).then_inc(tab_in, 16)
                act.dma_start(rp[:], rope).then_inc(tab_in, 16)
                act.dma_start(ffraw[:], ff_w[l]).then_inc(tab_in, 16)
                chain_std(l * 3 + 1, 0)
                with act.Fori(0, RH) as h:
                    act.wait_ge(*rg.at(l * RH + h, "T"))
                    act.activation(rgs[:, h, :], tg[:], ACT.Silu).then_inc(rg_act.sem, 1)
                act.wait_ge(*ffs.at(l, "ZB"))
                act.activation(fa[0:FF_W], fz[0:FF_W], ACT.Abs).then_inc(ffs_act.sem, 1)
                act.wait_ge(*ffs_act.at(l, "ABS"))
                act.activation(fa[0:FF_W], fa[0:FF_W], ACT.Exp, scale=-1.0).then_inc(ffs_act.sem, 1)
                act.wait_ge(*ffs_act.at(l, "EXP"))
                act.activation(fa[0:FF_W], fa[0:FF_W], ACT.Ln, bias=ones[0:FF_W, 0:1]).then_inc(ffs_act.sem, 1)
                retention(l)
                forgetting(l)
                with act.Fori(0, KD) as d:
                    it = l * KD + d
                    act.wait_ge(*mrg_d.at(it, "G"))
                    act.activation(sr[:], gate_r[:, d, :], ACT.Sigmoid).then_inc(mrg_a.sem, 1)
                    act.activation(sf[:], tgf[:], ACT.Sigmoid).then_inc(mrg_a.sem, 1)
                    act.wait_ge(*mrg_d.at(it, "M"))
                    act.activation(mh[:, d, :], mg[:], ACT.Copy).then_inc(mrg_a.sem, 1)
                squares(l * 3 + 2)
                chain_std(l * 3 + 2, 6)
                ffn_in(l * 2 + 1, l * 3 + 2)
                act.activation(root[:], eps[:], ACT.Sqrt).then_inc(sqrt_set, 1)
                squares(l * 3 + 3)
                act.wait_ge(sqrt_set, l + 1)
                chain_std(l * 3 + 3, 6)
            operands(0)
            with act.Fori(0, DEPTH) as m:
                hybrid(m)

        @block.vector
        def _(dve):
            def prepare(n, d, g):
                gain = vecs[:, bass.ds(g * KD + d, 1)]
                dve.wait_ge(*resid.at(n * KD + d, "X"))
                dve.tensor_scalar(xh[:, d, :], x[:, d, :], gain, None, ALU.mult).then_inc(prep.sem, 1)
                dve.wait_ge(*prep.at(n * KD + d, "XH"))
                dve.scalar_tensor_tensor(out=xl[:, d, :], in0=x[:, d, :], scalar=gain,
                                         in1=xh[:, d, :].bitcast(F32), op0=ALU.mult,
                                         op1=ALU.subtract).then_inc(prep.sem, 1)

            def operand_lo(m, d):
                dve.wait_ge(*hyb_act.at(m * KD + d, "XH"))
                dve.scalar_tensor_tensor(out=xl[:, d, :], in0=x[:, d, :],
                                         scalar=vecs[:, bass.ds((FINAL + 1 + m) * KD + d, 1)],
                                         in1=xh[:, d, :].bitcast(F32), op0=ALU.mult,
                                         op1=ALU.subtract).then_inc(hyb_xl.sem, 1)

            def add_squares(n, d):
                dve.wait_ge(*prep_sq.at(n * KD + d, "SQ"))
                if d == 0:
                    dve.tensor_copy(ssq[:], sq[:]).then_inc(acc.sem, 1)
                else:
                    dve.wait_ge(*acc.at(n * KD + d - 1, "ACC"))
                    dve.tensor_tensor(ssq[:], ssq[:], (sq, diag)[d % 2][:], ALU.add).then_inc(acc.sem, 1)

            def diagonal(dst, col, st):
                dve.tensor_tensor(dst[:].rearrange("p (t c) -> p t c", c=P),
                                  ident.rearrange("p (t c) -> p t c", t=1).to_broadcast([P, TT, P]),
                                  col.rearrange("p (t c) -> p t c", c=1).to_broadcast([P, TT, P]),
                                  ALU.mult).then_inc(st.sem, 1)

            def norm_chain(n, b, between=None):
                dve.wait_ge(*chain_sd.at(n, "SD"))
                dve.reciprocal(rstd_col[:], std_col[:]).then_inc(chain.sem, 1)
                dve.wait_ge(*chain.at(n, "RC"))
                diagonal(diag, rstd_col[:], chain)
                if between:
                    between()
                dve.wait_ge(*chain_bc_pe.at(n, "BC"))
                dve.tensor_copy(rstd[:], bank[b][:]).then_inc(chain.sem, 1)

            def scaled(dst, src, st):
                dve.tensor_tensor(dst, src, rstd[:], ALU.mult).then_inc(st.sem, 1)

            def ffn_in(f, n, idx):
                def pair(j, a, b, at):
                    it = f * KF + j
                    dve.wait_ge(panel_done, at + 1)
                    scaled(ta[:], a[:], fin)
                    dve.wait_ge(panel_done, at + 2)
                    scaled(tb[:], b[:], fin)
                    dve.wait_ge(*fin_act.at(it, "SILU"))
                    dve.wait_ge(*fin.at(it, "B"))
                    dve.tensor_tensor(u32[:], sa[:], tb[:], ALU.mult).then_inc(fin.sem, 1)
                    dve.wait_ge(*fin_act.at(it, "UH"))
                    dve.tensor_tensor(ul[:, j, :], u32[:], uh[:, j, :].bitcast(F32), ALU.subtract)\
                       .then_inc(fin.sem, 1)

                dve.wait_ge(*chain.at(n, "RB"))
                pair(0, bank[4], bank[5], idx)
                pair(1, bank[2], bank[3], idx + 2)
                with dve.Fori(1, KF // 2) as i:
                    for q in range(2):
                        pair(i * 2 + q, bank[2 * q], bank[2 * q + 1], idx + i * 4 + 2 * q)

            def ffn_out(f, n, idx):
                rest = KF - KT_MAJOR
                steps = 0
                for d in range(KD):
                    done = (d + 1) * rest
                    if done % UNITS == 0:
                        dve.wait_ge(panel_done, idx + KT_MAJOR + done // UNITS)
                    else:
                        dve.wait_ge(fout.sem, f * (KD - 2) + steps + 1)
                        steps += 1
                    dve.scalar_tensor_tensor(out=x[:, d, :], in0=bank[(4 + d) % 8][:], scalar=0.5,
                                             in1=x[:, d, :], op0=ALU.mult, op1=ALU.add).then_inc(resid.sem, 1)
                    prepare(n, d, n)
                    add_squares(n, d)

            def ret_norm(it):
                dve.wait_ge(*ret_sq.at(it, "SD"))
                dve.reciprocal(hinv[:], hstd[:]).then_inc(ret_n.sem, 1)
                dve.wait_ge(*ret_n.at(it, "RC"))
                for t in range(TT):
                    dve.tensor_scalar(yn[:, t * P:(t + 1) * P], bank[4][:, t * P:(t + 1) * P],
                                      hinv[:, t:t + 1], None, ALU.mult).then_inc(ret_n.sem, 1)

            def ret_out(it, l, h):
                dve.wait_ge(*ret_tr.at(it, "P"))
                dve.scalar_tensor_tensor(out=y32[:], in0=bank[5][:], scalar=vecs[:, bass.ds(l * RH + h + V_RET, 1)],
                                         in1=rgs[:, h, :], op0=ALU.mult, op1=ALU.mult).then_inc(ret_y.sem, 1)
                dve.wait_ge(*ret_h.at(it, "YH"))
                dve.tensor_tensor(yrl[:, h, :], y32[:], yrh[:, h, :].bitcast(F32), ALU.subtract).then_inc(ret_y.sem, 1)

            def retention(l, idx):
                def rotated(it, dst, src, name):
                    dve.wait_ge(*ret.at(it, name))
                    dve.tensor_tensor(m1[:], src[:], rp[:, 0, :], ALU.mult).then_inc(ret.sem, 1)
                    dve.wait_ge(*ret_sw.at(it, name + "1"))
                    dve.tensor_tensor(dst[:], sw[:], rp[:, 1, :], ALU.mult).then_inc(ret.sem, 1)
                    dve.wait_ge(*ret.at(it, name + "S"))
                    dve.tensor_tensor(dst[:], dst[:], m1[:], ALU.add).then_inc(ret.sem, 1)

                def head(h, first):
                    it = l * RH + h
                    at = idx + h * 4
                    if first:
                        dve.wait_ge(*rg_act.before((l + 1) * RH))
                    else:
                        ret_norm(it - 1)
                    dve.wait_ge(panel_done, at + 1)
                    scaled(tq[:], bank[0][:], ret)
                    rotated(it, qr, tq, "Q")
                    if not first:
                        dve.wait_ge(*ret.at(it, "QR"))
                        ret_out(it - 1, l, h - 1)
                    dve.wait_ge(panel_done, at + 2)
                    scaled(tk[:], bank[1][:], ret)
                    dve.wait_ge(*ret.at(it, "QR"))
                    rotated(it, kr, tk, "K")
                    dve.wait_ge(panel_done, at + 3)
                    scaled(gate_r[:, h * 2, :], bank[2][:], ret)
                    dve.wait_ge(*ret_sc.at(it, "P"))
                    for i in range(TT):
                        dve.tensor_tensor(pt[:, OFF[i]:OFF[i] + S - i * P], bank[4 + i][:, 0:S - i * P],
                                          dec[:, h, 0:S - i * P], ALU.mult).then_inc(ret.sem, 1)
                    dve.wait_ge(panel_done, at + 4)
                    scaled(gate_r[:, h * 2 + 1, :], bank[3][:], ret)

                head(0, True)
                with dve.Fori(1, RH) as h:
                    head(h, False)
                ret_norm(l * RH + RH - 1)

            def fox_load(it, t2, idx):
                for e, rows in enumerate((slice(FDH, FF_W), slice(0, FH))):
                    dve.tensor_scalar(fk[rows, e, :], cum[rows, :], cst[rows, bass.ds(t2 * 2 + C_HOT + e, 1)],
                                      None, ALU.mult).then_inc(fx_q.sem, 1)
                for k, dst in enumerate((fq, fk)):
                    dve.wait_ge(panel_done, idx + t2 * 2 + k + 1)
                    for e in range(2):
                        rows = slice(e * FDH, (e + 1) * FDH)
                        dve.tensor_tensor(dst[rows, e, :], bank[k][rows, :], rstd[rows, :], ALU.mult)\
                           .then_inc(fx_q.sem, 1)

            def fox_max(it, e):
                dve.wait_ge(*fx_s[e].at(it, "P"))
                for qt in range(TT):
                    b, c = HEAD_AT[qt]
                    last = dve.tensor_reduce(fmx[:, e, qt:qt + 1], bank[b][:, c:c + (qt + 1) * P], AX_X, ALU.max)
                last.then_inc(fx_m[e].sem, 1)
                dve.wait_ge(*fx_m[e].at(it, "M"))
                dve.tensor_scalar(fnm[:, e, :], fmx[:, e, :], -FDH ** -0.5, None, ALU.mult).then_inc(fx_m[e].sem, 1)

            def fox_turned(it, e, first):
                dve.wait_ge(*fx_t[e].at(it, "T1"))
                if e:
                    dve.wait_ge(*fx_v[0].at(it, "P"))
                elif not first:
                    dve.wait_ge(*fx_v[1].at(it - 1, "P"))
                dve.tensor_copy(fpt[:, 0:P], bank[7][:, 0:P])
                dve.tensor_copy(fpt[:, 3 * P:6 * P], bank[7][:, P:4 * P]).then_inc(fx_o[e].sem, 1)
                dve.wait_ge(*fx_x[e].at(it, "X"))
                dve.reciprocal(finv[:, e, :], fsum[:, e, :]).then_inc(fx_o[e].sem, 1)

            def fox_normed(it, e):
                dve.wait_ge(*fx_o[e].at(it, "R"))
                dve.wait_ge(*fx_v[e].at(it, "P"))
                dve.tensor_tensor(fo[:, :, e * FDH:(e + 1) * FDH],
                                  bank[5][:, 2 * P:2 * P + TT * FDH].rearrange("p (t c) -> p t c", c=FDH),
                                  finv[:, e, :].rearrange("p (t c) -> p t c", c=1).to_broadcast([P, TT, FDH]),
                                  ALU.mult).then_inc(fx_o[e].sem, 1)

            def fox_out(it, t2, b):
                dve.wait_ge(*fx_h.at(it, "YH"))
                dve.tensor_tensor(yfl[:, t2, :], bank[b][:], yfh[:, t2, :].bitcast(F32), ALU.subtract)\
                   .then_inc(fx_l.sem, 1)

            def forgetting(l, idx):
                pairs = FH // 2

                def pair(t2, first, last_pair):
                    it = l * pairs + t2
                    fox_turned(it, 0, first)
                    if not first:
                        fox_out(it - 1, t2 - 1, 1)
                    fox_max(it, 1)
                    fox_normed(it, 0)
                    if not last_pair:
                        fox_load(it + 1, t2 + 1, idx)
                    fox_turned(it, 1, first)
                    if not last_pair:
                        fox_max(it + 1, 0)
                    fox_normed(it, 1)

                ret_out(l * RH + RH - 1, l, RH - 1)
                dve.wait_ge(fx_set, l * 4 + 4)
                fox_load(l * pairs, 0, idx)
                fox_max(l * pairs, 0)
                pair(0, True, False)
                with dve.Fori(1, pairs - 1) as t2:
                    pair(t2, False, False)
                pair(pairs - 1, False, True)
                fox_out(l * pairs + pairs - 1, pairs - 1, 2)

            def merge(l, idx):
                def tile(d, q, gate_at, out_at):
                    it = l * KD + d
                    g, r, f = (bank[b] for b in ((0, 3, 4), (1, 6, 7))[q])
                    dve.wait_ge(panel_done, gate_at + 1)
                    scaled(tgf[:], g[:], mrg_d)
                    dve.wait_ge(panel_done, out_at + 1)
                    dve.wait_ge(*mrg_a.at(it, "SF"))
                    dve.tensor_tensor(mr[:], r[:], sr[:], ALU.mult).then_inc(mrg_d.sem, 1)
                    dve.tensor_tensor(mf[:], f[:], sf[:], ALU.mult).then_inc(mrg_d.sem, 1)
                    dve.wait_ge(*mrg_d.at(it, "F"))
                    dve.tensor_tensor(mg[:], mr[:], mf[:], ALU.add).then_inc(mrg_d.sem, 1)
                    dve.wait_ge(*mrg_a.at(it, "MH"))
                    dve.tensor_tensor(ml[:, d, :], mg[:], mh[:, d, :].bitcast(F32), ALU.subtract)\
                       .then_inc(mrg_d.sem, 1)

                for q in range(2):
                    tile(q, q, idx + q, idx + 2 + q)
                with dve.Fori(1, KD // 2) as i:
                    for q in range(2):
                        tile(i * 2 + q, q, idx + i * 4 + 2 * q, idx + i * 4 + 2 * q + 1)

            ROPE_ROWS = slice(64, 112)

            def angles():
                dve.tensor_copy(whole[ROPE_ROWS], posi[ROPE_ROWS, :]).then_inc(trig.sem, 1)
                dve.wait_ge(*trig.at(0, "F"))
                dve.tensor_scalar(turn[ROPE_ROWS], whole[ROPE_ROWS], cst[ROPE_ROWS, C_FREQ:C_FREQ + 1], None, ALU.mult)\
                   .then_inc(trig.sem, 1)

            def reduced(w, dst, shift, ready):
                a, k, dst = turn[ROPE_ROWS], whole[ROPE_ROWS], dst[ROPE_ROWS]
                full = 2 * np.pi
                c1 = 6.28125
                c2 = float(np.float32(full - c1))
                c3 = float(full - c1 - c2)
                limit = 3.1415925
                dve.wait_ge(*trig.at(0, ready))
                dve.tensor_scalar(k, a, 1 / full, shift, ALU.mult, ALU.add).then_inc(trig.sem, 1)
                dve.wait_ge(*trig.at(0, w + "0"))
                dve.tensor_scalar(k, k, 12582912.0, 12582912.0, ALU.add, ALU.subtract).then_inc(trig.sem, 1)
                dve.wait_ge(*trig.at(0, w + "1"))
                src = a
                for i, c in enumerate((c1, c2, c3)):
                    dve.scalar_tensor_tensor(out=dst, in0=k, scalar=-c, in1=src, op0=ALU.mult, op1=ALU.add)\
                       .then_inc(trig.sem, 1)
                    dve.wait_ge(*trig.at(0, w + str(i + 2)))
                    src = dst
                dve.tensor_scalar(dst, dst, shift * full, limit, ALU.add, ALU.min).then_inc(trig.sem, 1)
                dve.wait_ge(*trig.at(0, w + "5"))
                dve.tensor_scalar(dst, dst, -limit, None, ALU.max).then_inc(trig.sem, 1)

            def mla_max(m, h):
                it = m * MH + h
                dve.wait_ge(*mla_sc.at(it, "SC"))
                for qt in range(TT):
                    b, c = HEAD_AT[qt]
                    last = dve.tensor_reduce(smx[:, h % 2, qt:qt + 1], bank[b][:, c:c + (qt + 1) * P], AX_X, ALU.max)
                last.then_inc(mla_mx.sem, 1)
                dve.wait_ge(*mla_mx.at(it, "M"))
                dve.tensor_scalar(snm[:, h % 2, :], smx[:, h % 2, :], -(M_NOPE + M_ROPE) ** -0.5, None, ALU.mult)\
                   .then_inc(mla_mx.sem, 1)

            def swa_max(m, h):
                it = m * SWH + h
                dve.wait_ge(*swa_sc.at(it, "SC"))
                for i, b in enumerate(SWA_BANKS):
                    last = dve.tensor_reduce(smx[:, h % 2, 2 * i:2 * i + 2],
                                             bank[b][:].rearrange("p (t k) -> p t k", k=2 * P), AX_X, ALU.max)
                last.then_inc(swa_mx.sem, 1)
                dve.wait_ge(*swa_mx.at(it, "M"))
                dve.tensor_scalar(smx[:, h % 2, :], smx[:, h % 2, :], SDH ** -0.5,
                                  vecs[:, bass.ds(m * SWH + V_SINK + h, 1)], ALU.mult, ALU.max).then_inc(swa_mx.sem, 1)
                dve.wait_ge(*swa_mx.at(it, "S"))
                dve.tensor_scalar(snm[:, h % 2, :], smx[:, h % 2, :], -1.0, None, ALU.mult).then_inc(swa_mx.sem, 1)

            def normalised(dst, h, st):
                dve.tensor_tensor(dst[:, :, h * SDH:(h + 1) * SDH],
                                  bank[5][:, HEAD_OUT:HEAD_OUT + TT * SDH].rearrange("p (t c) -> p t c", c=SDH),
                                  sinv[:, h % 2, :].rearrange("p (t c) -> p t c", c=1).to_broadcast([P, TT, SDH]),
                                  ALU.mult).then_inc(st.sem, 1)

            def stick_log_sums(m, h):
                it = m * BH + h
                banks = STICK_BANKS[h % 2]
                dve.wait_ge(*sb_ln.at(it, "LN"))
                for b, c, n in PIECES:
                    last = dve.scalar_tensor_tensor(out=spl[:, h % 2, c:c + n], in0=bank[banks[b]][:, 0:n], scalar=0.0,
                                                    in1=lsg[:, h % 2, c:c + n], op0=ALU.max, op1=ALU.add)
                last.then_inc(sb_keep.sem, 1)
                dve.wait_ge(*sb_keep.at(it, "SP"))
                for b, c, n in PIECES:
                    last = dve.scalar_tensor_tensor(out=lsg[:, h % 2, c:c + n], in0=bank[banks[b]][:, 0:n], scalar=0.0,
                                                    in1=lsg[:, h % 2, c:c + n], op0=ALU.min, op1=ALU.subtract)
                last.then_inc(sb_keep.sem, 1)
                for c in STICK_AT:
                    last = dve.tensor_tensor(spl[:, h % 2, c:c + P], spl[:, h % 2, c:c + P],
                                             cst[:, C_KEEP:C_KEEP + P], ALU.mult)
                last.then_inc(sb_keep.sem, 1)

            def hybrid(m):
                q0 = SECOND + m * LAYER2
                n = FINAL + 1 + m
                norm_chain(n, 1)
                dve.wait_ge(panel_done, q0 + BT_TM + KD // 2)
                for t in range(TT):
                    dve.tensor_scalar(vtm[:, t, :], bank[4 + t][:, 0:TM_COLS], rstd_col[:, t:t + 1], None, ALU.mult)\
                       .then_inc(pj.sem, 1)
                dve.wait_ge(*chain.at(n, "RB"))
                for i, (dst, b) in enumerate(((cq[:, 0, :], 2), (cq[:, 1, :], 3), (ckv[:], 0))):
                    dve.wait_ge(panel_done, q0 + BT_CQ + i + 1)
                    scaled(dst, bank[b][:], pj)
                dve.wait_ge(*lat_act.at(m, "S1"))
                dve.tensor_tensor(qsq[:, 0, :], qsq[:, 0, :], qsq[:, 1, :], ALU.add).then_inc(lat.sem, 1)
                dve.wait_ge(panel_done, q0 + BT_AK + 1)
                scaled(ak[:], bank[1][:], pj)
                dve.wait_ge(*lat_act.at(m, "DK"))
                dve.reciprocal(linv[:], lstd[:]).then_inc(lat.sem, 1)
                dve.wait_ge(*lat.at(m, "I"))
                diagonal(diag_q, linv[:, 0, :], lat)
                diagonal(diag_k, linv[:, 1, :], lat)
                dve.wait_ge(panel_done, q0 + BT_AQ + 1)
                scaled(aq[:, 0, :], bank[2][:], pj)

                def latent(i):
                    src, g, b = ((cq[:, 0, :], m * 2 + V_QN, 5), (cq[:, 1, :], m * 2 + (V_QN + 1), 5),
                                 (ckv[:], m + V_KVN, 6))[i]
                    if i == 2:
                        dve.wait_ge(*lat.at(m, "L0"))
                    dve.scalar_tensor_tensor(out=cn[:, i % 2, :], in0=src, scalar=vecs[:, bass.ds(g, 1)],
                                             in1=bank[b][:], op0=ALU.mult, op1=ALU.mult).then_inc(lat.sem, 1)

                def latent_lo(i):
                    high, low = ((cqh[:, 0, :], cql[:, 0, :]), (cqh[:, 1, :], cql[:, 1, :]), (ckh[:], ckl[:]))[i]
                    dve.wait_ge(*lat_act.at(m, ("H0", "H1", "HK")[i]))
                    dve.tensor_tensor(low, cn[:, i % 2, :], high.bitcast(F32), ALU.subtract).then_inc(lat.sem, 1)

                dve.wait_ge(*lat_pe.at(m, "BC"))
                latent(0)
                latent(1)
                latent_lo(0)
                latent(2)
                latent_lo(1)
                latent_lo(2)
                dve.wait_ge(panel_done, q0 + BT_AQ + 2)
                scaled(aq[:, 1, :], bank[3][:], pj)
                R = ROPE_ROWS
                dve.memset(msw[R, :], 0.0).then_inc(mla.sem, 1)
                for h in range(MH):
                    dve.wait_ge(*mla_act.at(m, f"W{h}"))
                    if h:
                        dve.wait_ge(*mla.at(m, f"R{h - 1}"))
                    dve.tensor_tensor(t1[R, :], bank[4 + h][R, :], cos2[R, :], ALU.mult).then_inc(mla.sem, 1)
                    dve.tensor_tensor(t2[R, :], msw[R, :], sin2[R, :], ALU.mult).then_inc(mla.sem, 1)
                    dve.wait_ge(*mla.at(m, f"S{h}"))
                    dve.tensor_tensor(mq[R, h, :], t1[R, :], t2[R, :], ALU.add).then_inc(mla.sem, 1)
                for i in range(2):
                    dve.wait_ge(panel_done, q0 + BT_DQ + i + 1)
                    dve.scalar_tensor_tensor(out=dq[:, i, :], in0=bank[i][:], scalar=BDH ** -0.5, in1=rstd[:],
                                             op0=ALU.mult, op1=ALU.mult).then_inc(pj.sem, 1)
                dve.wait_ge(panel_done, q0 + BT_UKV + 1)
                for i in range(2):
                    dve.tensor_copy(vm[:, 2 * i:2 * i + 2, :], bank[4 + i][:].rearrange("p (t c) -> p t c", t=2))\
                       .then_inc(kv.sem, 1)
                dve.tensor_tensor(krs[0:KR_W, :], bank[6][0:KR_W, :], rstd[0:KR_W, :], ALU.mult).then_inc(kv.sem, 1)
                dve.wait_ge(*kv_act.at(m, "Y1"))
                dve.wait_ge(*mla.at(m, f"R{MH - 1}"))
                dve.tensor_tensor(t1[R, :], kx[R, :], cos2[R, :], ALU.mult).then_inc(kv.sem, 1)
                dve.tensor_tensor(t2[R, :], msw[R, :], sin2[R, :], ALU.mult).then_inc(kv.sem, 1)
                dve.wait_ge(*kv.at(m, "KM"))
                dve.tensor_tensor(mk[R, 0, :], t1[R, :], t2[R, :], ALU.add).then_inc(kv.sem, 1)
                def conv_step(c):
                    i, j = c // 3, c % 3
                    it = m * 2 + i
                    dve.wait_ge(panel_done, q0 + BT_CONV + c + 1)
                    src = bank[FILL_BANK[c]][:]
                    if j == 0:
                        if i:
                            dve.wait_ge(*conv.at(it - 1, "Y"))
                        else:
                            dve.memset(cu[:, 0:CONV_K - 1], 0.0)
                        scaled(cgs[:], src, conv)
                    elif j == 1:
                        scaled(cxs[:], src, conv)
                        dve.wait_ge(*conv.at(it, "X"))
                        dve.tensor_tensor(cu[:, CONV_K - 1:], cgs[:], cxs[:], ALU.mult).then_inc(conv.sem, 1)
                        dve.wait_ge(*conv.at(it, "U"))
                        w = m * 6 + V_CW + 3 * i
                        dve.tensor_scalar(cy[:], cu[:, 0:S], vecs[:, bass.ds(w, 1)],
                                          vecs[:, bass.ds(m * 2 + V_CB + i, 1)], ALU.mult, ALU.add)\
                           .then_inc(conv.sem, 1)
                        for k, name in ((1, "A"), (2, "B")):
                            dve.wait_ge(*conv.at(it, name))
                            dve.scalar_tensor_tensor(out=cy[:], in0=cu[:, k:k + S], scalar=vecs[:, bass.ds(w + k, 1)],
                                                     in1=cy[:], op0=ALU.mult, op1=ALU.add).then_inc(conv.sem, 1)
                    else:
                        scaled(cgs[:], src, conv)
                        dve.wait_ge(*conv.at(it, "G"))
                        dve.tensor_tensor(y_conv[:, i, :], cgs[:], cy[:], ALU.mult).then_inc(conv.sem, 1)

                def gate_load(g):
                    dve.wait_ge(panel_done, q0 + BT_GATE + g + 1)
                    scaled(gates[:, g, :], bank[FILL_BANK[6 + g]][:], gate_in)

                for i in range(2):
                    dve.wait_ge(panel_done, q0 + BT_DK + i + 1)
                    scaled(dk[:, i, :], bank[i][:], pj)
                mla_max(m, 0)
                for h in range(MH):
                    it = m * MH + h
                    dve.wait_ge(*mla_pe.at(it, "T1"))
                    if h:
                        dve.wait_ge(*mla_pe.at(it - 1, "V"))
                    dve.tensor_copy(prt[:, 0:P], bank[7][:, 0:P])
                    dve.tensor_copy(prt[:, 3 * P:6 * P], bank[7][:, P:4 * P]).then_inc(mla_dve.sem, 1)
                    dve.wait_ge(*mla_ex.at(it, "X"))
                    dve.reciprocal(sinv[:, h % 2, :], ssum[:, h % 2, :]).then_inc(mla_dve.sem, 1)
                    if h < MH - 1:
                        mla_max(m, h + 1)
                    else:
                        swa_max(m, 0)
                    dve.wait_ge(*mla_dve.at(it, "R"))
                    dve.wait_ge(*mla_pe.at(it, "V"))
                    normalised(y_mla, h, mla_dve)
                    conv_step(h)
                for h in range(SWH):
                    it = m * SWH + h
                    dve.wait_ge(*swa_pe.at(it, "T1"))
                    dve.wait_ge(*(swa_pe.at(it - 1, "V") if h else mla_pe.at(m * MH + MH - 1, "V")))
                    dve.tensor_copy(prt[:, P:4 * P], bank[7][:, 0:3 * P]).then_inc(swa_dve.sem, 1)
                    dve.wait_ge(*swa_ex.at(it, "K"))
                    dve.tensor_tensor(ssum[:, h % 2, :], ssum[:, h % 2, :], esk[:, h % 2, :], ALU.add)\
                       .then_inc(swa_dve.sem, 1)
                    dve.wait_ge(*swa_dve.at(it, "Q"))
                    dve.reciprocal(sinv[:, h % 2, :], ssum[:, h % 2, :]).then_inc(swa_dve.sem, 1)
                    if h < SWH - 1:
                        swa_max(m, h + 1)
                    dve.wait_ge(*swa_dve.at(it, "R"))
                    dve.wait_ge(*swa_pe.at(it, "V"))
                    normalised(y_swa, h, swa_dve)
                    if MH + h < CONV_TILES:
                        conv_step(MH + h)
                    else:
                        gate_load(MH + h - CONV_TILES)
                    if h == SWH - 1:
                        dve.wait_ge(*gn_act.at(m, "Q1"))
                        dve.tensor_tensor(cgs[:], cgs[:], cxs[:], ALU.add).then_inc(gn.sem, 1)
                stick_log_sums(m, 0)
                gate_load(2)
                for h in range(BH):
                    dve.wait_ge(*sb_pe.at(m * BH + h, "A"))
                    for b, c, n_ in PIECES:
                        last = dve.tensor_tensor(lsg[:, h % 2, c:c + n_], lsg[:, h % 2, c:c + n_],
                                                 bank[STICK_BANKS[h % 2][b]][:, 0:n_], ALU.add)
                    last.then_inc(sb_dve.sem, 1)
                    if h < BH - 1:
                        stick_log_sums(m, h + 1)
                        gate_load(3 + h)
                dve.wait_ge(*gn_act.at(m, "D0"))
                dve.reciprocal(ginv[:, 0:2, :], gstd[:, 0:2, :]).then_inc(gn.sem, 1)
                dve.wait_ge(*gn_pe.at(m, "COL"))
                dve.tensor_copy(gsum[:, 3, :], bank[7][:, 0:TT]).then_inc(gn.sem, 1)

                def group_scaled(y, i):
                    dve.tensor_tensor(y[:], y[:], ginv[:, i, :].rearrange("p (t c) -> p t c", c=1)
                                      .to_broadcast([P, TT, GROUP]), ALU.mult).then_inc(gn.sem, 1)

                dve.wait_ge(*gn.at(m, "I0"))
                group_scaled(y_swa, 0)
                group_scaled(y_mla, 1)
                dve.wait_ge(*gn_act.at(m, "D1"))
                dve.reciprocal(ginv[:, 2:4, :], gstd[:, 2:4, :]).then_inc(gn.sem, 1)
                dve.wait_ge(*gn.at(m, "I1"))
                group_scaled(y_sb, 2)
                diagonal(diag, ginv[:, 3, :], gn)
                gate_load(KD - 2)

                def gated(j):
                    d, it = READY[j], m * KD + j
                    if j >= 2:
                        dve.wait_ge(*gate_l.at(it - 2, "L"))
                    if d // 2 == 1:
                        if d == 2:
                            dve.wait_ge(*gn_pe.at(m, "BC"))
                            for c in range(2):
                                dve.scalar_tensor_tensor(out=y_conv[:, c, :], in0=y_conv[:, c, :],
                                                         scalar=vecs[:, bass.ds(m * KD + (V_GRP + 2 + c), 1)],
                                                         in1=bank[3][:], op0=ALU.mult, op1=ALU.mult)\
                                   .then_inc(gn.sem, 1)
                        dve.wait_ge(*gn.at(m, f"B{d - 2}"))
                        dve.tensor_tensor(yg[:, j % 2, :], y_conv[:, d - 2, :], gates[:, d, :], ALU.mult)\
                           .then_inc(gate_y.sem, 1)
                    else:
                        i = (0, None, 1, 2)[d // 2]
                        dve.wait_ge(*gate_s.at(m * KD + d, "S"))
                        dve.wait_ge(*gn_pe.at(m, f"T{i}"))
                        dve.scalar_tensor_tensor(out=yg[:, j % 2, :], in0=bank[GROUP_BANKS[i][d % 2]][:],
                                                 scalar=vecs[:, bass.ds(m * KD + (V_GRP + d), 1)], in1=gates[:, d, :],
                                                 op0=ALU.mult, op1=ALU.mult).then_inc(gate_y.sem, 1)

                def gated_lo(j):
                    dve.wait_ge(*gate_h.at(m * KD + j, "H"))
                    dve.tensor_tensor(ygl[:, READY[j], :], yg[:, j % 2, :], ygh[:, READY[j], :].bitcast(F32),
                                      ALU.subtract).then_inc(gate_l.sem, 1)

                gated(0)
                gated(1)
                for j in range(2, KD):
                    gated_lo(j - 2)
                    gated(j)
                    if j == 3:
                        gate_load(KD - 1)
                gated_lo(KD - 2)
                gated_lo(KD - 1)
                for d in range(KD):
                    dve.wait_ge(*z_act.at(m * KD + d, "Q"))
                    if d == 0:
                        dve.tensor_copy(ssq[:], sq[:]).then_inc(z_sum.sem, 1)
                    else:
                        dve.wait_ge(*z_sum.at(m * KD + d - 1, "A"))
                        dve.tensor_tensor(ssq[:], ssq[:], (sq, diag)[d % 2][:], ALU.add).then_inc(z_sum.sem, 1)
                dve.wait_ge(*post_sd.at(m, "SD"))
                dve.reciprocal(rstd_col[:], std_col[:]).then_inc(post.sem, 1)
                dve.wait_ge(*post.at(m, "RC"))
                diagonal(diag, rstd_col[:], post)
                dve.wait_ge(*post_pe.at(m, "BC"))
                def residual(d):
                    dve.wait_ge(*z_act.at(m * KD + d, "Z"))
                    dve.scalar_tensor_tensor(out=z[:, d, :], in0=z[:, d, :],
                                             scalar=vecs[:, bass.ds(m * KD + V_POST + d, 1)], in1=bank[3][:],
                                             op0=ALU.mult, op1=ALU.mult).then_inc(post.sem, 1)
                    dve.wait_ge(*post.at(m, f"Z{d}"))
                    dve.tensor_tensor(x[:, d, :], x[:, d, :], z[:, d, :], ALU.add).then_inc(resid.sem, 1)

                for d in range(KD + AHEAD):
                    if d < KD:
                        residual(d)
                    if d >= AHEAD:
                        operand_lo(m + 1, d - AHEAD)

            dve.memset(eps[:], EPS).then_inc(memsets, 1)
            dve.memset(start_d[:, KD:KD + 1], 0.0).then_inc(rg.sem, 1)
            dve.wait_ge(vec_in, 16)
            for d in range(KD):
                if d % (KD // X_PARTS) == 0:
                    dve.wait_ge(x_part[d * X_PARTS // KD], 16)
                dve.memset(start_d[:, d:d + 1], 0.0).then_inc(resid.sem, 1)
                prepare(0, d, 0)
            for d in range(KD):
                add_squares(0, d)
            dve.wait_ge(const_in, 16)
            dve.wait_ge(pos_in, 16)
            angles()
            reduced("s", ang, 0.0, "A")
            norm_chain(0, 7, lambda: reduced("c", turn, 0.25, "s6"))
            dve.tensor_copy(ident16[:], ident).then_inc(mask_set, 1)
            dve.tensor_copy(masks[:], cst[:, C_CAUSAL:C_KEEP]).then_inc(mask_set, 1)
            with dve.Fori(0, DEPTH) as l:
                p0 = l * LAYER1
                ffn_in(l * 2, l * 3, p0)
                n = l * 3 + 1
                ffn_out(l * 2, n, p0 + FFN_IN)
                dve.wait_ge(tab_in, l * 48 + 48)
                dve.tensor_copy(ffh[:], ffraw[:]).then_inc(ffs.sem, 1)
                dve.wait_ge(*ffs.at(l, "H"))
                dve.tensor_tensor(ffl[:], ffraw[:], ffh[:].bitcast(F32), ALU.subtract).then_inc(ffs.sem, 1)
                norm_chain(n, 1)
                for dst, at, banks in ((v_ret, AT_RV, (4, 5, 6, 7)), (v_fox, AT_FV, (0, 1, 2, 3))):
                    dve.wait_ge(panel_done, p0 + at + KD // 2)
                    for t in range(TT):
                        dve.tensor_scalar(dst[:, t, :], bank[banks[t]][:], rstd_col[:, t:t + 1], None, ALU.mult)\
                           .then_inc(tm.sem, 1)
                dve.wait_ge(*ffs_pe.at(l, "FF"))
                dve.wait_ge(*chain.at(n, "RB"))
                dve.tensor_tensor(fz[0:FF_W], bank[4][0:FF_W, :], rstd[0:FF_W, :], ALU.mult).then_inc(ffs.sem, 1)
                dve.wait_ge(*ffs.at(l, "Z"))
                dve.tensor_scalar(fz[0:FF_W], fz[0:FF_W], vecs[0:FF_W, bass.ds(l + V_BF, 1)], None, ALU.add)\
                   .then_inc(ffs.sem, 1)
                with dve.Fori(0, RH // 2) as i:
                    for q in range(2):
                        dve.wait_ge(panel_done, p0 + AT_RG + i * 2 + q + 1)
                        dve.wait_ge(*rg_act.before(l * RH + i * 2 + q))
                        scaled(tg[:], bank[q][:], rg)
                dve.wait_ge(*ffs_act.at(l, "LN"))
                dve.scalar_tensor_tensor(out=fz[0:FF_W], in0=fz[0:FF_W], scalar=0.0, in1=fa[0:FF_W],
                                         op0=ALU.min, op1=ALU.subtract).then_inc(ffs.sem, 1)
                dve.wait_ge(*ffs.at(l, "LF"))
                dve.tensor_tensor_scan(cum[0:FF_W, :], ones[0:FF_W, 0:1].to_broadcast([FF_W, S]), fz[0:FF_W], 0.0,
                                       ALU.mult, ALU.add).then_inc(ffs.sem, 1)
                dve.wait_ge(*ffs.at(l, "C"))
                for e, rows in enumerate((slice(FDH, P), slice(0, FDH))):
                    dve.memset(fq[rows, e, :], -FDH ** 0.5).then_inc(fx_set, 1)
                    dve.memset(fk[rows, e, :], 0.0).then_inc(fx_set, 1)
                retention(l, p0 + AT_RET)
                forgetting(l, p0 + AT_FOX)
                merge(l, p0 + AT_MERGE)
                n2 = l * 3 + 2
                for d in range(KD):
                    dve.wait_ge(panel_done, p0 + AT_WOUT + d + 1)
                    dve.tensor_tensor(x[:, d, :], bank[2 + 3 * (d % 2)][:], x[:, d, :], ALU.add).then_inc(resid.sem, 1)
                    prepare(n2, d, n2)
                    add_squares(n2, d)
                norm_chain(n2, 7)
                ffn_in(l * 2 + 1, n2, p0 + AT_FFN2)
                ffn_out(l * 2 + 1, l * 3 + 3, p0 + AT_FFN2 + FFN_IN)
                norm_chain(l * 3 + 3, 7)
            dve.wait_ge(*chain.at(FINAL, "RB"))
            def normed(d):
                dve.scalar_tensor_tensor(out=x[:, d, :], in0=x[:, d, :],
                                         scalar=vecs[:, FINAL * KD + d:FINAL * KD + d + 1],
                                         in1=rstd[:], op0=ALU.mult, op1=ALU.mult).then_inc(resid.sem, 1)

            for d in range(KD + 1):
                if d < KD:
                    normed(d)
                if d:
                    operand_lo(0, d - 1)
            with dve.Fori(0, DEPTH) as m:
                hybrid(m)


def table_of_constants():
    c = np.zeros((P, N_CONST), np.float32)
    i, j = np.arange(P)[:, None], np.arange(P)[None, :]
    c[:, C_ID:C_ID + P] = i == j
    c[:, C_ONE:C_ONE + P] = 1
    c[:, C_NONE:C_NONE + P] = -1
    c[:, C_NTRI:C_NTRI + P] = -1.0 * (i > j)
    c[:, C_CAUSAL:C_CAUSAL + P] = np.where(j <= i, 0, NEG)
    c[:, C_SWA:C_SWA + P] = np.where(j > i, 0, NEG)
    c[:, C_SWA + P:C_SWA + 2 * P] = np.where(j <= i, 0, NEG)
    c[:, C_SWA0:C_SWA0 + P] = NEG
    c[:, C_SWA0 + P:C_SWA0 + 2 * P] = np.where(j <= i, 0, NEG)
    c[:, C_STRICT:C_STRICT + P] = np.where(j > i, 0, NEG)
    c[:, C_KEEP:C_KEEP + P] = j > i
    half = M_ROPE // 2
    freqs = np.float32(10000.0) ** (-np.arange(half, dtype=np.float32) / np.float32(half))
    c[64:64 + half, C_FREQ] = freqs
    c[96:96 + half, C_FREQ] = freqs
    c[0:FH, C_HOT:C_HOT + FH] = c[FDH:FF_W, C_HOT:C_HOT + FH] = np.eye(FH)
    return c


def decay_table():
    gamma = 1 - 2.0 ** (-5 - np.arange(RH))
    gap = np.arange(S)[None, :] - np.arange(P)[:, None]
    t = np.where(gap[:, None, :] >= 0, gamma[None, :, None] ** np.maximum(gap, 0)[:, None, :], 0) * RDK ** -0.5
    return t.astype(np.float32)


def rope_table():
    half = RDK // 2
    inv = np.float32(10000.0) ** (-np.arange(0, RDK, 2, dtype=np.float32) / np.float32(RDK))
    ang = (np.arange(S, dtype=np.float32)[None, :] * inv[:, None]).astype(np.float64)
    t = np.zeros((P, 2, S))
    t[0:half, 0] = t[half:, 0] = np.cos(ang)
    t[0:half, 1], t[half:, 1] = -np.sin(ang), np.sin(ang)
    return t.astype(np.float32)


def col_panels(w):
    k, n = w.shape
    return w.reshape(KD, P, n // P, P).transpose(2, 1, 0, 3).reshape(n // P, P, PANEL)


def tok_panels(w):
    return w.reshape(KD // 2, 2, P, S).transpose(0, 2, 1, 3).reshape(KD // 2, P, PANEL)


def ffn_panels(w_in, w_out):
    a, b = col_panels(w_in[:, :F]), col_panels(w_in[:, F:])
    both = np.stack([a, b], 1).reshape(2 * KF, P, PANEL)
    whole = w_out[:KT_MAJOR * P].reshape(KT_MAJOR, P, PANEL)
    rest = w_out[KT_MAJOR * P:].reshape(KF - KT_MAJOR, P, KD, P).transpose(2, 0, 1, 3)
    rest = rest.reshape(-1, UNITS, P, P).transpose(0, 2, 1, 3).reshape(-1, P, PANEL)
    return [both, whole, rest]


def first_layer(a, l):
    w = a["w_in"][l]
    rq, rk, rv, rgw, fq, fk, fv = (w[:, i * 512:(i + 1) * 512] for i in range(7))
    gr, gf = w[:, 3592:4616], w[:, 4616:5640]
    crq, crk, cgr, cfq, cfk = map(col_panels, (rq, rk, gr, fq, fk))
    ret = np.stack([crq, crk, cgr[0::2], cgr[1::2]], 1).reshape(-1, P, PANEL)
    fox = np.stack([cfq, cfk], 1).reshape(-1, P, PANEL)
    wo = np.concatenate([a["w_o_ret"][l].reshape(RH, P, KD, P), a["w_o_fox"][l].reshape(FH // 2, P, KD, P)])
    wo = wo.transpose(2, 1, 0, 3).reshape(KD, P, PANEL)
    mrg = np.stack([col_panels(gf), wo], 1).reshape(-1, P, PANEL)
    mrg[[1, 2]] = mrg[[2, 1]]
    return [*ffn_panels(a["w_ffn1_in"][l], a["w_ffn1_out"][l]), tok_panels(rv), tok_panels(fv), col_panels(rgw),
            ret, fox, mrg, col_panels(a["w_out"][l]), *ffn_panels(a["w_ffn2_in"][l], a["w_ffn2_out"][l])]


def second_layer(a, l):
    w = a["w_in_2"][l]
    cuts = np.cumsum((256, 128, 128, 256, 256, 256, 256, 128, 32, 256, 256, 256))
    a_q, a_k, a_v, b_b, b_c, b_x, c_q, c_kv, c_kr, d_q, d_k, d_v, gate_w = np.split(w, cuts, axis=1)
    tokens = np.concatenate([a_v, d_v, np.zeros((D, S - TM_COLS), np.float32)], 1)
    a_q = a_q.reshape(D, SWH, SDH)[:, [0, 2, 1, 3]].reshape(D, SWH * SDH)
    half = M_ROPE // 2

    def spread(rope):
        gap = np.zeros((*rope.shape[:-1], half), np.float32)
        return np.concatenate([rope[..., :half], gap, rope[..., half:]], -1)

    uq = a["mla_w_uq_2"][l].reshape(2, P, MH, M_NOPE + M_ROPE)
    uq = np.concatenate([uq[..., :M_NOPE], spread(uq[..., M_NOPE:]), np.zeros((2, P, MH, P - MLA_K), np.float32)], -1)
    uq = uq.transpose(1, 2, 0, 3).reshape(1, P, PANEL)
    ukv = a["mla_w_ukv_2"][l].reshape(KVR, MH, M_NOPE + M_V)
    k_rope = spread(c_kr).reshape(KD, P, KR_W).transpose(1, 0, 2).reshape(P, KD * KR_W)
    up = np.concatenate([ukv[..., :M_NOPE].reshape(P, -1), ukv[..., M_NOPE:].reshape(P, -1), k_rope,
                         np.zeros((P, PANEL - KR_AT - KD * KR_W), np.float32)], 1)[None]
    conv = np.stack([col_panels(b_c), col_panels(b_x), col_panels(b_b)], 1).reshape(-1, P, PANEL)
    return [tok_panels(tokens), col_panels(c_q), col_panels(c_kv), col_panels(a_k), col_panels(a_q), uq,
            col_panels(d_q), up, col_panels(d_k), conv, col_panels(gate_w), col_panels(a["w_out_2"][l])]


def columns(v):
    return v.reshape(-1, P).T


def kernel(**inputs):
    import concourse.bacc as bacc
    from concourse.bass_utils import run_bass_kernel_spmd

    a = {k: np.asarray(v) for k, v in inputs.items()}
    panels = [p for l in range(DEPTH) for p in first_layer(a, l)]
    panels += [p for l in range(DEPTH) for p in second_layer(a, l)]
    stream = np.concatenate(panels)
    assert len(stream) == N_PANELS
    vec = np.zeros((P, N_VEC), np.float32)
    norms = [a[k][l] for l in range(DEPTH) for k in ("norm_ffn1", "norm_mix", "norm_ffn2")]
    norms += [a["norm_final"], a["norm_pre_2"][0], a["norm_pre_2"][1]]
    for i, g in enumerate(norms):
        vec[:, i * KD:(i + 1) * KD] = columns(g)
    vec[:, V_RET:V_RET + DEPTH * RH] = columns(a["ret_norm"])
    vec[:, V_GRP:V_GRP + DEPTH * KD] = columns(a["group_norm_2"])
    vec[:, V_POST:V_POST + DEPTH * KD] = columns(a["norm_post_2"])
    vec[:, V_QN:V_QN + DEPTH * 2] = columns(a["mla_q_norm_2"])
    vec[:, V_KVN:V_KVN + DEPTH] = columns(a["mla_kv_norm_2"])
    vec[:, V_CW:V_CW + DEPTH * 6] = a["conv_w_2"].reshape(DEPTH, CONV_K, 2, P).transpose(3, 0, 2, 1).reshape(P, -1)
    vec[:, V_CB:V_CB + DEPTH * 2] = columns(a["conv_b_2"])
    vec[:, V_SINK:V_SINK + DEPTH * SWH] = a["attn_sinks_2"].reshape(1, -1)
    vec[0:FH, V_BF:V_BF + DEPTH] = vec[FDH:FF_W, V_BF:V_BF + DEPTH] = a["b_forget"].T
    w_ff = a["w_in"][:, :, 3584:3592].reshape(DEPTH, KD, P, FH).transpose(0, 2, 1, 3)
    ff = np.zeros((DEPTH, P, FF_COLS), np.float32)
    by_tile = ff[:, :, :KD * FF_W].reshape(DEPTH, P, KD, FF_W)
    by_tile[..., 0:FH] = by_tile[..., FDH:] = w_ff
    arrays = {
        "stream": stream,
        "x_t": np.ascontiguousarray(a["x"][0].T.reshape(KD, P, S).transpose(1, 0, 2)),
        "vec": vec, "const": table_of_constants(), "decay": decay_table(), "rope": rope_table(),
        "ff_w": ff,
        "pos": np.ascontiguousarray(np.broadcast_to(a["positions_2"][0].astype(np.int32), (P, S))),
    }
    nc = bacc.Bacc("TRN2", target_bir_lowering=False, num_devices=1)
    args = [nc.dram_tensor(k, v.shape, mybir.dt.from_np(v.dtype), kind="ExternalInput").ap() for k, v in arrays.items()]
    out = nc.dram_tensor("out", [KD, P, S], F32, kind="ExternalOutput").ap()
    build(nc, *args, out)
    r = run_bass_kernel_spmd(nc, [arrays], core_ids=[0])
    return r.results[0]["out"].reshape(D, S).T[None].copy()
```
